# Optimizing a Trainium2 kernel written in Bass

```python
import math
import jax, jax.numpy as jnp
from jax import lax
import numpy as np

D_MODEL = 1024
BATCH = 1
SEQ = 512
DEPTH = 2

N_META = 16
N_MIXERS = 2
EXPAND = 2
D_INNER = EXPAND * D_MODEL
RMS_EPS = 1e-6
N_RWKV_LAYERS = (DEPTH + 1) // 2
N_MLA_LAYERS = DEPTH // 2

RWKV_HEAD = 64
RWKV_HEADS = D_INNER // RWKV_HEAD
DECAY_LORA = 64
AAA_LORA = 64
RWKV_WIDTHS = (D_INNER, D_INNER, D_INNER, D_INNER, DECAY_LORA, AAA_LORA)
N_LERP = len(RWKV_WIDTHS)
RWKV_IN = sum(RWKV_WIDTHS)
GN_EPS = 64e-5

MLA_HEADS = 16
QK_NOPE = 128
QK_ROPE = 64
V_HEAD = 128
Q_LORA = 512
KV_LORA = 256
MLA_IN = Q_LORA + KV_LORA + QK_ROPE + D_INNER
ROPE_THETA = 10000.0
Q_BLOCK = 128


def _rms_norm(x, g):
    xf = x.astype(jnp.float32)
    y = xf * lax.rsqrt(jnp.mean(xf * xf, axis=-1, keepdims=True) + RMS_EPS)
    return (y * g.astype(jnp.float32)).astype(x.dtype)

def _rope(x, pos):
    half = x.shape[-1] // 2
    inv_freq = jnp.exp(-math.log(ROPE_THETA) * jnp.arange(half, dtype=jnp.float32) / half)
    ang = pos[:, None] * inv_freq[None, :]
    ang = ang.reshape((1, ang.shape[0]) + (1,) * (x.ndim - 3) + (half,))
    cos, sin = jnp.cos(ang), jnp.sin(ang)
    xf = x.astype(jnp.float32)
    x1, x2 = xf[..., :half], xf[..., half:]
    return jnp.concatenate([x1 * cos - x2 * sin, x2 * cos + x1 * sin], axis=-1).astype(x.dtype)

def _wkv7_scan(r, decay, k, v, a_vec, b_vec):
    B, L, H, N = r.shape
    xs = tuple(jnp.moveaxis(t.astype(jnp.float32), 1, 0) for t in (r, decay, k, v, a_vec, b_vec))

    def step(S, inp):
        r_t, w_t, k_t, v_t, a_t, b_t = inp
        sa = jnp.einsum('bhij,bhj->bhi', S, a_t)
        S = S * w_t[:, :, None, :] + sa[..., None] * b_t[:, :, None, :] + v_t[..., None] * k_t[:, :, None, :]
        return S, jnp.einsum('bhij,bhj->bhi', S, r_t)

    S0 = jnp.zeros((B, H, N, N), jnp.float32)
    _, ys = lax.scan(step, S0, xs)
    return jnp.moveaxis(ys, 0, 1)

def _rwkv7_mixer(x, mu, w_in, w0, w2, a0, a2, k_k, k_a, r_k, ln_w, ln_b, w_out):
    B, L, _ = x.shape
    H, N = RWKV_HEADS, RWKV_HEAD
    x_prev = jnp.pad(x, ((0, 0), (1, 0), (0, 0)))[:, :-1]
    dx = x_prev - x
    widths = np.array(RWKV_WIDTHS)
    mu_cols = jnp.repeat(mu.T, widths, axis=1, total_repeat_length=RWKV_IN)
    w_comb = jnp.concatenate([w_in, mu_cols * w_in], axis=0)
    h = jnp.concatenate([x, dx], axis=-1) @ w_comb
    r, k, v, g, w_lo, a_lo = jnp.split(h, list(np.cumsum(widths)[:-1]), axis=-1)
    w = -jax.nn.softplus(-(w0 + jnp.tanh(w_lo) @ w2)) - 0.5
    a = jax.nn.sigmoid(a0 + a_lo @ a2)
    heads = lambda t: t.reshape(B, L, H, N)
    r, k, v, w, a = heads(r), heads(k), heads(v), heads(w), heads(a)
    k_k, k_a, r_k = k_k.reshape(H, N), k_a.reshape(H, N), r_k.reshape(H, N)
    kk = (k * k_k).astype(jnp.float32)
    kk = kk / jnp.maximum(jnp.linalg.norm(kk, axis=-1, keepdims=True), 1e-12)
    k = k * (1 + (a - 1) * k_a)
    decay = jnp.exp(-jnp.exp(w.astype(jnp.float32)))
    y = _wkv7_scan(r, decay, k, v, -kk, kk * a.astype(jnp.float32))
    mean = jnp.mean(y, axis=-1, keepdims=True)
    var = jnp.mean(jnp.square(y - mean), axis=-1, keepdims=True)
    y = ((y - mean) * lax.rsqrt(var + GN_EPS)).reshape(B, L, D_INNER)
    y = y * ln_w.astype(jnp.float32) + ln_b.astype(jnp.float32)
    bonus = (jnp.sum(r * k * r_k, axis=-1, keepdims=True) * v).reshape(B, L, D_INNER)
    y = (y + bonus.astype(jnp.float32)).astype(x.dtype) * jax.nn.silu(g)
    return y @ w_out

def _causal_block_attention(q_nope, q_rope, k_nope, k_rope, v):
    L = q_nope.shape[1]
    scale = (QK_NOPE + QK_ROPE) ** -0.5
    neg = jnp.finfo(jnp.float32).min
    bounds = [(0, N_META)] + [(s, min(s + Q_BLOCK, L)) for s in range(N_META, L, Q_BLOCK)]
    outs = []
    for s, e in bounds:
        sc = (jnp.einsum('bqhd,bkhd->bhqk', q_nope[:, s:e], k_nope[:, :e])
              + jnp.einsum('bqhr,bkr->bhqk', q_rope[:, s:e], k_rope[:, :e])).astype(jnp.float32) * scale
        mask = jnp.arange(s, e)[:, None] >= jnp.arange(e)[None, :]
        p = jax.nn.softmax(jnp.where(mask, sc, neg), axis=-1).astype(v.dtype)
        outs.append(jnp.einsum('bhqk,bkhd->bqhd', p, v[:, :e]))
    return jnp.concatenate(outs, axis=1)

def _mla_mixer(x, pos, w_in, q_norm, w_q_up, kv_norm, w_kv_up, w_out):
    B, L, _ = x.shape
    H = MLA_HEADS
    h = x @ w_in
    c_q, c_kv, k_rope, g = jnp.split(h, [Q_LORA, Q_LORA + KV_LORA, Q_LORA + KV_LORA + QK_ROPE], axis=-1)
    q = (_rms_norm(c_q, q_norm) @ w_q_up).reshape(B, L, H, QK_NOPE + QK_ROPE)
    q_nope, q_rope = q[..., :QK_NOPE], _rope(q[..., QK_NOPE:], pos)
    kv = (_rms_norm(c_kv, kv_norm) @ w_kv_up).reshape(B, L, H, QK_NOPE + V_HEAD)
    k_nope, v = kv[..., :QK_NOPE], kv[..., QK_NOPE:]
    k_rope = _rope(k_rope, pos)
    o = _causal_block_attention(q_nope, q_rope, k_nope, k_rope, v).reshape(B, L, D_INNER)
    return (o * jax.nn.silu(g)) @ w_out

def first_inputs(seed: int = 0) -> dict:
    key = jax.random.key(seed)
    ks = jax.random.split(key, 24)
    f32 = jnp.float32
    nrm = lambda k, shape, s: jax.random.normal(k, shape, f32) * s
    NR, NM = N_RWKV_LAYERS, N_MLA_LAYERS
    return {
        "x": nrm(ks[0], (BATCH, SEQ, D_MODEL), 1.0),
        "meta_tokens": nrm(ks[1], (N_META, D_MODEL), 1.0),
        "norm_pre": 1.0 + nrm(ks[2], (DEPTH, D_MODEL), 0.02),
        "norm_post": 1.0 + nrm(ks[3], (DEPTH, D_MODEL), 0.02),
        "rwkv_mu": jax.random.uniform(ks[4], (NR, N_LERP, D_MODEL), f32),
        "rwkv_w_in": nrm(ks[5], (NR, D_MODEL, RWKV_IN), D_MODEL ** -0.5),
        "rwkv_w0": -2.0 + nrm(ks[6], (NR, D_INNER), 0.5),
        "rwkv_w2": nrm(ks[7], (NR, DECAY_LORA, D_INNER), 0.5 * DECAY_LORA ** -0.5),
        "rwkv_a0": nrm(ks[8], (NR, D_INNER), 0.1),
        "rwkv_a2": nrm(ks[9], (NR, AAA_LORA, D_INNER), 0.5 * AAA_LORA ** -0.5),
        "rwkv_k_k": 0.85 + nrm(ks[10], (NR, D_INNER), 0.05),
        "rwkv_k_a": 1.0 + nrm(ks[11], (NR, D_INNER), 0.05),
        "rwkv_r_k": nrm(ks[12], (NR, D_INNER), 0.1),
        "rwkv_ln_w": 1.0 + nrm(ks[13], (NR, D_INNER), 0.02),
        "rwkv_ln_b": nrm(ks[14], (NR, D_INNER), 0.02),
        "rwkv_w_out": nrm(ks[15], (NR, D_INNER, D_MODEL), D_INNER ** -0.5),
        "mla_w_in": nrm(ks[16], (NM, D_MODEL, MLA_IN), D_MODEL ** -0.5),
        "mla_q_norm": 1.0 + nrm(ks[17], (NM, Q_LORA), 0.02),
        "mla_w_q_up": nrm(ks[18], (NM, Q_LORA, MLA_HEADS * (QK_NOPE + QK_ROPE)), Q_LORA ** -0.5),
        "mla_kv_norm": 1.0 + nrm(ks[19], (NM, KV_LORA), 0.02),
        "mla_w_kv_up": nrm(ks[20], (NM, KV_LORA, MLA_HEADS * (QK_NOPE + V_HEAD)), KV_LORA ** -0.5),
        "mla_w_out": nrm(ks[21], (NM, D_INNER, D_MODEL), D_INNER ** -0.5),
    }

def first_block(x, meta_tokens, norm_pre, norm_post,
              rwkv_mu, rwkv_w_in, rwkv_w0, rwkv_w2, rwkv_a0, rwkv_a2,
              rwkv_k_k, rwkv_k_a, rwkv_r_k, rwkv_ln_w, rwkv_ln_b, rwkv_w_out,
              mla_w_in, mla_q_norm, mla_w_q_up, mla_kv_norm, mla_w_kv_up, mla_w_out):
    B = x.shape[0]
    meta = jnp.broadcast_to(meta_tokens.astype(x.dtype)[None], (B, N_META, D_MODEL))
    h = jnp.concatenate([meta, x], axis=1)
    pos = jnp.arange(h.shape[1], dtype=jnp.float32)
    for i in range(DEPTH):
        j = i // N_MIXERS
        u = _rms_norm(h, norm_pre[i])
        if i % N_MIXERS == 0:
            m = _rwkv7_mixer(u, rwkv_mu[j], rwkv_w_in[j], rwkv_w0[j], rwkv_w2[j], rwkv_a0[j], rwkv_a2[j],
                             rwkv_k_k[j], rwkv_k_a[j], rwkv_r_k[j], rwkv_ln_w[j], rwkv_ln_b[j], rwkv_w_out[j])
        else:
            m = _mla_mixer(u, pos, mla_w_in[j], mla_q_norm[j], mla_w_q_up[j], mla_kv_norm[j],
                           mla_w_kv_up[j], mla_w_out[j])
        h = h + _rms_norm(m, norm_post[i])
    return h[:, N_META:]


GRID_W = 64
EPS = 1e-6

A_HEADS = 8
A_HEAD_DIM = D_MODEL // 16
A_WIDTH = A_HEADS * A_HEAD_DIM
CONV_WIDTH = 3
B_GROUPS = 4
B_GROUP_DIM = D_MODEL // 8
B_WIDTH = B_GROUPS * B_GROUP_DIM
EVEN_IN = 4 * A_WIDTH + 2 * B_WIDTH
EVEN_MIX = A_WIDTH + B_WIDTH

HEAD_DIM = 128
N_HEADS = D_MODEL // HEAD_DIM
N_KV_HEADS = N_HEADS // 4
Q_WIDTH = N_HEADS * HEAD_DIM
KV_WIDTH = N_KV_HEADS * HEAD_DIM
ODD_IN = 2 * Q_WIDTH + 2 * KV_WIDTH

N_EVEN = (DEPTH + 1) // 2
N_ODD = DEPTH // 2


def rms_norm(x, g):
    xf = x.astype(jnp.float32)
    y = xf * lax.rsqrt(jnp.mean(xf * xf, axis=-1, keepdims=True) + EPS)
    return (y * g.astype(jnp.float32)).astype(x.dtype)

def centred_depthwise_conv(u, w):
    s = u.shape[1]
    pad = CONV_WIDTH // 2
    up = jnp.pad(u, ((0, 0), (pad, CONV_WIDTH - 1 - pad), (0, 0)))
    out = up[:, 0:s] * w[0]
    for tap in range(1, CONV_WIDTH):
        out = out + up[:, tap:tap + s] * w[tap]
    return out

def short_conv_fourier_mixer(h, w_in, conv_w, w_out):
    bsz, s, _ = h.shape
    proj = h @ w_in
    a_x, a_b, a_c, a_z, b_u, b_z = jnp.split(
        proj,
        [A_WIDTH, 2 * A_WIDTH, 3 * A_WIDTH, 4 * A_WIDTH, 4 * A_WIDTH + B_WIDTH],
        axis=-1)
    y_a = a_b * centred_depthwise_conv(a_c * a_x, conv_w) * jax.nn.silu(a_z)
    u = b_u.reshape(bsz, s, B_GROUPS, B_GROUP_DIM).astype(jnp.float32)
    f = jnp.fft.fft2(u, axes=(1, 3), norm="ortho").real
    y_b = f.reshape(bsz, s, B_WIDTH).astype(h.dtype) * jax.nn.silu(b_z)
    return jnp.concatenate([y_a, y_b], axis=-1) @ w_out

def axial_rope_tables(s):
    rows = s // GRID_W
    row = jnp.repeat(jnp.arange(rows), GRID_W).astype(jnp.float32)
    col = jnp.tile(jnp.arange(GRID_W), rows).astype(jnp.float32)
    n_pair = HEAD_DIM // 4
    inv = ROPE_THETA ** (-jnp.arange(n_pair, dtype=jnp.float32) / n_pair)
    ang = jnp.concatenate([row[:, None] * inv, col[:, None] * inv], axis=-1)
    return jnp.cos(ang), jnp.sin(ang)

def apply_rope(x, cos, sin):
    xf = x.astype(jnp.float32).reshape(x.shape[:-1] + (HEAD_DIM // 2, 2))
    x1, x2 = xf[..., 0], xf[..., 1]
    c = cos[None, :, None, :]
    sn = sin[None, :, None, :]
    out = jnp.stack([x1 * c - x2 * sn, x1 * sn + x2 * c], axis=-1)
    return out.reshape(x.shape).astype(x.dtype)

def gqa_axial_mixer(h, w_in, q_gain, k_gain, w_out):
    bsz, s, _ = h.shape
    proj = h @ w_in
    q, k, v, z = jnp.split(
        proj, [Q_WIDTH, Q_WIDTH + KV_WIDTH, Q_WIDTH + 2 * KV_WIDTH], axis=-1)
    q = q.reshape(bsz, s, N_HEADS, HEAD_DIM)
    k = k.reshape(bsz, s, N_KV_HEADS, HEAD_DIM)
    v = v.reshape(bsz, s, N_KV_HEADS, HEAD_DIM)
    cos, sin = axial_rope_tables(s)
    q = apply_rope(rms_norm(q, q_gain), cos, sin)
    k = apply_rope(rms_norm(k, k_gain), cos, sin)
    groups = N_HEADS // N_KV_HEADS
    n_blk = s // Q_BLOCK
    qb = q.reshape(bsz, n_blk, Q_BLOCK, N_KV_HEADS, groups, HEAD_DIM).transpose(1, 0, 3, 4, 2, 5)
    kt = k.transpose(0, 2, 1, 3)
    vt = v.transpose(0, 2, 1, 3)
    scale = HEAD_DIM ** -0.5

    def attend_block(q_blk):
        sc = jnp.einsum('bkgqd,bksd->bkgqs', q_blk, kt,
                        preferred_element_type=jnp.float32) * scale
        p = jax.nn.softmax(sc, axis=-1)
        return jnp.einsum('bkgqs,bksd->bkgqd', p.astype(vt.dtype), vt)

    o = lax.map(attend_block, qb)
    o = o.transpose(1, 0, 4, 2, 3, 5).reshape(bsz, s, Q_WIDTH)
    return (o * jax.nn.silu(z)) @ w_out

def second_inputs(seed: int = 0) -> dict:
    key = jax.random.key(seed)
    ks = jax.random.split(key, 12)
    f32 = jnp.float32
    x = jax.random.normal(ks[0], (BATCH, SEQ, D_MODEL), f32)
    norm_even = 1.0 + 0.02 * jax.random.normal(ks[1], (N_EVEN, D_MODEL), f32)
    w_in_even = jax.random.normal(ks[2], (N_EVEN, D_MODEL, EVEN_IN), f32) * D_MODEL ** -0.5
    conv_w = jax.random.normal(ks[3], (N_EVEN, CONV_WIDTH, A_WIDTH), f32) * CONV_WIDTH ** -0.5
    w_out_even = jax.random.normal(ks[4], (N_EVEN, EVEN_MIX, D_MODEL), f32) * EVEN_MIX ** -0.5
    norm_odd = 1.0 + 0.02 * jax.random.normal(ks[5], (N_ODD, D_MODEL), f32)
    w_in_odd = jax.random.normal(ks[6], (N_ODD, D_MODEL, ODD_IN), f32) * D_MODEL ** -0.5
    q_gain = 1.0 + 0.02 * jax.random.normal(ks[7], (N_ODD, HEAD_DIM), f32)
    k_gain = 1.0 + 0.02 * jax.random.normal(ks[8], (N_ODD, HEAD_DIM), f32)
    w_out_odd = jax.random.normal(ks[9], (N_ODD, Q_WIDTH, D_MODEL), f32) * Q_WIDTH ** -0.5
    final_norm = 1.0 + 0.02 * jax.random.normal(ks[10], (D_MODEL,), f32)
    return {"x": x, "norm_even": norm_even, "w_in_even": w_in_even, "conv_w": conv_w,
            "w_out_even": w_out_even, "norm_odd": norm_odd, "w_in_odd": w_in_odd,
            "q_gain": q_gain, "k_gain": k_gain, "w_out_odd": w_out_odd,
            "final_norm": final_norm}

def second_block(x, norm_even, w_in_even, conv_w, w_out_even, norm_odd, w_in_odd,
              q_gain, k_gain, w_out_odd, final_norm):
    for layer in range(DEPTH):
        i = layer // 2
        if layer % 2 == 0:
            x = x + short_conv_fourier_mixer(rms_norm(x, norm_even[i]), w_in_even[i],
                                             conv_w[i], w_out_even[i])
        else:
            x = x + gqa_axial_mixer(rms_norm(x, norm_odd[i]), w_in_odd[i],
                                    q_gain[i], k_gain[i], w_out_odd[i])
    return rms_norm(x, final_norm)


def setup_inputs(seed=0):
    out = dict(first_inputs(seed))
    for name, value in second_inputs(seed + 1).items():
        if name != "x":
            out[name + "_2"] = value
    return out


def reference(
    x, meta_tokens, norm_pre, norm_post, rwkv_mu, rwkv_w_in, rwkv_w0, rwkv_w2, rwkv_a0, rwkv_a2,
    rwkv_k_k, rwkv_k_a, rwkv_r_k, rwkv_ln_w, rwkv_ln_b, rwkv_w_out, mla_w_in, mla_q_norm,
    mla_w_q_up, mla_kv_norm, mla_w_kv_up, mla_w_out, norm_even_2, w_in_even_2, conv_w_2,
    w_out_even_2, norm_odd_2, w_in_odd_2, q_gain_2, k_gain_2, w_out_odd_2, final_norm_2,
):
    x = first_block(
        x, meta_tokens, norm_pre, norm_post, rwkv_mu, rwkv_w_in, rwkv_w0, rwkv_w2, rwkv_a0,
        rwkv_a2, rwkv_k_k, rwkv_k_a, rwkv_r_k, rwkv_ln_w, rwkv_ln_b, rwkv_w_out, mla_w_in,
        mla_q_norm, mla_w_q_up, mla_kv_norm, mla_w_kv_up, mla_w_out,
    )
    return second_block(
        x, norm_even_2, w_in_even_2, conv_w_2, w_out_even_2, norm_odd_2, w_in_odd_2, q_gain_2,
        k_gain_2, w_out_odd_2, final_norm_2,
    )


_drawn_inputs = setup_inputs


def setup_inputs(seed=0):
    import zlib

    import numpy as np

    out = dict(_drawn_inputs(seed))
    spreads = {}
    factors = {'rwkv_k_k': 2.969,
     'rwkv_ln_w': 2.708,
     'mla_q_norm': 4.872,
     'mla_kv_norm': 3.178,
     'norm_even_2': 5.321,
     'norm_odd_2': 8.0,
     'q_gain_2': 29.949,
     'k_gain_2': 28.316,
     'final_norm_2': 8.186}
    for name, (base, spread) in spreads.items():
        noise = np.random.default_rng([zlib.crc32(name.encode()), seed]).standard_normal(out[name].shape)
        drawn = base * np.exp(spread * noise) if base else spread * noise
        out[name] = __import__('jax').numpy.asarray(drawn.astype(out[name].dtype))
    for name, factor in factors.items():
        out[name] = (out[name] * factor).astype(out[name].dtype)
    return out
```

```python
import math
from contextlib import ExitStack

import numpy as np

import concourse.bass as bass
from concourse import mybir

F32 = mybir.dt.float32
ALU = mybir.AluOpType
ACT = mybir.ActivationFunctionType
AX_X = mybir.AxisListType.X

P = 128
D = 1024
DI = 2048
SEQ = 512
META = 16
L = META + SEQ
HALF = L // 2
KD = D // P
KI = DI // P
PAIRS = DI // P
C = 64
NC = -(-L // C)
LP = NC * C
PAD = LP - L
LORA = 64
RMS_EPS = 1e-6
GN_EPS = 64e-5
EXP_M_HALF = math.exp(-0.5)
Q_TILES, KV_TILES = 4, 2
HEADS = 16
KROPE = 64
E_G, E_DIM = 4, 128
G_HEADS, G_KV = 8, 2
BIG = 1e30

SLOT = 1024
SLOTS = 4
LOADS = [("lora", 1), ("rwkv_in", 4 * PAIRS), ("rwkv_out", 2 * KD), ("mla_in", Q_TILES + KV_TILES + 1 + KI),
         ("mla_v", 4), ("mla_up", HEADS), ("mla_out", 2 * KD), ("even_in", 24), ("even_out", KD),
         ("odd_in", 2 * G_HEADS + G_KV), ("odd_v", 2), ("odd_out", KD)]
FIRST = {}
_n = 0
for _name, _count in LOADS:
    FIRST[_name] = _n
    _n += _count
N_LOADS = _n

PAR = {}
_n = 0
for _name, _count in [("pre0", KD), ("post0", KD), ("pre1", KD), ("post1", KD), ("mu", 6 * KD), ("rwkv", 7 * PAIRS),
                      ("q_norm", Q_TILES), ("kv_norm", KV_TILES), ("even", KD), ("conv", 12), ("odd", KD),
                      ("q_gain", 1), ("k_gain", 1), ("final", KD)]:
    PAR[_name] = _n
    _n += _count
N_PAR = _n
W0, A0, KK, KA, RK, LNW, LNB = range(7)

CON, CON_OF = {}, {}
_n = 0
for _part, _names in [("all", [("ident", P), ("ones", P), ("heads", P), ("reset", LP)]),
                      ("rwkv", [("levels", 6 * 3 * P), ("level0T", 3 * P), ("ident3", 3 * P), ("tri", 3 * 2 * C)]),
                      ("mla", [("causal", P), ("rot_mla", P), ("cos_mla", L), ("sin_mla", L)]),
                      ("odd", [("rot_odd", P), ("cos_odd", SEQ), ("sin_odd", SEQ), ("dft_d", 2 * E_DIM)])]:
    _first = _n
    for _name, _count in _names:
        CON[_name] = _n
        _n += _count
    CON_OF[_part] = (_first, _n - _first)
N_CON = _n

F_AR, F_B, F_K, F_V, F_SG, F_BON, F_PC = 0, 2 * LP, 3 * LP, 4 * LP, 5 * LP, 6 * LP, 7 * LP
F_COLS = F_PC + NC


class Count:

    def __init__(self, sem, per=1):
        self.sem, self.per = sem, per

    def at(self, i, k):
        return i * self.per + k

    def before(self, i):
        return i * self.per


class Ring:

    def __init__(self, tile, full, used):
        self.tile, self.full, self.used = tile, full, used

    def slot(self, load):
        return self.tile[:, load % SLOTS, :]

    def wait_full(self, eng, load, step=0):
        eng.wait_ge(self.full[load % SLOTS], (step + load // SLOTS + 1) * 16)

    def wait_used(self, eng, load, step=0):
        eng.wait_ge(self.used[load % SLOTS], step + load // SLOTS + 1)

    def done(self, load):
        return self.used[load % SLOTS]

    def load(self, sp, stream, load, step=0):
        if not (isinstance(step, int) and load + SLOTS * step < SLOTS):
            sp.wait_ge(self.used[load % SLOTS], step + load // SLOTS)
        sp.dma_start(self.slot(load), stream[step * SLOTS + load]).then_inc(self.full[load % SLOTS], 16)


class Norms:

    def __init__(self, squared, summed, rooted, inverted):
        self.squared, self.summed, self.rooted, self.inverted = squared, summed, rooted, inverted


def program(nc, x_in, stream, lora_in, par_in, con_in, dft_in, out, forms, mixed):
    with ExitStack() as ctx:
        def sb(name, *shape):
            return ctx.enter_context(nc.sbuf_tensor(name, [P, *shape], F32))

        def sem(name):
            return ctx.enter_context(nc.semaphore(name))

        wide = [ctx.enter_context(nc.psum_tensor(f"wide{j}", [P, 2, 512], F32)) for j in range(4)]
        ring = Ring(sb("weights", SLOTS, SLOT), [sem(f"weights_full{s}") for s in range(SLOTS)],
                    [sem(f"weights_used{s}") for s in range(SLOTS)])
        par = sb("par", N_PAR)
        con = sb("con", CON_OF["all"][1])
        inv_rms = sb("inv_rms", L)
        epsilon = sb("epsilon", 2)

        half_w0 = sb("half_w0a0", 2 * PAIRS)

        def cons(name, width):
            return con[:, CON[name]:CON[name] + width]

        def pcol(name, n=0):
            return par[:, PAR[name] + n:PAR[name] + n + 1]

        ident, ones, heads = cons("ident", P), cons("ones", P), cons("heads", P)

        x_loaded, con_loaded = sem("x_loaded"), sem("con_loaded")
        const_set, eps_set = sem("const_set"), sem("eps_set")
        phase_done = sem("phase_done")
        squared, summed, rooted, inverted = (sem(n) for n in ("squared", "summed", "rooted", "inverted"))
        applied = sem("applied")

        PHASES = {"pe": 0, "act": 0, "dve": 0, "pool": 0, "sp": 0}

        def end_phase(eng, who):
            PHASES[who] += 1
            eng.drain().then_inc(phase_done, 1)
            eng.wait_ge(phase_done, 4 * PHASES[who])

        class N:
            sq = 0
            n = 0

        def halves(ap, width):
            return ap.rearrange("p (b n) -> p b n", b=2) if width == L else ap

        def act_norm(act, st, src, kt, width, sq, ps, eps, div):
            for k in range(kt):
                act.activation(sq(k), src(k), ACT.Square).then_inc(squared, 1)
            st.sq += kt
            st.n += 1
            act.wait_ge(summed, st.n)
            act.activation(halves(inv_rms[:, 0:width], width), ps(width), ACT.Sqrt,
                           bias=epsilon[:, 0:1], scale=1.0 / div).then_inc(rooted, 1)

        def pe_norm(pe, st, kt, width, sq, ps):
            w = ps(width)
            parts = [(w[:, b, :], slice(b * HALF, (b + 1) * HALF)) for b in range(2)] if width == L else [(w, slice(0, width))]
            for k in range(kt):
                st.sq += 1
                pe.wait_ge(squared, st.sq)
                for dst, cols in parts:
                    mm = pe.matmul(dst, ones, sq(k)[:, cols], start=k == 0, stop=k == kt - 1)
            mm.then_inc(summed, 1)

        def dve_norm(dve, st, width):
            st.n += 1
            dve.wait_ge(rooted, st.n)
            dve.reciprocal(inv_rms[:, 0:width], inv_rms[:, 0:width]).then_inc(inverted, 1)
            dve.wait_ge(inverted, st.n)

        def wide_ps(j):
            return lambda width: wide[j][:, :, 0:HALF] if width == L else wide[j][:, 0, 0:width]

        norm = {who: N() for who in ("pe", "act", "dve")}
        for st in norm.values():
            st.sq = st.n = 0

        A = ExitStack()

        def sa(name, *shape):
            return A.enter_context(nc.sbuf_tensor(name, [P, *shape], F32))

        x_t = sa("x", KD, L)
        u = sa("u", KD, 1 + L)
        mixed_in = sa("mixed_in", 4, KD, L)
        diff = sa("diff", KD, L)
        lora = sa("lora", L)
        lora_w = sa("lora_w", P)
        a_r, a_k, a_lw, a_cum, a_a, a_kk, a_sq, a_inv, a_k2, a_rk, a_tg, a_Pinv = (
            sa(n, LP) for n in ("r", "k", "log_decay", "log_cum", "a", "kk", "kk_sq", "kk_inv", "k2", "rk", "tanh_g", "p_inv"))
        a_P = sa("p_cum", NC, 1 + C)
        form = sa("form", F_COLS)
        A.close()
        f_ar = form[:, F_AR:F_AR + 2 * LP].rearrange("p (c s n) -> p c s n", c=NC, s=2)
        f_b, f_k, f_v, f_sg, f_bon = (form[:, o:o + LP] for o in (F_B, F_K, F_V, F_SG, F_BON))
        f_pc = form[:, F_PC:F_PC + NC]
        LERP = {"k": 0, "r": 1, "v": 2, "g": 3}
        MU = {"r": 0, "k": 1, "v": 2, "g": 3, "w": 4, "a": 5}

        def real(ap):
            return ap[:, PAD:LP].rearrange("p (b n) -> p b n", b=2)

        def by_chunk(ap):
            return ap.rearrange("p (c n) -> p c n", c=NC)

        def rw(which, pair):
            if isinstance(pair, int):
                return pcol("rwkv", which * PAIRS + pair)
            return par[:, bass.ds(pair + (PAR["rwkv"] + which * PAIRS), 1)]

        a_sems = {n: sem("a_" + n) for n in (
            "lerp", "lora_loaded", "lora_low", "proj_w", "proj_a", "tanh_w", "tanh_a", "k_copied", "r_copied", "kk_squared",
            "p_exp", "kk_summed", "kk_rooted", "v_copied", "g_tanh", "pc_copied", "rk_summed", "dve", "pool", "stored")}

        def half_bias(n, pair):
            if isinstance(pair, int):
                return half_w0[:, n * PAIRS + pair:n * PAIRS + pair + 1]
            return half_w0[:, bass.ds(pair + n * PAIRS, 1)]

        s = a_sems
        DVE_A = Count(s["dve"], 15)
        POOL_A = Count(s["pool"], 2)
        EXP_A = Count(s["p_exp"], 2)

        def sp_setup(sp):
            for k in range(KD):
                sp.dma_start(x_t[:, k, :], x_in[:, k, :]).then_inc(x_loaded, 16)
            sp.dma_start(par[:], par_in).then_inc(con_loaded, 16)
            sp.dma_start(con[:], con_in[:, 0:CON_OF["all"][1]]).then_inc(con_loaded, 16)
            ring.load(sp, stream, 0)
            for j in range(3):
                ring.load(sp, stream, 1 + j)

        def act_setup(act):
            act.wait_ge(eps_set, 2)
            act.wait_ge(x_loaded, 16 * KD)
            act_norm(act, norm["act"], lambda k: x_t[:, k, :], KD, L, lambda k: mixed_in[:, 0, k, :], wide_ps(0), 0, D)

        def pe_setup(pe):
            pe.wait_ge(con_loaded, 32)
            pe_norm(pe, norm["pe"], KD, L, lambda k: mixed_in[:, 0, k, :], wide_ps(0))

        def pool_setup(pool):
            pool.memset(u[:, :, 0:1], 0.0).then_inc(const_set, 1)
            for t in (a_r, a_k, a_lw, a_a, a_kk, a_sq, a_inv, form):
                pool.memset(t[:], 0.0).then_inc(const_set, 1)
            pool.memset(a_P[:, :, 0:1], 1.0).then_inc(const_set, 1)

        N_SET = 10

        def dve_setup(dve):
            dve.memset(epsilon[:, 0:1], RMS_EPS).then_inc(eps_set, 1)
            dve.memset(epsilon[:, 1:2], GN_EPS).then_inc(eps_set, 1)
            dve.wait_ge(con_loaded, 32)
            dve.tensor_scalar(half_w0[:], par[:, PAR["rwkv"]:PAR["rwkv"] + 2 * PAIRS], 0.5, None, ALU.mult).then_inc(applied, 1)
            dve_norm(dve, norm["dve"], L)
            dve.wait_ge(const_set, N_SET)
            for k in range(KD):
                dve.scalar_tensor_tensor(u[:, k, 1:], x_t[:, k, :], pcol("pre0", k), inv_rms[:], ALU.mult, ALU.mult).then_inc(applied, 1)
            dve.wait_ge(applied, 1 + KD)
            dve.tensor_tensor(diff[:], u[:, :, 0:L], u[:, :, 1:], ALU.subtract).then_inc(applied, 1)
            dve.wait_ge(applied, 2 + KD)

            def lerp(dst, which):
                for k in range(KD):
                    dve.scalar_tensor_tensor(dst[:, k, :], diff[:, k, :], pcol("mu", MU[which] * KD + k), u[:, k, 1:],
                                             ALU.mult, ALU.add).then_inc(s["lerp"], 1)
            lerp(mixed_in[:, 2], "w")
            lerp(mixed_in[:, 3], "a")
            lerp(mixed_in[:, 0], "k")
            lerp(mixed_in[:, 1], "r")
            dve.wait_ge(s["proj_w"], 1)
            dve.wait_ge(s["proj_a"], 1)
            lerp(mixed_in[:, 2], "v")
            lerp(mixed_in[:, 3], "g")

        def product(pe, dst, load, rhs, step=0, kt=KD):
            for b in range(2):
                for k in range(kt):
                    mm = pe.matmul(dst[:, b, 0:HALF], ring.slot(load)[:, k * P:(k + 1) * P], rhs[:, k, b * HALF:(b + 1) * HALF],
                                   start=k == 0, stop=k == kt - 1)
            return mm

        def pe_lora(pe):
            ring.wait_full(pe, 0)
            pe.wait_ge(s["lerp"], KD)
            product(pe, wide[0], 0, mixed_in[:, 2]).then_inc(s["proj_w"], 1)
            pe.wait_ge(s["lerp"], 2 * KD)
            product(pe, wide[1], 0, mixed_in[:, 3]).then_inc(ring.done(0), 1)
            pe.drain().then_inc(s["proj_a"], 1)

        def act_lora(act):
            act.wait_ge(s["proj_w"], 1)
            act.activation(lora[0:LORA, :].rearrange("p (b n) -> p b n", b=2), wide[0][0:LORA, :, 0:HALF], ACT.Tanh).then_inc(s["lora_low"], 1)
            act.wait_ge(s["proj_a"], 1)
            act.activation(lora[LORA:P, :].rearrange("p (b n) -> p b n", b=2), wide[1][LORA:P, :, 0:HALF], ACT.Copy).then_inc(s["lora_low"], 1)

        LERP_OF = [("k", 2), ("r", 3), ("v", 0), ("g", 1)]

        def pe_pair(pe, i, first):
            pe.wait_ge(s["lora_loaded"], 16 * i + 16)
            if first:
                pe.wait_ge(s["lora_low"], 2)
            else:
                pe.wait_ge(s["v_copied"], i)
            for b in range(2):
                mm = pe.matmul(wide[0][:, b, 0:HALF], lora_w[0:LORA, :], lora[0:LORA, b * HALF:(b + 1) * HALF], start=True, stop=True)
            mm.then_inc(s["proj_w"], 1)
            if not first:
                pe.wait_ge(DVE_A.sem, DVE_A.before(i))
            for b in range(2):
                mm = pe.matmul(wide[1][:, b, 0:HALF], lora_w[LORA:P, :], lora[LORA:P, b * HALF:(b + 1) * HALF], start=True, stop=True)
            mm.then_inc(s["proj_a"], 1)

            def project(j, dst, lerps):
                ring.wait_full(pe, 1 + j, i)
                if first:
                    pe.wait_ge(s["lerp"], lerps * KD)
                product(pe, dst, 1 + j, mixed_in[:, j], i).then_inc(ring.done(1 + j), 1)

            if not first:
                pe.wait_ge(s["kk_rooted"], i)
            project(0, wide[2], 3)
            project(1, wide[3], 4)
            pe.wait_ge(s["tanh_w"], i + 1)
            project(2, wide[0], 5)
            pe.wait_ge(s["k_copied"], i + 1)
            pe.wait_ge(s["kk_squared"], i + 1)
            for b in range(2):
                mm = pe.matmul(wide[2][:, b, 0:HALF], heads, a_sq[:, PAD + b * HALF:PAD + (b + 1) * HALF], start=True, stop=True)
            mm.then_inc(s["kk_summed"], 1)
            pe.wait_ge(s["tanh_a"], i + 1)
            project(3, wide[1], 6)
            pe.wait_ge(s["r_copied"], i + 1)
            pe.wait_ge(DVE_A.sem, DVE_A.at(i, 13))
            for b in range(2):
                mm = pe.matmul(wide[3][:, b, 0:HALF], heads, a_rk[:, PAD + b * HALF:PAD + (b + 1) * HALF], start=True, stop=True)
            mm.then_inc(s["rk_summed"], 1)

        def act_pair(act, i, first):
            if first:
                act.wait_ge(const_set, N_SET)
                act.wait_ge(applied, 1)
            else:
                act.wait_ge(DVE_A.sem, DVE_A.before(i))
                act.wait_ge(POOL_A.sem, POOL_A.before(i))
            act.wait_ge(s["proj_w"], i + 2)
            act.activation(real(a_lw), wide[0][:, :, 0:HALF], ACT.Tanh, bias=half_bias(0, i), scale=0.5).then_inc(s["tanh_w"], 1)
            act.wait_ge(s["proj_a"], i + 2)
            act.activation(real(a_a), wide[1][:, :, 0:HALF], ACT.Tanh, bias=half_bias(1, i), scale=0.5).then_inc(s["tanh_a"], 1)
            act.wait_ge(DVE_A.sem, DVE_A.at(i, 2))
            act.activation(a_P[:, :, 1:], by_chunk(a_cum[:]), ACT.Exp).then_inc(EXP_A.sem, 1)
            act.activation(a_Pinv[:], a_cum[:], ACT.Exp, scale=-1.0).then_inc(EXP_A.sem, 1)
            ring.wait_used(act, 1, i)
            act.activation(real(a_k), wide[2][:, :, 0:HALF], ACT.Copy).then_inc(s["k_copied"], 1)
            act.wait_ge(DVE_A.sem, DVE_A.at(i, 3))
            act.activation(a_sq[:], a_kk[:], ACT.Square).then_inc(s["kk_squared"], 1)
            ring.wait_used(act, 2, i)
            act.activation(real(a_r), wide[3][:, :, 0:HALF], ACT.Copy).then_inc(s["r_copied"], 1)
            ring.wait_used(act, 3, i)
            if not first:
                act.wait_ge(s["stored"], 16 * i)
            act.activation(real(f_v), wide[0][:, :, 0:HALF], ACT.Copy).then_inc(s["v_copied"], 1)
            act.wait_ge(s["kk_summed"], i + 1)
            act.activation(real(a_inv), wide[2][:, :, 0:HALF], ACT.Sqrt).then_inc(s["kk_rooted"], 1)
            ring.wait_used(act, 4, i)
            act.activation(real(a_tg), wide[1][:, :, 0:HALF], ACT.Tanh, scale=0.5).then_inc(s["g_tanh"], 1)
            act.wait_ge(EXP_A.sem, EXP_A.at(i, 1))
            act.activation(f_pc, a_P[:, :, C:C + 1].rearrange("p c n -> p (c n)"), ACT.Copy).then_inc(s["pc_copied"], 1)

        def dve_pair(dve, i, first):
            def step(ins):
                ins.then_inc(DVE_A.sem, 1)

            def after(k):
                dve.wait_ge(DVE_A.sem, DVE_A.at(i, k))

            half = 0.5 * EXP_M_HALF
            dve.wait_ge(s["tanh_w"], i + 1)
            step(dve.tensor_scalar(a_lw[:, PAD:], a_lw[:, PAD:], -half, -half, ALU.mult, ALU.add))
            after(1)
            step(dve.tensor_tensor_scan(a_cum[:], cons("reset", LP), a_lw[:], 0.0, ALU.mult, ALU.add))
            dve.wait_ge(s["k_copied"], i + 1)
            step(dve.tensor_scalar(a_kk[:], a_k[:], rw(KK, i), None, ALU.mult))
            dve.wait_ge(s["tanh_a"], i + 1)
            step(dve.tensor_scalar(a_a[:, PAD:], a_a[:, PAD:], 0.5, 0.5, ALU.mult, ALU.add))
            dve.wait_ge(s["kk_rooted"], i + 1)
            step(dve.tensor_scalar(a_inv[:, PAD:], a_inv[:, PAD:], 1e-12, None, ALU.max))
            after(5)
            step(dve.reciprocal(a_inv[:, PAD:], a_inv[:, PAD:]))
            after(6)
            step(dve.tensor_tensor(a_kk[:, PAD:], a_kk[:, PAD:], a_inv[:, PAD:], ALU.mult))
            after(7)
            dve.wait_ge(EXP_A.sem, EXP_A.at(i, 2))
            if not first:
                dve.wait_ge(s["stored"], 16 * i)
            step(dve.scalar_tensor_tensor(f_ar[:, :, 0, :], by_chunk(a_kk[:]), -1.0, a_P[:, :, 0:C], ALU.mult, ALU.mult))
            step(dve.tensor_tensor(a_inv[:, PAD:], a_kk[:, PAD:], a_a[:, PAD:], ALU.mult))
            after(9)
            step(dve.tensor_tensor(f_b[:, PAD:], a_inv[:, PAD:], a_Pinv[:, PAD:], ALU.mult))
            step(dve.tensor_scalar(a_k2[:], a_a[:], 1.0, rw(KA, i), ALU.subtract, ALU.mult))
            after(11)
            step(dve.scalar_tensor_tensor(a_k2[:], a_k2[:], 1.0, a_k[:], ALU.add, ALU.mult))
            after(12)
            dve.wait_ge(s["r_copied"], i + 1)
            step(dve.scalar_tensor_tensor(a_rk[:], a_r[:], rw(RK, i), a_k2[:], ALU.mult, ALU.mult))
            dve.wait_ge(s["v_copied"], i + 1)
            dve.wait_ge(s["rk_summed"], i + 1)
            step(dve.tensor_tensor(real(f_bon), wide[3][:, :, 0:HALF], real(f_v), ALU.mult))
            dve.wait_ge(s["g_tanh"], i + 1)
            step(dve.scalar_tensor_tensor(real(f_sg), real(a_tg), 1.0, wide[1][:, :, 0:HALF], ALU.add, ALU.mult))

        def pool_pair(pool, i, first):
            pool.wait_ge(EXP_A.sem, EXP_A.at(i, 2))
            if not first:
                pool.wait_ge(s["stored"], 16 * i)
            pool.wait_ge(DVE_A.sem, DVE_A.at(i, 12))
            pool.tensor_tensor(f_k, a_k2[:], a_Pinv[:], ALU.mult).then_inc(POOL_A.sem, 1)
            pool.wait_ge(s["r_copied"], i + 1)
            pool.tensor_tensor(f_ar[:, :, 1, :], by_chunk(a_r[:]), a_P[:, :, 1:], ALU.mult).then_inc(POOL_A.sem, 1)

        def sp_store(sp, i):
            sp.wait_ge(DVE_A.sem, DVE_A.at(i, 15))
            sp.wait_ge(POOL_A.sem, POOL_A.at(i, 2))
            sp.wait_ge(s["v_copied"], i + 1)
            sp.wait_ge(s["pc_copied"], i + 1)
            sp.dma_start(forms[i], form[:]).then_inc(s["stored"], 16)

        def sp_a(sp):
            sp.dma_start(lora_w[:], lora_in[0]).then_inc(s["lora_loaded"], 16)
            ring.load(sp, stream, 4)
            with sp.Fori(1, PAIRS) as i:
                sp.wait_ge(s["proj_a"], i + 1)
                sp.dma_start(lora_w[:], lora_in[i]).then_inc(s["lora_loaded"], 16)
                for j in range(4):
                    ring.load(sp, stream, 1 + j, i)
                sp_store(sp, i - 1)
            sp_store(sp, PAIRS - 1)

        def over_pairs(eng, body):
            body(eng, 0, True)
            with eng.Fori(1, PAIRS) as i:
                body(eng, i, False)

        B = ExitStack()

        def sbb(name, *shape):
            return B.enter_context(nc.sbuf_tensor(name, [P, *shape], F32))

        GROUPS, GC = 3, NC // 3
        LEVEL_BUFS = 3
        LEVELS = 5
        b_ar = sbb("a_r", NC, 2, C)
        b_b, b_k, b_v = (sbb(n, NC, P) for n in ("b_diag", "k_diag", "v_diag"))
        b_a, b_r = (sbb(n, 2, NC, P) for n in ("a_diag", "r_diag"))
        b_sgbon, b_pc = sbb("gate_bonus", 2, 2, LP), sbb("p_chunk", 2, NC)
        qg = sbb("b_with_a_r", 2, NC, 2, P)
        mg = sbb("k_with_a_r", 2, NC, 2, P)
        tokens_of = sbb("token_rows", 2, 3, NC, P)
        n_all, n_lvl = sbb("n", NC, P), sbb("n_levels", LEVEL_BUFS, NC, P)
        w_inv = sbb("w_inv", 2, NC, P)
        x_inv, e_mid = sbb("x_inv", NC, P), sbb("e_mid", NC, P)
        state, state_p, r_row, u_row = (sbb(n, P) for n in ("state", "state_decayed", "r_rows", "u_rows"))
        y_rows, y_sq, y_diag = sbb("y_rows", NC, C), sbb("y_sq", NC, C), sbb("y_diag", NC, P)
        y_sum, y_mean, y_var = sbb("y_sum", NC), sbb("y_mean", NC), sbb("y_var", NC)
        b_con = sbb("masks", CON_OF["rwkv"][1])
        y_ln = sbb("y_ln", NC, C)
        B.close()
        inv_bank = [wide[0][:, 0, :], wide[0][:, 1, :], wide[1][:, 0, :]]
        odd_bank = [wide[1][:, 1, :], wide[2][:, 0, :]]
        chunk_bank, y_bank, post_bank = wide[2][:, 1, :], wide[3][:, 0, :], wide[3][:, 1, :]
        state_bank = odd_bank[1]
        b_names = ("forms_loaded", "scan_loaded", "qg_made", "mg_made", "token_mm", "token_rows", "n_turned", "n_rows",
                   "w_start", "x_start", "n_level", "e_mm", "e_rows", "w_mm", "w_added", "x_turned", "x_rows", "r_mm", "r_rows",
                   "u_mm", "u_rows", "s_mm", "s_rows", "y_mm", "y_rows", "g_mm", "k_mm", "post", "y_rooted", "y_turned", "z_sum",
                   "z_made", "z_stored", "diag_set")
        sb_ = {n: sem("b_" + n) for n in b_names}
        q = sb_
        HEAD_ROWS = (slice(0, C), slice(C, P))
        N_DIAG = 9
        POST = 15

        def three(ap):
            return ap[:, 0:GC * P].rearrange("p (c n) -> p c n", c=GC)

        def grp(g):
            return slice(g * GC, (g + 1) * GC)

        def con3(name, n=0):
            at = CON[name] - CON_OF["rwkv"][0] + n * GC * P
            return b_con[:, at:at + GC * P].rearrange("p (c n) -> p c n", c=GC)

        def sp_diag(sp, dst, pair, col, sem_):
            for hd, rows in enumerate(HEAD_ROWS):
                sp.dma_start(dst[rows, :, hd * C:(hd + 1) * C], forms[pair, rows, col:col + LP].rearrange("p (c n) -> p c n", c=NC)).then_inc(sem_, 16)

        def sp_b_pair(sp, i, par_, post):
            if not (isinstance(i, int) and i == 0):
                sp.wait_ge(q["token_mm"], 9 * i)
            sp.dma_start(b_ar[:], forms[i, :, F_AR:F_AR + 2 * LP].rearrange("p (c s n) -> p c s n", c=NC, s=2)).then_inc(q["forms_loaded"], 16)
            for dst, col in ((b_b, F_B), (b_k, F_K), (b_v, F_V)):
                sp_diag(sp, dst, i, col, q["forms_loaded"])
            if post:
                sp.wait_ge(q["y_mm"], 9 * (i - 1))
                sp.wait_ge(q["s_rows"], 9 * (i - 1))
            for dst, o in ((b_a, 0), (b_r, 1)):
                for hd, rows in enumerate(HEAD_ROWS):
                    src = forms[i, rows, F_AR:F_AR + 2 * LP].rearrange("p (c s n) -> p c s n", c=NC, s=2)
                    sp.dma_start(dst[rows, par_, :, hd * C:(hd + 1) * C], src[:, :, o, :]).then_inc(q["scan_loaded"], 16)
            sp.dma_start(b_pc[:, par_, :], forms[i, :, F_PC:F_PC + NC]).then_inc(q["scan_loaded"], 16)
            if post:
                sp_z(sp, i - 2, par_)
                sp.wait_ge(q["z_stored"], 16 * (i - 1))
            sp.dma_start(b_sgbon[:, par_], forms[i, :, F_SG:F_SG + 2 * LP].rearrange("p (s n) -> p s n", s=2)).then_inc(q["scan_loaded"], 16)

        FORMS_DMAS, SCAN_DMAS = 16 * 7, 16 * 6

        def sp_z(sp, pair, par_):
            sp.wait_ge(q["z_made"], pair + 1)
            sp.dma_start(mixed[pair], b_sgbon[:, par_, 0, PAD:]).then_inc(q["z_stored"], 16)

        def is0(i):
            return isinstance(i, int) and i == 0

        def pe_pass(pe, i, par_, inv, scan, post):
            p = i - 1
            step = [0]

            def walk():
                if not scan or step[0] == 3 * NC:
                    return
                c, part = divmod(step[0], 3)
                step[0] += 1
                pw = 1 - par_
                if part == 0:
                    if c == 0:
                        pe.wait_ge(q["scan_loaded"], SCAN_DMAS * i)
                        pe.wait_ge(q["mg_made"], GROUPS * i)
                        pe.wait_ge(q["token_rows"], 9 * i)
                    mm = pe.matmul(chunk_bank[:, 0:P], mg[:, pw, c, 0, :], tokens_of[:, pw, 2, c, :], start=True, stop=c == 0)
                    if c > 0:
                        pe.wait_ge(q["s_rows"], 9 * p + c)
                        mm = pe.matmul(chunk_bank[:, 0:P], b_a[:, pw, c, :], state[:], start=False, stop=True)
                    mm.then_inc(q["r_mm"], 1)
                    if c == 0:
                        if inv:
                            pe.wait_ge(q["token_rows"], 9 * i + 9)
                        if not is0(p):
                            pe.wait_ge(q["s_rows"], 9 * p)
                    pe.matmul(state_bank[:, 0:P], tokens_of[:, pw, 1, c, :], tokens_of[:, pw, 2, c, :], start=True, stop=False)
                    if not (is0(p) and c == 0):
                        pe.wait_ge(q["y_rows"], 9 * p + c)
                    if c > 0:
                        pe.matmul(y_bank[:, 0:P], b_r[:, pw, c, :], state[:], start=True, stop=False)
                    pe.matmul(y_bank[:, 0:P], mg[:, pw, c, 1, :], tokens_of[:, pw, 2, c, :], start=c == 0, stop=False)
                elif part == 1:
                    pe.wait_ge(q["r_rows"], 9 * p + c + 1)
                    if c == 0:
                        pe.wait_ge(q["w_added"], 15 * i)
                    pe.matmul(chunk_bank[:, P:2 * P], w_inv[:, pw, c, :], r_row[:], start=True, stop=True).then_inc(q["u_mm"], 1)
                else:
                    pe.wait_ge(q["u_rows"], 9 * p + c + 1)
                    pe.matmul(state_bank[:, 0:P], tokens_of[:, pw, 0, c, :], u_row[:], start=False, stop=True).then_inc(q["s_mm"], 1)
                    pe.matmul(y_bank[:, 0:P], qg[:, pw, c, 1, :], u_row[:], start=False, stop=True).then_inc(q["y_mm"], 1)

            if inv:
                pe.wait_ge(q["forms_loaded"], FORMS_DMAS * i + FORMS_DMAS)
                if not is0(i):
                    pe.wait_ge(q["w_added"], 15 * i)
                for g in range(GROUPS):
                    for c in range(GC):
                        mm = pe.matmul(inv_bank[g][:, c * P:(c + 1) * P], b_b[:, g * GC + c, :], b_ar[:, g * GC + c], start=True, stop=True)
                    mm.then_inc(q["g_mm"], 1)
                if not is0(i):
                    pe.wait_ge(q["token_rows"], 9 * i)
                    if not (isinstance(i, int) and i == 1):
                        pe.wait_ge(q["s_rows"], 9 * (i - 1))
                for g in range(GROUPS):
                    if g == 2:
                        pe.wait_ge(q["mg_made"], GROUPS * i + 1)
                    for c in range(GC):
                        mm = pe.matmul(odd_bank[g % 2][:, c * P:(c + 1) * P], b_k[:, g * GC + c, :], b_ar[:, g * GC + c], start=True, stop=True)
                    mm.then_inc(q["k_mm"], 1)
                for g in range(GROUPS):
                    pe.wait_ge(q["qg_made"], GROUPS * i + g + 1)
                    for c in range(GC):
                        mm = pe.transpose(inv_bank[g][:, c * P:(c + 1) * P], qg[:, par_, g * GC + c, 0, :], ident)
                    mm.then_inc(q["n_turned"], 1)
                for n in range(9):
                    src = (b_b, b_k, b_v)[n // 3]
                    if n < 2:
                        pe.wait_ge(q["mg_made"], GROUPS * i + n + 2)
                    else:
                        pe.wait_ge(q["token_rows"], 9 * i + n - 1)
                    for c in range(GC):
                        mm = pe.transpose(odd_bank[(n + 1) % 2][:, c * P:(c + 1) * P], src[:, n % 3 * GC + c, :], ident)
                    mm.then_inc(q["token_mm"], 1)
            if post:
                for g in range(GROUPS):
                    if g == 0:
                        pe.wait_ge(q["post"], POST * (i - 2) + 9)
                    else:
                        pe.wait_ge(q["post"], POST * (i - 2) + 9 + 2 * g)
                    for c in range(GC):
                        mm = pe.transpose(post_bank[:, c * P:(c + 1) * P], y_diag[:, g * GC + c, :], ident)
                    mm.then_inc(q["y_turned"], 1)
            if inv:
                for lv in range(LEVELS):
                    for g in range(GROUPS):
                        if lv == 0:
                            pe.wait_ge(q["w_start"], 6 * i + 2 * g + 2)
                            pe.wait_ge(q["n_rows"], GROUPS * i + g + 1)
                        else:
                            pe.wait_ge(q["x_rows"], 12 * i + 3 * lv - 2 + g)
                        pe.wait_ge(q["n_level"], 15 * i + 3 * lv + g + 1)
                        for c in range(GC):
                            mm = pe.matmul(inv_bank[g][:, c * P:(c + 1) * P], n_lvl[:, lv % LEVEL_BUFS, g * GC + c, :], w_inv[:, par_, g * GC + c, :], start=True, stop=True)
                        mm.then_inc(q["e_mm"], 1)
                        walk()
                    for g in range(GROUPS):
                        pe.wait_ge(q["e_rows"], 15 * i + 3 * lv + g + 1)
                        if lv == 0:
                            pe.wait_ge(q["x_start"], 6 * i + 2 * g + 2)
                        for c in range(GC):
                            mm = pe.matmul(inv_bank[g][:, c * P:(c + 1) * P], x_inv[:, g * GC + c, :], e_mid[:, g * GC + c, :], start=True, stop=True)
                        mm.then_inc(q["w_mm"], 1)
                        if g != 1 or lv < 2:
                            walk()
                    if lv < LEVELS - 1:
                        for g in range(GROUPS):
                            pe.wait_ge(q["w_added"], 15 * i + 3 * lv + g + 1)
                            for c in range(GC):
                                mm = pe.transpose(inv_bank[g][:, c * P:(c + 1) * P], w_inv[:, par_, g * GC + c, :], ident)
                            mm.then_inc(q["x_turned"], 1)
            while scan and step[0] < 3 * NC:
                walk()

        def act_pass(act, i, par_, inv, scan, post):
            p = i - 1
            step = [0]

            def walk():
                if not scan or step[0] == 3 * NC:
                    return
                c, part = divmod(step[0], 3)
                step[0] += 1
                if part == 0:
                    act.wait_ge(q["r_mm"], 9 * p + c + 1)
                    act.activation(r_row[:], chunk_bank[:, 0:P], ACT.Copy).then_inc(q["r_rows"], 1)
                elif part == 2:
                    act.wait_ge(q["y_mm"], 9 * p + c + 1)
                    if c == 0 and not is0(p):
                        act.wait_ge(q["post"], POST * (p - 1) + 3)
                    for hd, rows in enumerate(HEAD_ROWS):
                        ins = act.activation(y_rows[rows, c, :], y_bank[rows, hd * C:(hd + 1) * C], ACT.Copy)
                    ins.then_inc(q["y_rows"], 1)

            if inv:
                if not is0(i):
                    act.wait_ge(q["n_level"], 15 * i)
                for g in range(GROUPS):
                    act.wait_ge(q["n_turned"], GROUPS * i + g + 1)
                    act.activation(n_all[:, grp(g), :], three(inv_bank[g]), ACT.Copy).then_inc(q["n_rows"], 1)
                for n in range(9):
                    act.wait_ge(q["token_mm"], 9 * i + n + 1)
                    act.activation(tokens_of[:, par_, n // 3, grp(n % 3), :], three(odd_bank[(n + 1) % 2]), ACT.Copy).then_inc(q["token_rows"], 1)
            if post:
                act.wait_ge(q["post"], POST * (i - 2) + 6)
                act.activation(y_var[:], y_var[:], ACT.Sqrt, bias=epsilon[:, 1:2], scale=1.0 / C).then_inc(q["y_rooted"], 1)
            if inv:
                for lv in range(LEVELS):
                    for g in range(GROUPS):
                        act.wait_ge(q["e_mm"], 15 * i + 3 * lv + g + 1)
                        act.activation(e_mid[:, grp(g), :], three(inv_bank[g]), ACT.Copy).then_inc(q["e_rows"], 1)
                        walk()
                    for g in range(GROUPS):
                        if g != 1 or lv < 2:
                            walk()
                    if lv < LEVELS - 1:
                        for g in range(GROUPS):
                            act.wait_ge(q["x_turned"], 12 * i + 3 * lv + g + 1)
                            act.activation(x_inv[:, grp(g), :], three(inv_bank[g]), ACT.Copy).then_inc(q["x_rows"], 1)
            while scan and step[0] < 3 * NC:
                walk()

        def dve_pass(dve, i, par_, inv, scan, post):
            p = i - 1
            pw = 1 - par_
            step = [0]

            def walk():
                if not scan or step[0] == 3 * NC:
                    return
                c, part = divmod(step[0], 3)
                step[0] += 1
                if part == 1:
                    dve.wait_ge(q["u_mm"], 9 * p + c + 1)
                    dve.tensor_copy(u_row[:], chunk_bank[:, P:2 * P]).then_inc(q["u_rows"], 1)
                elif part == 2:
                    if c == 0:
                        dve.wait_ge(q["scan_loaded"], SCAN_DMAS * i)
                    dve.wait_ge(q["s_mm"], 9 * p + c + 1)
                    decay = b_pc[:, pw, c:c + 1]
                    if c == 0:
                        dve.tensor_scalar(state[:], state_bank[:, 0:P], decay, None, ALU.mult).then_inc(q["s_rows"], 1)
                    else:
                        dve.wait_ge(q["z_sum"], 8 * p + c)
                        dve.scalar_tensor_tensor(state[:], state_bank[:, 0:P], decay, state_p[:], ALU.mult, ALU.add).then_inc(q["s_rows"], 1)
                    if c < NC - 1:
                        dve.wait_ge(q["s_rows"], 9 * p + c + 1)
                        dve.tensor_scalar(state_p[:], state[:], b_pc[:, pw, c + 1:c + 2], None, ALU.mult).then_inc(q["z_sum"], 1)

            def done(k):
                return q["post"]

            if inv:
                for bank, mm, dst, made in ((inv_bank, "g_mm", qg, "qg_made"), (None, "k_mm", mg, "mg_made")):
                    for g in range(GROUPS):
                        src = bank[g] if bank else odd_bank[g % 2]
                        dve.wait_ge(q[mm], GROUPS * i + g + 1)
                        for hd, rows in enumerate(HEAD_ROWS):
                            ins = dve.tensor_tensor(dst[rows, par_, grp(g), :, hd * C:(hd + 1) * C],
                                                    src[rows, 0:GC * P].rearrange("p (c s n) -> p c s n", c=GC, s=2),
                                                    con3("tri")[rows].rearrange("p c (s n) -> p c s n", s=2), ALU.mult)
                        ins.then_inc(q[made], 1)
            if post:
                dve_post(dve, i - 2, par_)
            if inv:
                for lv in range(LEVELS):
                    for g in range(GROUPS):
                        walk()
                    for g in range(GROUPS):
                        dve.wait_ge(q["w_mm"], 15 * i + 3 * lv + g + 1)
                        w = w_inv[:, par_, grp(g), :]
                        dve.tensor_tensor(w, three(inv_bank[g]), w, ALU.add).then_inc(q["w_added"], 1)
                        if g != 1 or lv < 2:
                            walk()
            while scan and step[0] < 3 * NC:
                walk()
            if scan:
                dve_stats(dve, p)

        def dve_stats(dve, p):
            def step(ins):
                ins.then_inc(q["post"], 1)

            def after(k):
                dve.wait_ge(q["post"], POST * p + k)

            dve.wait_ge(q["y_rows"], 9 * p + 9)
            step(dve.tensor_reduce(y_sum[:], y_rows[:], AX_X, ALU.add))
            after(1)
            step(dve.tensor_scalar(y_mean[:], y_sum[:], 1.0 / C, None, ALU.mult))
            after(2)
            step(dve.tensor_tensor(y_sq[:], y_rows[:], y_mean[:].unsqueeze(2).to_broadcast([P, NC, C]), ALU.subtract))
            after(3)
            step(dve.tensor_tensor(y_ln[:], y_sq[:], y_sq[:], ALU.mult))
            after(4)
            step(dve.tensor_reduce(y_sum[:], y_ln[:], AX_X, ALU.add))
            after(5)
            step(dve.tensor_copy(y_var[:], y_sum[:]))

        def dve_post(dve, p, pp):
            def step(ins):
                ins.then_inc(q["post"], 1)

            def after(k):
                dve.wait_ge(q["post"], POST * p + k)

            dve.wait_ge(q["y_rooted"], p + 1)
            step(dve.reciprocal(y_mean[:], y_var[:]))
            after(7)
            for hd, rows in enumerate(HEAD_ROWS):
                step(dve.tensor_tensor(y_diag[rows, :, hd * C:(hd + 1) * C], y_sq[rows],
                                       y_mean[rows].unsqueeze(2).to_broadcast([C, NC, C]), ALU.mult))
            for g in range(GROUPS):
                dve.wait_ge(q["y_turned"], GROUPS * p + g + 1)
                for hd, rows in enumerate(HEAD_ROWS):
                    step(dve.tensor_scalar(y_ln[rows, grp(g), :], three(post_bank)[rows, :, hd * C:(hd + 1) * C],
                                           rw(LNW, p)[rows], rw(LNB, p)[rows], ALU.mult, ALU.add))
            after(15)
            gate, bonus = b_sgbon[:, pp, 0, PAD:], b_sgbon[:, pp, 1, PAD:]
            y = y_ln[:].rearrange("p c n -> p (c n)")[:, PAD:]
            dve.wait_ge(q["scan_loaded"], SCAN_DMAS * p + SCAN_DMAS)
            dve.tensor_tensor(bonus, y, bonus, ALU.add).then_inc(q["diag_set"], 1)
            dve.wait_ge(q["diag_set"], N_DIAG + p + 1)
            dve.scalar_tensor_tensor(gate, bonus, 0.5, gate, ALU.mult, ALU.mult).then_inc(q["z_made"], 1)

        def pool_pass(pool, i, par_, inv, scan, post):
            if not inv:
                return
            if is0(i):
                pool.wait_ge(con_loaded, 48)
            for g in range(GROUPS):
                pool.wait_ge(q["qg_made"], GROUPS * i + g + 1)
                w = w_inv[:, par_, grp(g), :]
                pool.tensor_tensor(w, qg[:, par_, grp(g), 0, :], con3("level0T"), ALU.mult).then_inc(q["w_start"], 1)
                pool.wait_ge(q["w_start"], 6 * i + 2 * g + 1)
                pool.tensor_tensor(w, w, con3("ident3"), ALU.add).then_inc(q["w_start"], 1)
            for g in range(GROUPS):
                pool.wait_ge(q["n_rows"], GROUPS * i + g + 1)
                pool.tensor_tensor(n_lvl[:, 0, grp(g), :], n_all[:, grp(g), :], con3("levels", 1), ALU.mult).then_inc(q["n_level"], 1)
                x = x_inv[:, grp(g), :]
                pool.tensor_tensor(x, n_all[:, grp(g), :], con3("levels", 0), ALU.mult).then_inc(q["x_start"], 1)
                pool.wait_ge(q["x_start"], 6 * i + 2 * g + 1)
                pool.tensor_tensor(x, x, con3("ident3"), ALU.add).then_inc(q["x_start"], 1)
            for lv in range(1, LEVELS):
                for g in range(GROUPS):
                    if lv >= LEVEL_BUFS:
                        pool.wait_ge(q["e_mm"], 15 * i + 3 * (lv - LEVEL_BUFS) + g + 1)
                    pool.tensor_tensor(n_lvl[:, lv % LEVEL_BUFS, grp(g), :], n_all[:, grp(g), :], con3("levels", lv + 1), ALU.mult).then_inc(q["n_level"], 1)

        def dve_b_setup(dve):
            dve.wait_ge(s["stored"], 16 * PAIRS)
            for t in (b_b, b_k, b_v, b_a, b_r, qg, mg, y_diag, state):
                dve.memset(t[:], 0.0).then_inc(q["diag_set"], 1)
            dve.wait_ge(q["diag_set"], N_DIAG)
            dve.wait_ge(con_loaded, 48)

        def passes(eng, body):
            body(eng, 0, 0, True, False, False)
            body(eng, 1, 1, True, True, False)
            with eng.Fori(1, PAIRS // 2) as j:
                body(eng, 2 * j, 0, True, True, True)
                body(eng, 2 * j + 1, 1, True, True, True)
            body(eng, PAIRS, 0, False, True, True)
            body(eng, PAIRS + 1, 1, False, False, True)

        def sp_b(sp):
            sp.wait_ge(phase_done, 4)
            sp.wait_ge(s["stored"], 16 * PAIRS)
            first, n = CON_OF["rwkv"]
            sp.dma_start(b_con[:], con_in[:, first:first + n]).then_inc(con_loaded, 16)
            sp.wait_ge(q["diag_set"], N_DIAG)
            sp_b_pair(sp, 0, 0, False)
            sp_b_pair(sp, 1, 1, False)
            with sp.Fori(1, PAIRS // 2) as j:
                sp_b_pair(sp, 2 * j, 0, True)
                sp_b_pair(sp, 2 * j + 1, 1, True)
            sp_z(sp, PAIRS - 2, 0)
            sp_z(sp, PAIRS - 1, 1)

        h = sb("h", KD, L)
        m_t = sb("mixer_out", KD, L)
        u2 = sb("normed", KD, L)
        sq = sb("squares", 2, L)
        sq_sum = sb("sq_sum", L)
        tile_left, sq_made, sq_added = (sem(n) for n in ("tile_left", "sq_made", "sq_added"))
        n_summed, n_rooted, n_inverted, n_used = (sem(n) for n in ("n_summed", "n_rooted", "n_inverted", "n_used"))
        h_added = sem("h_added")

        class Seen:
            def __init__(self):
                self.left = self.squares = self.added = self.norms = self.h = 0

        seen = {who: Seen() for who in ("pe", "act", "dve")}

        def tokens(ap, width):
            return ap if width == L else ap[:, META:]

        def tile_ps(t, width):
            return wide[t][:, :, 0:HALF] if width == L else wide[t][:, 0, 0:width]

        def over_tiles(eng, count, per_turn, body):
            with eng.Fori(0, count // per_turn) as j:
                for t in range(per_turn):
                    body(j, t, per_turn * j + t)

        def pe_tiles(pe, load, count, kt, rhs, width, loop=True, after=None):
            st, per = seen["pe"], kt // KD
            turn = SLOTS // per

            def tile(j, t, n):
                pe.wait_ge(tile_left, st.left + n + 1)
                for k in range(kt):
                    if k % KD == 0:
                        ring.wait_full(pe, load + per * t + k // KD, j)
                for b in range(2 if width == L else 1):
                    for k in range(kt):
                        at = load + per * t + k // KD
                        mm = pe.matmul(wide[t][:, b, 0:HALF if width == L else width],
                                       ring.slot(at)[:, k % KD * P:(k % KD + 1) * P], rhs(k, b), start=k == 0, stop=k == kt - 1)
                        if k % KD == KD - 1 and b == (1 if width == L else 0):
                            mm.then_inc(ring.done(at), 1)
                if after:
                    after(n, t)

            if loop:
                over_tiles(pe, count, turn, tile)
            else:
                for n in range(count):
                    tile(n // turn, n % turn, n)
            st.left += count + turn

        def act_tiles(act, load, count, kt, take, loop=True, before=None):
            st, per = seen["act"], kt // KD
            turn = SLOTS // per
            act.drain().then_inc(tile_left, turn)

            def tile(j, t, n):
                if before:
                    before(n, t)
                ring.wait_used(act, load + per * t + per - 1, j)
                take(j, t, n)

            if loop:
                over_tiles(act, count, turn, tile)
            else:
                for n in range(count):
                    tile(n // turn, n % turn, n)
            st.left += count + turn

        def act_square(act, src, slot, n, width):
            st = seen["act"]
            act.wait_ge(sq_added, st.added + n + 1)
            return act.activation(halves(sq[:, slot, 0:width], width) if len(src.shape) == 3 else sq[:, slot, 0:width], src, ACT.Square).then_inc(sq_made, 1)

        def act_root(act, tiles, width):
            st = seen["act"]
            st.norms += 1
            st.squares += tiles
            st.added += tiles + 2
            act.wait_ge(n_summed, st.norms)
            if st.norms > 1:
                act.wait_ge(n_used, st.norms - 1)
            act.activation(halves(inv_rms[:, 0:width], width), tile_ps(3, width), ACT.Sqrt,
                           bias=epsilon[:, 0:1], scale=1.0 / (tiles * P)).then_inc(n_rooted, 1)

        def pe_norm_sum(pe, tiles, width):
            st = seen["pe"]
            st.norms += 1
            st.added += tiles + 2
            pe.wait_ge(sq_added, st.added)
            if st.norms > 1:
                pe.wait_ge(n_rooted, st.norms - 1)
            for b in range(2 if width == L else 1):
                n = HALF if width == L else width
                mm = pe.matmul(wide[3][:, b, 0:n], ones, sq_sum[:, b * n:(b + 1) * n], start=True, stop=True)
            mm.then_inc(n_summed, 1)

        def dve_sum_start(dve, width):
            st = seen["dve"]
            if st.norms:
                dve.wait_ge(n_summed, st.norms)
            dve.memset(sq_sum[:, 0:width], 0.0).then_inc(sq_added, 2)

        def dve_sum(dve, slot, n, width):
            st = seen["dve"]
            dve.wait_ge(sq_made, st.squares + n + 1)
            dve.wait_ge(sq_added, st.added + n + 2)
            dve.tensor_tensor(sq_sum[:, 0:width], sq_sum[:, 0:width], sq[:, slot, 0:width], ALU.add).then_inc(sq_added, 1)

        def dve_invert(dve, tiles, width):
            st = seen["dve"]
            st.norms += 1
            st.squares += tiles
            st.added += tiles + 2
            dve.wait_ge(n_rooted, st.norms)
            dve.reciprocal(inv_rms[:, 0:width], inv_rms[:, 0:width]).then_inc(n_inverted, 1)
            dve.wait_ge(n_inverted, st.norms)

        def dve_apply(dve, tiles, width, src, dst, gain):
            for k in range(tiles):
                ins = dve.scalar_tensor_tensor(dst(k), src(k), pcol(gain, k), inv_rms[:, 0:width], ALU.mult, ALU.mult)
            ins.then_inc(n_used, 1)

        def h_of(k, width):
            return tokens(h[:, k, :], width)

        def pe_project_out(pe, load, kt, src, width, post):
            pe_tiles(pe, load, KD, kt, src, width)
            if post:
                pe_norm_sum(pe, KD, width)
            pe_norm_sum(pe, KD, width if not post else post)

        def act_project_out(act, load, kt, width, post):
            st = seen["act"]
            turn = SLOTS * KD // kt

            def take(j, t, n):
                dst = m_t[:].rearrange("p k n -> p (k n)")[:, bass.ds(n * L, width)]
                if post:
                    act_square(act, tile_ps(t, width), t % 2, n, width)
                    act.activation(halves(dst, width), tile_ps(t, width), ACT.Copy).then_inc(tile_left, 1)
                else:
                    act.activation(dst, tile_ps(t, width), ACT.Copy).then_inc(tile_left, 1)
                    act.wait_ge(h_added, st.h + n + 1)
                    act_square(act, h[:].rearrange("p k n -> p (k n)")[:, bass.ds(n * L + META, width)], t % 2, n, width)
            act_tiles(act, load, KD, kt, take)
            if post:
                act_root(act, KD, width)
                for k in range(KD):
                    act.wait_ge(h_added, st.h + 2 * k + 2)
                    act_square(act, h_of(k, post), k % 2, k, post)
                st.h += KD
            st.h += KD
            act_root(act, KD, post if post else width)

        def dve_project_out(dve, kt, width, post, post_gain, gain, dst):
            st = seen["dve"]
            turn = SLOTS * KD // kt
            dve_sum_start(dve, width)

            def take(j, t, n):
                if not post:
                    dve.wait_ge(tile_left, st.left + turn + n + 1)
                    hn = h[:].rearrange("p k n -> p (k n)")[:, bass.ds(n * L + META, width)]
                    mn = m_t[:].rearrange("p k n -> p (k n)")[:, bass.ds(n * L, width)]
                    dve.tensor_tensor(hn, hn, mn, ALU.add).then_inc(h_added, 1)
                dve_sum(dve, t % 2, n, width)
            over_tiles(dve, KD, turn, take)
            st.left += KD + turn
            if post:
                dve_invert(dve, KD, width)
                dve_sum_start(dve, post)
                for k in range(KD):
                    dve.scalar_tensor_tensor(m_t[:, k, :], m_t[:, k, :], pcol(post_gain, k), inv_rms[:], ALU.mult, ALU.mult).then_inc(h_added, 1)
                    dve.wait_ge(h_added, st.h + 2 * k + 1)
                    ins = dve.tensor_tensor(h[:, k, :], h[:, k, :], m_t[:, k, :], ALU.add).then_inc(h_added, 1)
                    if k:
                        dve_sum(dve, (k - 1) % 2, k - 1, post)
                dve.drain().then_inc(n_used, 1)
                dve_sum(dve, (KD - 1) % 2, KD - 1, post)
                st.h += KD
            st.h += KD
            last = post if post else width
            dve_invert(dve, KD, last)
            dve_apply(dve, KD, last, lambda k: h_of(k, last), dst, gain)

        M = ExitStack()

        def sm(name, *shape):
            return M.enter_context(nc.sbuf_tensor(name, [P, *shape], F32))

        z_t = sm("gated", KI, L)
        latents = sm("latents", Q_TILES + KV_TILES, L)
        k_rope = sm("k_rope", L)
        Q_EDGES = [0] + list(range(META, L + 1, P))
        Q_BLOCKS = len(Q_EDGES) - 1
        v_rows = sm("v_rows", Q_BLOCKS, DI)
        m_con = sm("mla_tables", CON_OF["mla"][1])
        P_AT = [sum(Q_EDGES[1:t + 1]) for t in range(Q_BLOCKS + 1)]
        probs = sm("probs", P_AT[-1])
        probs_t = sm("probs_turned", Q_BLOCKS, L)
        v_now = sm("v_now", 2, Q_BLOCKS, P)
        row_max, row_bias, row_sum = (sm(n, Q_BLOCKS) for n in ("row_max", "row_bias", "row_sum"))
        M.close()
        tanh_gate = [m_t[:, t, :] for t in range(SLOTS)]
        k_rope_raw, rope_cos = m_t[:, SLOTS, :], m_t[:, SLOTS + 1, :]
        q_nope, k_nope, q_rope, q_rope_raw = (u2[:, k, :] for k in range(4))

        def mcon(name, width):
            at = CON[name] - CON_OF["mla"][0]
            return m_con[:, at:at + width]

        mixed_loaded, h_loaded = sem("mixed_loaded"), sem("h_loaded")
        d = {n: sem("d_" + n) for n in ("gated", "rope_mm", "rope", "v_mm", "v_copied", "stats_set")}

        def sp_c(sp):
            sp.wait_ge(q["z_stored"], 16 * PAIRS)
            sp.wait_ge(phase_done, 8)
            for i in range(PAIRS):
                sp.dma_start(z_t[:, i, :], mixed[i]).then_inc(mixed_loaded, 16)
            sp.dma_start(h[:], x_in).then_inc(h_loaded, 16)
            first, n = CON_OF["mla"]
            sp.dma_start(m_con[:], con_in[:, first:first + n]).then_inc(con_loaded, 16)

        def half_of(ap):
            return lambda k, b: ap[:, k, b * HALF:(b + 1) * HALF]

        MLA_IN = FIRST["mla_in"]
        MLA_GATE = MLA_IN + Q_TILES + KV_TILES + 1

        def pe_mla_in(pe):
            st = seen["pe"]
            pe.wait_ge(n_used, st.norms)
            pe_tiles(pe, MLA_IN, Q_TILES, KD, half_of(u2), L, loop=False)
            pe.wait_ge(tile_left, st.left)
            pe_norm_sum(pe, Q_TILES, L)
            pe_tiles(pe, MLA_IN + Q_TILES, KV_TILES + 1, KD, half_of(u2), L, loop=False)
            pe.wait_ge(con_loaded, 64)
            pe.wait_ge(tile_left, st.left)
            for b in range(2):
                mm = pe.matmul(wide[2][:, b, 0:HALF], mcon("rot_mla", P), k_rope_raw[:, b * HALF:(b + 1) * HALF], start=True, stop=True)
            mm.then_inc(d["rope_mm"], 1)
            pe_norm_sum(pe, KV_TILES, L)
            pe.wait_ge(d["rope"], 2)
            pe_tiles(pe, MLA_GATE, KI, KD, half_of(u2), L)
            pe.wait_ge(tile_left, st.left)
            pe.wait_ge(n_used, st.norms)
            n = 0
            for c in range(4):
                load = FIRST["mla_v"] + c
                ring.wait_full(pe, load)
                for t in range(Q_BLOCKS):
                    rows = Q_EDGES[t + 1] - Q_EDGES[t]
                    if n >= 8:
                        pe.wait_ge(d["v_copied"], n - 7)
                    for k in range(KV_TILES):
                        mm = pe.matmul(wide[n // 2 % 4][0:rows, n % 2, :], latents[:, Q_TILES + k, Q_EDGES[t]:Q_EDGES[t + 1]],
                                       ring.slot(load)[:, k * 512:(k + 1) * 512], start=k == 0, stop=k == KV_TILES - 1)
                    mm.then_inc(d["v_mm"], 1)
                    n += 1
                pe.drain().then_inc(ring.done(load), 1)

        def act_mla_in(act):
            st = seen["act"]
            flat = z_t[:].rearrange("p k n -> p (k n)")

            def latent(first):
                def take(j, t, n):
                    if first + n < Q_TILES + KV_TILES:
                        act_square(act, tile_ps(t, L), n % 2, n, L)
                        dst = latents[:, first + n, :]
                    else:
                        dst = k_rope_raw
                    act.activation(halves(dst, L), tile_ps(t, L), ACT.Copy).then_inc(tile_left, 1)
                return take
            act_tiles(act, MLA_IN, Q_TILES, KD, latent(0), loop=False)
            act_root(act, Q_TILES, L)
            act_tiles(act, MLA_IN + Q_TILES, KV_TILES + 1, KD, latent(Q_TILES), loop=False)
            act_root(act, KV_TILES, L)

            def gate(j, t, n):
                act.wait_ge(d["gated"], n + 1)
                act.activation(halves(tanh_gate[t], L), tile_ps(t, L), ACT.Tanh, scale=0.5)
                act.activation(halves(flat[:, bass.ds(n * L, L)], L), tile_ps(t, L), ACT.Copy).then_inc(tile_left, 1)
            act_tiles(act, MLA_GATE, KI, KD, gate)
            n = 0
            for c in range(4):
                for t in range(Q_BLOCKS):
                    rows = Q_EDGES[t + 1] - Q_EDGES[t]
                    act.wait_ge(d["v_mm"], n + 1)
                    act.activation(v_rows[0:rows, t, c * 512:(c + 1) * 512], wide[n // 2 % 4][0:rows, n % 2, :], ACT.Copy).then_inc(d["v_copied"], 1)
                    n += 1

        def dve_mla_in(dve):
            st = seen["dve"]
            flat = z_t[:].rearrange("p k n -> p (k n)")
            for t in (row_max, row_bias, row_sum):
                dve.memset(t[:], 1.0).then_inc(d["stats_set"], 1)
            dve_sum_start(dve, L)
            for n in range(Q_TILES):
                dve_sum(dve, n % 2, n, L)
            dve_invert(dve, Q_TILES, L)
            dve_sum_start(dve, L)
            st.left += Q_TILES + SLOTS
            dve.wait_ge(tile_left, st.left)
            dve_apply(dve, Q_TILES, L, lambda k: latents[:, k, :], lambda k: latents[:, k, :], "q_norm")
            for n in range(KV_TILES):
                dve_sum(dve, n % 2, n, L)
            st.left += KV_TILES + 1 + SLOTS
            dve.wait_ge(con_loaded, 64)
            dve.wait_ge(tile_left, st.left)
            dve.tensor_tensor(k_rope[:], k_rope_raw, mcon("cos_mla", L), ALU.mult).then_inc(d["rope"], 1)
            dve.wait_ge(d["rope_mm"], 1)
            dve.tensor_tensor(halves(rope_cos, L), wide[2][:, :, 0:HALF], halves(mcon("sin_mla", L), L), ALU.mult).then_inc(d["rope"], 1)
            dve.wait_ge(d["rope"], 2)
            dve.tensor_tensor(k_rope[:], k_rope[:], rope_cos, ALU.add).then_inc(d["rope"], 1)
            dve_invert(dve, KV_TILES, L)
            dve_apply(dve, KV_TILES, L, lambda k: latents[:, Q_TILES + k, :], lambda k: latents[:, Q_TILES + k, :], "kv_norm")
            dve.drain().then_inc(d["gated"], SLOTS)

            def gate(j, t, n):
                dve.wait_ge(tile_left, st.left + SLOTS + n + 1)
                at = flat[:, bass.ds(n * L, L)]
                dve.scalar_tensor_tensor(at, tanh_gate[t], 1.0, at, ALU.add, ALU.mult).then_inc(d["gated"], 1)
            over_tiles(dve, KI, SLOTS, gate)
            st.left += KI + SLOTS

        MLA_SCALE = (P + KROPE) ** -0.5
        UP = FIRST["mla_up"]
        PER_TURN = 4
        e = {n: sem("e_" + n) for n in ("made", "evac", "rope", "scores", "dve", "exp", "turned", "pt", "pv", "v_now", "gated")}
        DVE_E = Count(e["dve"], 19)
        SCORE_OF = [wide[0][:, 0, P_AT[t]:P_AT[t + 1]] for t in range(3)] + [wide[0][:, 1, 0:Q_EDGES[4]], wide[1][:, :, 0:HALF]]
        TURNED = [(0, 0, 4, 0, 0, 0), (0, 4, 5, 0, 1, 1), (2, 2, 5, P, 1, 1), (1, 1, 5, 0, 0, 2), (3, 3, 5, 0, 1, 3), (4, 4, 5, 2 * P, 1, 3)]

        def size(t):
            return Q_EDGES[t + 1] - Q_EDGES[t]

        def p_of(t, lo=0, hi=L):
            return probs[0:size(t), P_AT[t] + lo:P_AT[t] + min(hi, Q_EDGES[t + 1])]

        def of_pair(x):
            return UP + 2 * (x // 2), UP + 2 * (x // 2) + 1

        def head_weights(x):
            q_load, k_load = of_pair(x)
            o = x % 2
            return (ring.slot(q_load)[:, o * 512:(o + 1) * 512], ring.slot(k_load)[:, 512 + o * 256:512 + (o + 1) * 256],
                    ring.slot(k_load)[:, 0:512])

        def pe_up(pe, H, x, j, first=False):
            st = seen["pe"]
            wq, wk, wr = head_weights(x)
            q_load, k_load = of_pair(x)

            def product(dst, w, k0, kt):
                for b in range(2):
                    for k in range(kt):
                        mm = pe.matmul(dst[:, b, 0:HALF], w[:, k * P:(k + 1) * P], latents[:, k0 + k, b * HALF:(b + 1) * HALF],
                                       start=k == 0, stop=k == kt - 1)
                return mm

            if not first:
                pe.wait_ge(e["pt"], 6 * H)
            pair = (PER_TURN * j + x) // 2 if isinstance(j, int) else PER_TURN // 2 * j + x // 2
            if x % 2 == 0:
                ring.wait_full(pe, k_load, j)
                product(wide[2], wr, 0, Q_TILES).then_inc(e["made"], 1)
            if not first:
                pe.wait_ge(e["gated"], 2 * H)
            mm = product(wide[3], wk, Q_TILES, KV_TILES)
            mm.then_inc(e["made"] if x % 2 == 0 else ring.done(k_load), 1)
            if x % 2 == 0:
                ring.wait_full(pe, q_load, j)
                pe.wait_ge(e["evac"], 5 * pair + 1)
            mm = product(wide[2], wq, 0, Q_TILES)
            mm.then_inc(e["made"] if x % 2 == 0 else ring.done(q_load), 1)
            if x % 2 == 0:
                pe.wait_ge(e["evac"], 5 * pair + 2)
                for b in range(2):
                    mm = pe.matmul(wide[3][:, b, 0:HALF], mcon("rot_mla", P), q_rope_raw[:, b * HALF:(b + 1) * HALF], start=True, stop=True)
                mm.then_inc(e["made"], 1)

        def act_up(act, x, j, what):
            q_load, k_load = of_pair(x)
            pair = (PER_TURN * j + x) // 2 if isinstance(j, int) else PER_TURN // 2 * j + x // 2
            if x % 2 == 0:
                act.wait_ge(e["made"], 4 * pair + 1 + what)
            else:
                ring.wait_used(act, k_load if what == 1 else q_load, j)
            dst, src = ((q_rope_raw, wide[2]), (k_nope, wide[3]), (q_nope, wide[2]))[what]
            act.activation(halves(dst, L), src[:, :, 0:HALF], ACT.Copy).then_inc(e["evac"], 1)

        def dve_rope(dve, j, x):
            pair = (PER_TURN * j + x) // 2 if isinstance(j, int) else PER_TURN // 2 * j + x // 2
            dve.wait_ge(e["evac"], 5 * pair + 1)
            dve.tensor_tensor(q_rope, q_rope_raw, mcon("cos_mla", L), ALU.mult).then_inc(e["rope"], 1)
            dve.wait_ge(e["made"], 4 * pair + 4)
            dve.tensor_tensor(halves(rope_cos, L), wide[3][:, :, 0:HALF], halves(mcon("sin_mla", L), L), ALU.mult).then_inc(e["rope"], 1)
            dve.wait_ge(e["rope"], 3 * pair + 2)
            dve.tensor_tensor(q_rope, q_rope, rope_cos, ALU.add).then_inc(e["rope"], 1)

        def pe_head(pe, j, x, last):
            H = PER_TURN * j + x
            ends = last and x == PER_TURN - 1
            pair = (PER_TURN * j + x) // 2 if isinstance(j, int) else PER_TURN // 2 * j + x // 2
            pe.wait_ge(e["evac"], 5 * pair + (3 if x % 2 == 0 else 5))
            pe.wait_ge(e["rope"], 3 * pair + 3)
            rows = HEAD_ROWS[x % 2]
            for t in (4, 3, 0, 1, 2):
                lo, hi = Q_EDGES[t], Q_EDGES[t + 1]
                for b in range(2 if t == 4 else 1):
                    keys = slice(b * HALF, (b + 1) * HALF) if t == 4 else slice(0, hi)
                    dst = SCORE_OF[t][0:size(t), b, :] if t == 4 else SCORE_OF[t][0:size(t)]
                    pe.matmul(dst, q_nope[:, lo:hi], k_nope[:, keys], start=True, stop=False)
                    mm = pe.matmul(dst, q_rope[rows, lo:hi], k_rope[rows, keys], start=False, stop=True)
                if t in (4, 3, 2):
                    mm.then_inc(e["scores"], 1)
            if not ends:
                pe_up(pe, H + 1, (x + 1) % PER_TURN, j + (x + 1) // PER_TURN)
                pair_next = pair + (x % 2)
                pe.wait_ge(e["evac"], 5 * pair_next + (3 if x % 2 else 5))
            else:
                pe.wait_ge(e["pt"], 6 * H + 6)
            for n, (kb, q0, q1, col, bank, piece) in enumerate(TURNED):
                if n == 0:
                    pe.wait_ge(DVE_E.sem, DVE_E.at(H, 19))
                if n == 3:
                    pe.wait_ge(e["pt"], 6 * H + 7)
                if n == 4:
                    pe.wait_ge(e["pt"], 6 * H + 9)
                for t in reversed(range(q0, q1)):
                    at = col + Q_EDGES[t] - Q_EDGES[q0]
                    mm = pe.transpose(wide[2][0:size(kb), bank, at:at + size(t)], p_of(t, Q_EDGES[kb], Q_EDGES[kb + 1]), ident[0:size(t), 0:size(t)])
                if n in (0, 2, 3, 5):
                    mm.then_inc(e["turned"], 1)
            pe.wait_ge(e["v_now"], 2 * H + 2)
            if not ends:
                if x % 2:
                    pe.wait_ge(e["rope"], 3 * pair_next + 2)
            else:
                pe.wait_ge(e["gated"], 2 * H + 2)
            cut = Q_EDGES[3]
            for kb, done in ((0, 2), (2, 3), (1, 4), (3, 5), (4, 6)):
                pe.wait_ge(e["pt"], 6 * H + 6 + done)
                for b, (lo, hi) in enumerate(((0, cut), (cut, L))):
                    seen_from = max(lo, Q_EDGES[kb])
                    if seen_from < hi:
                        mm = pe.matmul(wide[3][:, b, seen_from - lo:hi - lo], v_now[0:size(kb), x % 2, kb, :],
                                       probs_t[0:size(kb), kb, seen_from:hi], start=kb == 0, stop=kb == (1, 4)[b])
            mm.then_inc(e["pv"], 1)

        def act_head(act, j, x, last):
            H = PER_TURN * j + x
            ends = last and x == PER_TURN - 1
            nx, nj = (x + 1) % PER_TURN, j + (x + 1) // PER_TURN

            def soften(t, step):
                act.wait_ge(DVE_E.sem, DVE_E.at(H, step))
                act.activation(halves(p_of(t), L) if t == 4 else p_of(t), SCORE_OF[t][0:size(t)], ACT.Exp, bias=row_bias[0:size(t), t:t + 1],
                               scale=MLA_SCALE, accum_out=row_sum[0:size(t), t:t + 1]).then_inc(e["exp"], 1)

            soften(4, 5)
            soften(3, 5)
            if not ends and nx % 2 == 0:
                act_up(act, nx, nj, 0)
            for t in (2, 1, 0):
                soften(t, 12)
            if not ends:
                act_up(act, nx, nj, 1)
                act_up(act, nx, nj, 2)
            for n, (kb, q0, q1, col, bank, piece) in enumerate(TURNED):
                act.wait_ge(e["turned"], 4 * H + piece + 1)
                if n == 0:
                    act.wait_ge(e["pv"], H + 1)
                lo, hi = Q_EDGES[q0], Q_EDGES[q1]
                act.activation(probs_t[0:size(kb), kb, lo:hi], wide[2][0:size(kb), bank, col:col + hi - lo], ACT.Copy).then_inc(e["pt"], 1)

        def dve_head(dve, j, x, last):
            H = PER_TURN * j + x
            ends = last and x == PER_TURN - 1

            def step(ins):
                ins.then_inc(DVE_E.sem, 1)

            def after(k):
                dve.wait_ge(DVE_E.sem, DVE_E.at(H, k))

            def maxima(t, k):
                n = size(t)
                diag = SCORE_OF[t][:, 1, HALF - n:HALF] if t == 4 else SCORE_OF[t][0:n, Q_EDGES[t]:Q_EDGES[t + 1]]
                step(dve.tensor_tensor(diag, diag, mcon("causal", P)[0:n, 0:n], ALU.add))
                after(k)
                step(dve.tensor_reduce(row_max[0:n, t:t + 1], SCORE_OF[t][0:n], mybir.AxisListType.XY if t == 4 else AX_X, ALU.max))

            def bias(ts):
                step(dve.tensor_scalar(row_bias[:, ts], row_max[:, ts], -MLA_SCALE, None, ALU.mult))

            def share(t):
                n = size(t)
                step(dve.tensor_scalar(p_of(t), p_of(t), row_sum[0:n, t:t + 1], None, ALU.mult))

            dve.wait_ge(e["scores"], 3 * H + 1)
            maxima(4, 1)
            dve.wait_ge(e["scores"], 3 * H + 2)
            maxima(3, 3)
            after(4)
            bias(slice(3, 5))
            dve.wait_ge(e["scores"], 3 * H + 3)
            maxima(2, 6)
            maxima(1, 8)
            maxima(0, 10)
            after(11)
            bias(slice(0, 3))
            dve.wait_ge(e["exp"], Q_BLOCKS * H + 2)
            step(dve.reciprocal(row_sum[:, 3:5], row_sum[:, 3:5]))
            after(13)
            share(4)
            share(3)
            dve.wait_ge(e["exp"], Q_BLOCKS * H + 5)
            step(dve.reciprocal(row_sum[:, 0:3], row_sum[:, 0:3]))
            after(16)
            share(2)
            share(1)
            share(0)
            if not ends and x % 2:
                dve_rope(dve, j + (x + 1) // PER_TURN, (x + 1) % PER_TURN)
            dve.wait_ge(e["pv"], H + 2)
            flat = z_t[:].rearrange("p k n -> p (k n)")
            cut = Q_EDGES[3]
            for b, (lo, hi) in enumerate(((0, cut), (cut, L))):
                at = flat[:, bass.ds(H * L + lo, hi - lo)]
                dve.scalar_tensor_tensor(at, wide[3][:, b, 0:hi - lo], 0.5, at, ALU.mult, ALU.mult).then_inc(e["gated"], 1)

        def pool_v(pool, H, slot):
            flat = v_rows[:].rearrange("p t n -> p (t n)")
            pool.tensor_copy(v_now[0:META, slot, 0, :], flat[0:META, bass.ds(H * P, P)]).then_inc(e["v_now"], 1)
            src = v_rows[:, 1:Q_BLOCKS, bass.ds(H * P, P)]
            pool.tensor_copy(v_now[:, slot, 1:Q_BLOCKS, :], src).then_inc(e["v_now"], 1)

        def pool_head(pool, j, x, last):
            H = PER_TURN * j + x
            if last and x >= 2:
                return
            pool.wait_ge(e["pv"], H + 2)
            pool_v(pool, H + 2, x % 2)

        def over_heads(eng, body):
            with eng.Fori(0, HEADS // PER_TURN - 1) as j:
                for x in range(PER_TURN):
                    body(eng, j, x, False)
            for x in range(PER_TURN):
                body(eng, HEADS // PER_TURN - 1, x, True)

        def pe_mla(pe):
            st = seen["pe"]
            pe.wait_ge(d["v_copied"], 4 * Q_BLOCKS)
            pe.drain().then_inc(e["pv"], 1)
            pe_up(pe, 0, 0, 0, first=True)
            over_heads(pe, pe_head)

        def act_mla(act):
            act.drain().then_inc(e["pt"], 6)
            for what in range(3):
                act_up(act, 0, 0, what)
            over_heads(act, act_head)

        def dve_mla(dve):
            dve.drain().then_inc(e["gated"], 2)
            dve_rope(dve, 0, 0)
            dve.wait_ge(d["stats_set"], 3)
            over_heads(dve, dve_head)

        def pool_mla(pool):
            pool.wait_ge(d["v_copied"], 4 * Q_BLOCKS)
            pool_v(pool, 0, 0)
            pool_v(pool, 1, 1)
            over_heads(pool, pool_head)

        def sp_stream(sp, first, end):
            turns = (end - first) // SLOTS
            with sp.Fori(0, turns) as j:
                for n in range(SLOTS):
                    ring.load(sp, stream, first + n, j)
            for n in range(first + turns * SLOTS, end):
                ring.load(sp, stream, n)


        G = ExitStack()

        def sg(name, *shape):
            return G.enter_context(nc.sbuf_tensor(name, [P, *shape], F32))

        g_con = sb("second_tables", CON_OF["odd"][1])
        dft = sg("dft", 2, SEQ // P, SEQ)
        parts = sg("even_parts", 24, SEQ)
        padded = sg("a_c_a_x", 4, SEQ + 2)
        conv = sg("conv", 4, SEQ)
        tanh_z = sg("tanh_z", 4, SEQ)
        spectrum = sg("spectrum", 4, E_G, 2 * E_DIM)
        G.close()
        B_U, A_C, A_X, A_B, A_Z, B_Z = range(0, 24, 4)
        g = {n: sem("g_" + n) for n in ("tanh", "steps", "padded", "part_mm", "part_copied", "dft_mm", "y")}

        def gcon(name, width):
            at = CON[name] - CON_OF["odd"][0]
            return g_con[:, at:at + width]

        def sp_g(sp):
            sp.wait_ge(phase_done, 12)
            first, n = CON_OF["odd"]
            sp.dma_start(g_con[:], con_in[:, first:first + n]).then_inc(con_loaded, 16)
            sp.dma_start(dft[:], dft_in).then_inc(con_loaded, 16)

        def whole(ap):
            return lambda k, b: ap[:, k, 0:SEQ]

        EVEN_FIRST = 16

        def pe_even(pe):
            st = seen["pe"]
            pe_tiles(pe, FIRST["even_in"], EVEN_FIRST, KD, whole(u2), SEQ)
            pe_tiles(pe, FIRST["even_in"] + EVEN_FIRST, 24 - EVEN_FIRST, KD, whole(u2), SEQ)
            pe.wait_ge(con_loaded, 96)
            for n in range(8):
                pair, t = n // 4, n % 4
                if n % 2 == 0:
                    pe.wait_ge(tile_left, st.left - (3 - n // 2 if n < 6 else 0))
                for o in range(2):
                    mm = pe.matmul(wide[n // 2][:, n % 2, o * 256:(o + 1) * 256], parts[:, B_U + 2 * pair + o, t * P:(t + 1) * P],
                                   gcon("dft_d", 2 * E_DIM), start=True, stop=True)
                mm.then_inc(g["part_mm"], 1)
            for grp_ in range(E_G):
                pe.wait_ge(g["part_copied"], 4 + grp_ // 2 * 4)
                for t in range(4):
                    for o in range(2):
                        mm = pe.matmul(wide[grp_][:, 0, :], spectrum[:, t, grp_, o * E_DIM:(o + 1) * E_DIM], dft[:, o, t, :],
                                       start=t + o == 0, stop=t + o == 4)
                mm.then_inc(g["dft_mm"], 1)
            pe.wait_ge(g["y"], 8)

            def y(k, b):
                return parts[:, A_B + k if k < 4 else B_Z + k - 4, :]
            pe_project_out(pe, FIRST["even_out"], KD, y, SEQ, None)

        def act_even(act):
            st = seen["act"]
            flat = parts[:].rearrange("p k n -> p (k n)")

            def keep(j, t, n):
                act.activation(flat[:, bass.ds(n * SEQ, SEQ)], tile_ps(t, SEQ), ACT.Copy).then_inc(tile_left, 1)

            def gate(j, t, n):
                act.wait_ge(g["tanh"], n + 1)
                act.activation(tanh_z[:, t, :], tile_ps(t, SEQ), ACT.Tanh, scale=0.5)
                act.activation(flat[:, bass.ds((n + EVEN_FIRST) * SEQ, SEQ)], tile_ps(t, SEQ), ACT.Copy).then_inc(tile_left, 1)
            act_tiles(act, FIRST["even_in"], EVEN_FIRST, KD, keep)
            act_tiles(act, FIRST["even_in"] + EVEN_FIRST, 24 - EVEN_FIRST, KD, gate)
            for n in range(8):
                pair, t = n // 4, n % 4
                act.wait_ge(g["part_mm"], n + 1)
                act.activation(spectrum[:, t, 2 * pair:2 * pair + 2, :], wide[n // 2][:, n % 2, :].rearrange("p (g n) -> p g n", g=2),
                               ACT.Copy).then_inc(g["part_copied"], 1)
            act_project_out(act, FIRST["even_out"], KD, SEQ, None)

        def dve_even(dve):
            st = seen["dve"]
            dve.memset(padded[:, :, 0:1], 0.0).then_inc(g["padded"], 1)
            dve.memset(padded[:, :, SEQ + 1:SEQ + 2], 0.0).then_inc(g["padded"], 1)
            dve.drain().then_inc(g["tanh"], 4)
            steps = [0]

            def step(ins):
                ins.then_inc(g["steps"], 1)
                steps[0] += 1

            def after():
                dve.wait_ge(g["steps"], steps[0])

            def tiles(n):
                dve.wait_ge(tile_left, st.left + SLOTS + n)
            tiles(A_X + 4)
            step(dve.tensor_tensor(padded[:, :, 1:SEQ + 1], parts[:, A_C:A_C + 4, :], parts[:, A_X:A_X + 4, :], ALU.mult))
            dve.wait_ge(g["padded"], 2)
            after()
            for tap in range(3):
                for t in range(4):
                    w = pcol("conv", tap * 4 + t)
                    src = padded[:, t, tap:tap + SEQ]
                    if tap == 0:
                        step(dve.tensor_scalar(conv[:, t, :], src, w, None, ALU.mult))
                    else:
                        step(dve.scalar_tensor_tensor(conv[:, t, :], src, w, conv[:, t, :], ALU.mult, ALU.add))
                after()
            tiles(A_B + 4)
            step(dve.tensor_tensor(parts[:, A_B:A_B + 4, :], parts[:, A_B:A_B + 4, :], conv[:], ALU.mult))
            after()
            st.left += EVEN_FIRST + SLOTS
            for n in range(8):
                tiles(n + 1)
                z = parts[:, A_Z + n, :]
                step(dve.scalar_tensor_tensor(z, tanh_z[:, n % 4, :], 1.0, z, ALU.add, ALU.mult))
                dve.drain().then_inc(g["tanh"], 1)
                if n < 4:
                    after()
                    y = parts[:, A_B + n, :]
                    dve.scalar_tensor_tensor(y, y, 0.5, z, ALU.mult, ALU.mult).then_inc(g["y"], 1)
            st.left += 24 - EVEN_FIRST + SLOTS
            after()
            for n in range(E_G):
                dve.wait_ge(g["dft_mm"], n + 1)
                z = parts[:, B_Z + n, :]
                dve.scalar_tensor_tensor(z, wide[n][:, 0, :], 0.5, z, ALU.mult, ALU.mult).then_inc(g["y"], 1)
            dve_project_out(dve, KD, SEQ, None, None, "odd", lambda k: u2[:, k, 0:SEQ])

        HH = ExitStack()

        def sh(name, *shape):
            return HH.enter_context(nc.sbuf_tensor(name, [P, *shape], F32))

        NQK = G_HEADS + G_KV
        qk = sh("q_k", NQK, SEQ)
        z_odd = sh("z_odd", G_HEADS, SEQ)
        with_gain, qk_sq, qk_root = sh("with_gain", 2, SEQ), sh("qk_squares", 2, SEQ), sh("qk_root", 2, SEQ)
        rot_sin = sh("rot_sin", SEQ)
        v_odd = sh("v_odd", 4, G_KV * P)
        q_now = sh("q_now", 2, SEQ)
        o_probs, o_probs_t = sh("odd_probs", 2, SEQ), sh("odd_probs_t", 2, SEQ)
        o_max, o_bias, o_sum = (sh("odd_" + n, 8) for n in ("max", "bias", "sum"))
        tanh_odd = sh("tanh_odd", 2, SEQ)
        HH.close()
        o = {n: sem("o_" + n) for n in ("sq", "sum", "rot", "root", "dve", "v_mm", "v_copied", "q_now", "scores", "turned", "pt", "pv",
                                        "exp", "bias", "share", "tanh", "z", "gated")}
        ODD_Z, ODD_K, ODD_V = FIRST["odd_in"] + G_HEADS, FIRST["odd_in"] + 2 * G_HEADS, FIRST["odd_v"]
        ODD_SCALE = P ** -0.5
        DVE_O = Count(o["dve"], 6)
        qk_flat = qk[:].rearrange("p k n -> p (k n)")
        z_flat = z_odd[:].rearrange("p k n -> p (k n)")

        def qk_of(n):
            return qk_flat[:, bass.ds(n * SEQ, SEQ)]

        def pe_qk(pe, n, t):
            pe.wait_ge(o["sq"], n + 1)
            pe.wait_ge(o["root"], n + 1)
            pe.matmul(wide[t % 2][:, 1, :], ones, qk_sq[:, t % 2, :], start=True, stop=True).then_inc(o["sum"], 1)
            pe.wait_ge(o["dve"], 6 * n + 12 + 1)
            pe.matmul(wide[2 + t % 2][:, 1, :], gcon("rot_odd", P), with_gain[:, t % 2, :], start=True, stop=True).then_inc(o["rot"], 1)

        def act_qk(act, n, t):
            act.wait_ge(o["sum"], n + 1)
            act.activation(qk_sq[:, t % 2, :], qk_of(n), ACT.Square).then_inc(o["sq"], 1)
            act.wait_ge(o["sum"], n + 3)
            act.wait_ge(o["dve"], 6 * n + 6)
            act.activation(qk_root[:, t % 2, :], wide[t % 2][:, 1, :], ACT.Sqrt, bias=epsilon[:, 0:1], scale=1.0 / P).then_inc(o["root"], 1)

        def dve_qk(dve, n, t, gain):
            def step(ins):
                ins.then_inc(o["dve"], 1)

            def after(k):
                dve.wait_ge(o["dve"], 6 * n + 12 + k)
            x, y = with_gain[:, t % 2, :], qk_of(n)
            dve.wait_ge(o["rot"], n + 1)
            step(dve.tensor_scalar(x, y, pcol(gain), None, ALU.mult))
            dve.wait_ge(o["sq"], n + 1)
            after(1)
            step(dve.tensor_tensor(y, x, gcon("cos_odd", SEQ), ALU.mult))
            dve.wait_ge(o["rot"], n + 3)
            step(dve.tensor_tensor(rot_sin[:], wide[2 + t % 2][:, 1, :], gcon("sin_odd", SEQ), ALU.mult))
            after(3)
            step(dve.tensor_tensor(y, y, rot_sin[:], ALU.add))
            dve.wait_ge(o["root"], n + 3)
            step(dve.reciprocal(qk_root[:, t % 2, :], qk_root[:, t % 2, :]))
            after(5)
            step(dve.tensor_tensor(y, y, qk_root[:, t % 2, :], ALU.mult))

        def pe_odd_in(pe):
            st = seen["pe"]
            pe.wait_ge(n_used, st.norms)
            pe_tiles(pe, FIRST["odd_in"], G_HEADS, KD, whole(u2), SEQ)
            pe.drain().then_inc(o["sum"], 2)
            pe.drain().then_inc(o["rot"], 2)
            pe_tiles(pe, ODD_Z, G_HEADS, KD, whole(u2), SEQ, after=lambda n, t: pe_qk(pe, n, t))
            pe_tiles(pe, ODD_K, G_KV, KD, whole(u2), SEQ, loop=False)
            for n in range(G_KV):
                pe_qk(pe, G_HEADS + n, n)
            for k in range(2):
                ring.wait_full(pe, ODD_V + k)
            at = ODD_V % SLOTS
            w = ring.tile[:, at:at + 2, :].rearrange("p s (k n) -> p (s k) n", n=G_KV * P)
            for t in range(4):
                pe.wait_ge(tile_left, st.left)
                for k in range(KD):
                    mm = pe.matmul(wide[t][:, 0, 0:G_KV * P], u2[:, k, t * P:(t + 1) * P], w[:, k, :], start=k == 0, stop=k == KD - 1)
                mm.then_inc(o["v_mm"], 1)
            for k in range(2):
                pe.drain().then_inc(ring.done(ODD_V + k), 1)

        def act_odd_in(act):
            act_tiles(act, FIRST["odd_in"], G_HEADS, KD,
                      lambda j, t, n: act.activation(qk_of(n), tile_ps(t, SEQ), ACT.Copy).then_inc(tile_left, 1))
            act.wait_ge(tile_left, seen["act"].left)
            act.drain().then_inc(o["root"], 2)

            def keep_z(j, t, n):
                act.activation(z_flat[:, bass.ds(n * SEQ, SEQ)], tile_ps(t, SEQ), ACT.Copy).then_inc(tile_left, 1)
            act_tiles(act, ODD_Z, G_HEADS, KD, keep_z, before=lambda n, t: act_qk(act, n, t))
            act_tiles(act, ODD_K, G_KV, KD,
                      lambda j, t, n: act.activation(qk_of(G_HEADS + n), tile_ps(t, SEQ), ACT.Copy).then_inc(tile_left, 1), loop=False)
            act.wait_ge(tile_left, seen["act"].left)
            for n in range(G_KV):
                act_qk(act, G_HEADS + n, n)
            for t in range(4):
                act.wait_ge(o["v_mm"], t + 1)
                act.activation(v_odd[:, t, :], wide[t][:, 0, 0:G_KV * P], ACT.Copy).then_inc(o["v_copied"], 1)

        def dve_odd_in(dve):
            st = seen["dve"]
            dve.drain().then_inc(o["dve"], 12)
            dve.wait_ge(tile_left, st.left + G_HEADS + SLOTS)
            over_tiles(dve, G_HEADS, SLOTS, lambda j, t, n: dve_qk(dve, n, t, "q_gain"))
            st.left += 2 * (G_HEADS + SLOTS) + G_KV + SLOTS
            dve.wait_ge(tile_left, st.left)
            for n in range(G_KV):
                dve_qk(dve, G_HEADS + n, n, "k_gain")

        TURNS = G_HEADS // G_KV
        UNITS = G_KV * 4
        AHEAD = 3
        S_BANK = [wide[n // 2][:, n % 2, :] for n in range(4)]

        def pe_scores(pe, j, u):
            j, u = j + u // UNITS, u % UNITS
            x, t = u // 4, u % 4
            if t == 0:
                pe.wait_ge(o["q_now"], 2 * j + x + 1)
            pe.matmul(S_BANK[u % 4], q_now[:, x, t * P:(t + 1) * P], qk[:, G_HEADS + x, :], start=True, stop=True).then_inc(o["scores"], 1)

        def pe_turn(pe, j, last):
            for u in range(UNITS):
                x, t = u // 4, u % 4
                U = UNITS * j + u
                pe.wait_ge(o["share"], 2 * U + 2)
                pe.wait_ge(o["pt"], U + 1)
                for k in range(4):
                    mm = pe.transpose(wide[2][:, u % 2, k * P:(k + 1) * P], o_probs[:, u % 2, k * P:(k + 1) * P], ident)
                mm.then_inc(o["turned"], 1)
                if not (last and u + AHEAD >= UNITS):
                    pe_scores(pe, j, u + AHEAD)
                pe.wait_ge(o["pt"], U + 3)
                if t == 0:
                    pe.wait_ge(o["gated"], 2 * j + x + 1)
                for k in range(4):
                    mm = pe.matmul(wide[3][:, x, t * P:(t + 1) * P], v_odd[:, k, x * P:(x + 1) * P], o_probs_t[:, u % 2, k * P:(k + 1) * P],
                                   start=k == 0, stop=k == 3)
                mm.then_inc(o["pv"], 1)

        def act_turn(act, j, last):
            for x in range(2):
                act.wait_ge(o["z"], 2 * j + x + 1)
                act.activation(tanh_odd[:, x, :], z_flat[:, bass.ds((4 * x + j) * SEQ, SEQ)], ACT.Tanh, scale=0.5).then_inc(o["tanh"], 1)
            for u in range(UNITS):
                U = UNITS * j + u
                act.wait_ge(o["bias"], 2 * U + 2)
                act.wait_ge(o["turned"], U + 1)
                act.activation(o_probs[:, u % 2, :], S_BANK[u % 4], ACT.Exp, bias=o_bias[:, u:u + 1], scale=ODD_SCALE,
                               accum_out=o_sum[:, u:u + 1]).then_inc(o["exp"], 1)
                act.wait_ge(o["turned"], U + 3)
                act.wait_ge(o["pv"], U + 1)
                act.activation(o_probs_t[:, u % 2, :], wide[2][:, u % 2, :], ACT.Copy).then_inc(o["pt"], 1)

        def dve_max(dve, j, u):
            U = UNITS * j + u
            u = u % UNITS
            dve.wait_ge(o["scores"], U + 1)
            dve.tensor_reduce(o_max[:, u:u + 1], S_BANK[u % 4], AX_X, ALU.max).then_inc(o["bias"], 1)
            dve.wait_ge(o["bias"], 2 * U + 1)
            dve.tensor_scalar(o_bias[:, u:u + 1], o_max[:, u:u + 1], -ODD_SCALE, None, ALU.mult).then_inc(o["bias"], 1)

        def dve_turn(dve, j, last):
            for x in range(2):
                dve.wait_ge(o["tanh"], 2 * j + x + 1)
                z = z_flat[:, bass.ds((4 * x + j) * SEQ, SEQ)]
                dve.scalar_tensor_tensor(z, tanh_odd[:, x, :], 1.0, z, ALU.add, ALU.mult).then_inc(o["z"], 1)
            for u in range(UNITS):
                U = UNITS * j + u
                if not (last and u + 1 == UNITS):
                    dve_max(dve, j, u + 1)
                dve.wait_ge(o["exp"], U + 1)
                dve.reciprocal(o_sum[:, u:u + 1], o_sum[:, u:u + 1]).then_inc(o["share"], 1)
                dve.wait_ge(o["share"], 2 * U + 1)
                dve.tensor_scalar(o_probs[:, u % 2, :], o_probs[:, u % 2, :], o_sum[:, u:u + 1], None, ALU.mult).then_inc(o["share"], 1)
                if u % 4 == 3:
                    x = u // 4
                    dve.wait_ge(o["pv"], U + 3)
                    dve.wait_ge(o["z"], 2 * j + x + 3)
                    z = z_flat[:, bass.ds((4 * x + j) * SEQ, SEQ)]
                    dve.scalar_tensor_tensor(z, wide[3][:, x, :], 0.5, z, ALU.mult, ALU.mult).then_inc(o["gated"], 1)

        def pool_q(pool, j, x):
            pool.tensor_copy(q_now[:, x, :], qk_of(4 * x + j)).then_inc(o["q_now"], 1)

        def pool_turn(pool, j, last):
            if not last:
                for x in range(2):
                    pool.wait_ge(o["scores"], UNITS * j + 4 * x + 4)
                    pool_q(pool, j + 1, x)

        def over_turns(eng, body):
            with eng.Fori(0, TURNS - 1) as j:
                body(eng, j, False)
            body(eng, TURNS - 1, True)

        def pe_odd(pe):
            pe.drain().then_inc(o["turned"], 2)
            pe.drain().then_inc(o["pv"], 2)
            pe.wait_ge(o["dve"], 6 * NQK + 12)
            pe.wait_ge(o["v_copied"], 4)
            for u in range(AHEAD):
                pe_scores(pe, 0, u)
            over_turns(pe, pe_turn)
            pe.wait_ge(o["gated"], G_HEADS + 2)
            pe_project_out(pe, FIRST["odd_out"], KD, whole(z_odd), SEQ, None)

        def act_odd(act):
            act.drain().then_inc(o["pt"], 2)
            over_turns(act, act_turn)
            act_project_out(act, FIRST["odd_out"], KD, SEQ, None)

        def dve_odd(dve):
            dve.drain().then_inc(o["z"], 2)
            dve.drain().then_inc(o["gated"], 2)
            dve_max(dve, 0, 0)
            over_turns(dve, dve_turn)
            dve_project_out(dve, KD, SEQ, None, None, "final", lambda k: u2[:, k, 0:SEQ])

        def pool_odd(pool):
            pool.wait_ge(o["dve"], 6 * NQK + 12)
            for x in range(2):
                pool_q(pool, 0, x)
            over_turns(pool, pool_turn)

        def sp_end(sp):
            sp.wait_ge(n_used, NORMS)
            sp.dma_start(out, u2[:, :, 0:SEQ]).then_inc(stored, 16)
            sp.wait_ge(stored, 16)

        stored = sem("stored")
        NORMS = 8

        block = ctx.enter_context(nc.Block())

        @block.sync
        def _(sp):
            sp_setup(sp)
            sp_a(sp)
            sp.wait_ge(s["stored"], 16 * PAIRS)
            for n in range(SLOTS):
                ring.load(sp, stream, FIRST["rwkv_out"] + n)
            sp_b(sp)
            sp_c(sp)
            sp_stream(sp, FIRST["rwkv_out"] + SLOTS, FIRST["even_in"] + SLOTS)
            sp_g(sp)
            sp_stream(sp, FIRST["even_in"] + SLOTS, N_LOADS)
            sp_end(sp)

        @block.tensor
        def _(pe):
            pe_setup(pe)
            pe_lora(pe)
            over_pairs(pe, pe_pair)
            end_phase(pe, "pe")
            passes(pe, pe_pass)
            end_phase(pe, "pe")
            pe.wait_ge(mixed_loaded, 16 * PAIRS)
            pe_project_out(pe, FIRST["rwkv_out"], KI, half_of(z_t), L, L)
            pe_mla_in(pe)
            pe_mla(pe)
            pe.wait_ge(e["gated"], 2 * HEADS + 2)
            pe_project_out(pe, FIRST["mla_out"], KI, half_of(z_t), L, SEQ)
            end_phase(pe, "pe")
            pe_even(pe)
            pe_odd_in(pe)
            pe_odd(pe)

        @block.scalar
        def _(act):
            act_setup(act)
            act_lora(act)
            over_pairs(act, act_pair)
            end_phase(act, "act")
            passes(act, act_pass)
            end_phase(act, "act")
            act_project_out(act, FIRST["rwkv_out"], KI, L, L)
            act_mla_in(act)
            act_mla(act)
            act_project_out(act, FIRST["mla_out"], KI, L, SEQ)
            end_phase(act, "act")
            act_even(act)
            act_odd_in(act)
            act_odd(act)

        @block.vector
        def _(dve):
            dve_setup(dve)
            over_pairs(dve, dve_pair)
            end_phase(dve, "dve")
            dve_b_setup(dve)
            passes(dve, dve_pass)
            end_phase(dve, "dve")
            dve.wait_ge(h_loaded, 16)
            dve_project_out(dve, KI, L, L, "post0", "pre1", lambda k: u2[:, k, :])
            dve_mla_in(dve)
            dve_mla(dve)
            dve_project_out(dve, KI, L, SEQ, "post1", "even", lambda k: u2[:, k, 0:SEQ])
            end_phase(dve, "dve")
            dve_even(dve)
            dve_odd_in(dve)
            dve_odd(dve)

        @block.gpsimd
        def _(pool):
            pool_setup(pool)
            over_pairs(pool, pool_pair)
            end_phase(pool, "pool")
            passes(pool, pool_pass)
            end_phase(pool, "pool")
            pool_mla(pool)
            end_phase(pool, "pool")
            pool_odd(pool)


def tile_columns(w, width=P):
    k, n = w.shape
    return np.ascontiguousarray(w.reshape(k // P, P, n // width, width).transpose(2, 1, 0, 3).reshape(n // width, P, k // P * width))


def loads_of(tiles):
    n, _, m = tiles.shape
    if m >= SLOT:
        return tiles.reshape(n, P, m // SLOT, SLOT).transpose(0, 2, 1, 3).reshape(-1, P, SLOT)
    g = SLOT // m
    return tiles.reshape(n // g, g, P, m).transpose(0, 2, 1, 3).reshape(n // g, P, SLOT)


def weight_stream(a):
    w = a["rwkv_w_in"][0]
    n_main = 4 * DI
    main = tile_columns(w[:, :n_main]).reshape(4, PAIRS, P, SLOT)
    pieces = [tile_columns(w[:, n_main:])]
    pieces.append(np.stack([main[1], main[0], main[2], main[3]], 1).reshape(-1, P, SLOT))
    pieces.append(loads_of(tile_columns(a["rwkv_w_out"][0])))
    m = a["mla_w_in"][0]
    nq, nkv = Q_TILES * P, KV_TILES * P
    rope = m[:, nq + nkv:nq + nkv + KROPE]
    pieces += [tile_columns(m[:, :nq + nkv]), tile_columns(np.concatenate([rope, rope], 1)), tile_columns(m[:, nq + nkv + KROPE:])]
    kv = a["mla_w_kv_up"][0].reshape(nkv, HEADS, 2, P)
    pieces.append(tile_columns(kv[:, :, 1].reshape(nkv, HEADS * P), 512))
    q = a["mla_w_q_up"][0].reshape(nq, HEADS // 2, 2, P + KROPE)
    for j in range(HEADS // 2):
        pieces.append(loads_of(tile_columns(q[:, j, :, :P].reshape(nq, 2 * P))))
        last = np.concatenate([tile_columns(q[:, j, :, P:].reshape(nq, P))[0],
                               tile_columns(kv[:, 2 * j, 0])[0], tile_columns(kv[:, 2 * j + 1, 0])[0]], 1)
        pieces.append(last[None])
    pieces.append(loads_of(tile_columns(a["mla_w_out"][0])))
    e = a["w_in_even_2"][0]
    e = e.reshape(D, 6, 4 * P)
    pieces.append(tile_columns(np.ascontiguousarray(e[:, [4, 2, 0, 1, 3, 5]]).reshape(D, -1)))
    pieces.append(tile_columns(a["w_out_even_2"][0]))
    o = a["w_in_odd_2"][0]
    nq, nkv = G_HEADS * P, G_KV * P
    pieces += [tile_columns(o[:, :nq]), tile_columns(o[:, nq + 2 * nkv:]), tile_columns(o[:, nq:nq + nkv])]
    pieces.append(loads_of(tile_columns(o[:, nq + nkv:nq + 2 * nkv], 2 * P)))
    pieces.append(tile_columns(a["w_out_odd_2"][0]))
    stream = np.concatenate(pieces, 0)
    assert stream.shape == (N_LOADS, P, SLOT), stream.shape
    return stream


def columns(v):
    return np.ascontiguousarray(v.reshape(-1, P).T)


def parameters(a):
    out = np.zeros((P, N_PAR), np.float32)

    def put(name, v):
        c = columns(v)
        out[:, PAR[name]:PAR[name] + c.shape[1]] = c
    for n in range(2):
        put(f"pre{n}", a["norm_pre"][n])
        put(f"post{n}", a["norm_post"][n])
    put("mu", a["rwkv_mu"][0])
    put("rwkv", np.concatenate([a[n][0] for n in ("rwkv_w0", "rwkv_a0", "rwkv_k_k", "rwkv_k_a", "rwkv_r_k", "rwkv_ln_w", "rwkv_ln_b")]))
    put("q_norm", a["mla_q_norm"][0])
    put("kv_norm", a["mla_kv_norm"][0])
    put("even", a["norm_even_2"][0])
    put("conv", a["conv_w_2"][0])
    put("odd", a["norm_odd_2"][0])
    put("q_gain", a["q_gain_2"][0])
    put("k_gain", a["k_gain_2"][0])
    put("final", a["final_norm_2"])
    return out


def constants():
    con = np.zeros((P, N_CON), np.float64)

    def put(name, v):
        con[:, CON[name]:CON[name] + v.shape[1]] = v
    r, c = np.arange(P)[:, None], np.arange(P)[None, :]
    put("ident", np.eye(P))
    put("ones", np.ones((P, P)))
    put("heads", r // C == c // C)
    for n in range(6):
        m = 1 << n
        put_at = (r // (2 * m) == c // (2 * m)) & (r // m % 2 == 1) & (c // m % 2 == 0)
        con[:, CON["levels"] + n * 3 * P:CON["levels"] + (n + 1) * 3 * P] = np.tile(put_at, (1, 3))
        if n == 0:
            put("level0T", np.tile(put_at.T, (1, 3)))
    put("ident3", np.tile(np.eye(P), (1, 3)))
    s, t = np.arange(P)[:, None] % C, np.arange(C)[None, :]
    put("tri", np.tile(np.concatenate([s < t, s <= t], 1), (1, 3)))
    put("reset", np.repeat((np.arange(LP) % C != 0)[None], P, 0))
    put("causal", np.where(c <= r, 0.0, -BIG))
    half = KROPE // 2
    inv = np.exp(-math.log(10000.0) * np.arange(half) / half)
    ang = (inv[:, None] * np.arange(L)[None, :])[np.arange(P) % half]
    put("cos_mla", np.cos(ang))
    put("sin_mla", np.sin(ang))
    rot = np.zeros((P, P))
    for b in range(0, P, KROPE):
        for n in range(half):
            rot[b + half + n, b + n] = -1
            rot[b + n, b + half + n] = 1
    put("rot_mla", rot)
    pos = np.arange(SEQ)
    inv = 10000.0 ** (-np.arange(P // 4) / (P // 4))
    ang = np.concatenate([(pos // 64)[None] * inv[:, None], (pos % 64)[None] * inv[:, None]], 0)[np.arange(P) // 2]
    put("cos_odd", np.cos(ang))
    put("sin_odd", np.sin(ang))
    rot = np.zeros((P, P))
    for n in range(0, P, 2):
        rot[n + 1, n] = -1
        rot[n, n + 1] = 1
    put("rot_odd", rot)
    d = np.outer(np.arange(E_DIM), np.arange(E_DIM)) % E_DIM * (2 * math.pi / E_DIM)
    put("dft_d", np.concatenate([np.cos(d), np.sin(d)], 1))
    n = np.outer(np.arange(SEQ), np.arange(SEQ)) % SEQ * (2 * math.pi / SEQ)
    scale = (SEQ * E_DIM) ** -0.5
    dft = np.stack([np.cos(n) * scale, -np.sin(n) * scale]).reshape(2, SEQ // P, P, SEQ).transpose(2, 0, 1, 3)
    return con.astype(np.float32), np.ascontiguousarray(dft.astype(np.float32))


def device_inputs(a):
    tokens = np.concatenate([a["meta_tokens"], a["x"][0]], 0)
    con, dft = constants()
    lora = np.concatenate([a["rwkv_w2"][0], a["rwkv_a2"][0]], 0)
    return {
        "tokens": np.ascontiguousarray(tokens.T.reshape(KD, P, L).transpose(1, 0, 2)),
        "stream": weight_stream(a),
        "lora": np.ascontiguousarray(lora.reshape(P, PAIRS, P).transpose(1, 0, 2)),
        "par": parameters(a), "con": con, "dft": dft,
    }


def build(nc, arrays):
    def dram(name, shape, kind):
        return nc.dram_tensor(name, shape, F32, kind=kind).ap()

    ins = [dram(f"in_{n}", arrays[n].shape, "ExternalInput") for n in ("tokens", "stream", "lora", "par", "con", "dft")]
    out = dram("out", (P, KD, SEQ), "ExternalOutput")
    program(nc, *ins, out, dram("forms", (PAIRS, P, F_COLS), "Internal"), dram("mixed", (PAIRS, P, L), "Internal"))


def kernel(**inputs):
    import concourse.bacc as bacc
    from concourse.bass_utils import run_bass_kernel_spmd

    arrays = device_inputs({n: np.asarray(v) for n, v in inputs.items()})
    nc = bacc.Bacc("TRN2", target_bir_lowering=False, num_devices=1)
    build(nc, arrays)
    r = run_bass_kernel_spmd(nc, [{f"in_{n}": v for n, v in arrays.items()}], core_ids=[0])
    got = r.results[0]["out"]
    return np.ascontiguousarray(got.transpose(2, 1, 0).reshape(1, SEQ, D))
```

```python
import math
from contextlib import ExitStack

import numpy as np

import concourse.bass as bass
from concourse import mybir

F32 = mybir.dt.float32
ALU = mybir.AluOpType
ACT = mybir.ActivationFunctionType
AX_X = mybir.AxisListType.X

P = 128
D = 1024
DI = 2048
SEQ = 512
META = 16
L = META + SEQ
HALF = L // 2
KD = D // P
KI = DI // P
PAIRS = DI // P
C = 64
NC = -(-L // C)
LP = NC * C
PAD = LP - L
LORA = 64
RMS_EPS = 1e-6
GN_EPS = 64e-5
EXP_M_HALF = math.exp(-0.5)
Q_TILES, KV_TILES = 4, 2
HEADS = 16
KROPE = 64
E_G, E_DIM = 4, 128
G_HEADS, G_KV = 8, 2
BIG = 1e30

SLOT = 1024
SLOTS = 4
LOADS = [("lora", 1), ("rwkv_in", 4 * PAIRS), ("rwkv_out", 2 * KD), ("mla_in", Q_TILES + KV_TILES + 1 + KI),
         ("mla_v", 4), ("mla_up", HEADS), ("mla_out", 2 * KD), ("even_in", 24), ("even_out", KD),
         ("odd_in", 2 * G_HEADS + G_KV), ("odd_v", 2), ("odd_out", KD)]
FIRST = {}
_n = 0
for _name, _count in LOADS:
    FIRST[_name] = _n
    _n += _count
N_LOADS = _n

PAR = {}
_n = 0
for _name, _count in [("pre0", KD), ("post0", KD), ("pre1", KD), ("post1", KD), ("mu", 6 * KD), ("rwkv", 7 * PAIRS),
                      ("q_norm", Q_TILES), ("kv_norm", KV_TILES), ("even", KD), ("conv", 12), ("odd", KD),
                      ("q_gain", 1), ("k_gain", 1), ("final", KD)]:
    PAR[_name] = _n
    _n += _count
N_PAR = _n
W0, A0, KK, KA, RK, LNW, LNB = range(7)

CON, CON_OF = {}, {}
_n = 0
for _part, _names in [("all", [("ident", P), ("ones", P), ("heads", P), ("reset", LP)]),
                      ("rwkv", [("levels", 6 * P), ("level0T", P), ("tri", 2 * C)]),
                      ("mla", [("causal", P), ("rot_mla", P), ("cos_mla", L), ("sin_mla", L)]),
                      ("odd", [("rot_odd", P), ("cos_odd", SEQ), ("sin_odd", SEQ), ("dft_d", 2 * E_DIM)])]:
    _first = _n
    for _name, _count in _names:
        CON[_name] = _n
        _n += _count
    CON_OF[_part] = (_first, _n - _first)
N_CON = _n

F_AR, F_B, F_K, F_V, F_SG, F_BON, F_PC = 0, 2 * LP, 3 * LP, 4 * LP, 5 * LP, 6 * LP, 7 * LP
F_COLS = F_PC + NC


class Count:

    def __init__(self, sem, per=1):
        self.sem, self.per = sem, per

    def at(self, i, k):
        return i * self.per + k

    def before(self, i):
        return i * self.per


class Ring:

    def __init__(self, tile, full, used):
        self.tile, self.full, self.used = tile, full, used

    def slot(self, load):
        return self.tile[:, load % SLOTS, :]

    def wait_full(self, eng, load, step=0):
        eng.wait_ge(self.full[load % SLOTS], (step + load // SLOTS + 1) * 16)

    def wait_used(self, eng, load, step=0):
        eng.wait_ge(self.used[load % SLOTS], step + load // SLOTS + 1)

    def done(self, load):
        return self.used[load % SLOTS]

    def load(self, sp, stream, load, step=0):
        if not (isinstance(step, int) and load + SLOTS * step < SLOTS):
            sp.wait_ge(self.used[load % SLOTS], step + load // SLOTS)
        sp.dma_start(self.slot(load), stream[step * SLOTS + load]).then_inc(self.full[load % SLOTS], 16)


class Norms:

    def __init__(self, squared, summed, rooted, inverted):
        self.squared, self.summed, self.rooted, self.inverted = squared, summed, rooted, inverted


def program(nc, x_in, stream, lora_in, par_in, con_in, dft_in, out, forms, mixed):
    with ExitStack() as ctx:
        def sb(name, *shape):
            return ctx.enter_context(nc.sbuf_tensor(name, [P, *shape], F32))

        def sem(name):
            return ctx.enter_context(nc.semaphore(name))

        wide = [ctx.enter_context(nc.psum_tensor(f"wide{j}", [P, 2, 512], F32)) for j in range(4)]
        ring = Ring(sb("weights", SLOTS, SLOT), [sem(f"weights_full{s}") for s in range(SLOTS)],
                    [sem(f"weights_used{s}") for s in range(SLOTS)])
        par = sb("par", N_PAR)
        con = sb("con", CON_OF["all"][1])
        inv_rms = sb("inv_rms", L)
        epsilon = sb("epsilon", 2)

        half_w0 = sb("half_w0a0", 2 * PAIRS)

        def cons(name, width):
            return con[:, CON[name]:CON[name] + width]

        def pcol(name, n=0):
            return par[:, PAR[name] + n:PAR[name] + n + 1]

        ident, ones, heads = cons("ident", P), cons("ones", P), cons("heads", P)

        x_loaded, con_loaded = sem("x_loaded"), sem("con_loaded")
        const_set, eps_set = sem("const_set"), sem("eps_set")
        phase_done = sem("phase_done")
        squared, summed, rooted, inverted = (sem(n) for n in ("squared", "summed", "rooted", "inverted"))
        applied = sem("applied")

        PHASES = {"pe": 0, "act": 0, "dve": 0, "pool": 0, "sp": 0}

        def end_phase(eng, who):
            PHASES[who] += 1
            eng.drain().then_inc(phase_done, 1)
            eng.wait_ge(phase_done, 4 * PHASES[who])

        class N:
            sq = 0
            n = 0

        def halves(ap, width):
            return ap.rearrange("p (b n) -> p b n", b=2) if width == L else ap

        def act_norm(act, st, src, kt, width, sq, ps, eps, div):
            for k in range(kt):
                act.activation(sq(k), src(k), ACT.Square).then_inc(squared, 1)
            st.sq += kt
            st.n += 1
            act.wait_ge(summed, st.n)
            act.activation(halves(inv_rms[:, 0:width], width), ps(width), ACT.Sqrt,
                           bias=epsilon[:, 0:1], scale=1.0 / div).then_inc(rooted, 1)

        def pe_norm(pe, st, kt, width, sq, ps):
            w = ps(width)
            parts = [(w[:, b, :], slice(b * HALF, (b + 1) * HALF)) for b in range(2)] if width == L else [(w, slice(0, width))]
            for k in range(kt):
                st.sq += 1
                pe.wait_ge(squared, st.sq)
                for dst, cols in parts:
                    mm = pe.matmul(dst, ones, sq(k)[:, cols], start=k == 0, stop=k == kt - 1)
            mm.then_inc(summed, 1)

        def dve_norm(dve, st, width):
            st.n += 1
            dve.wait_ge(rooted, st.n)
            dve.reciprocal(inv_rms[:, 0:width], inv_rms[:, 0:width]).then_inc(inverted, 1)
            dve.wait_ge(inverted, st.n)

        def wide_ps(j):
            return lambda width: wide[j][:, :, 0:HALF] if width == L else wide[j][:, 0, 0:width]

        norm = {who: N() for who in ("pe", "act", "dve")}
        for st in norm.values():
            st.sq = st.n = 0

        A = ExitStack()

        def sa(name, *shape):
            return A.enter_context(nc.sbuf_tensor(name, [P, *shape], F32))

        x_t = sa("x", KD, L)
        u = sa("u", KD, 1 + L)
        mixed_in = sa("mixed_in", 4, KD, L)
        diff = sa("diff", KD, L)
        lora = sa("lora", L)
        lora_w = sa("lora_w", P)
        a_r, a_k, a_lw, a_cum, a_a, a_kk, a_sq, a_inv, a_k2, a_rk, a_tg, a_Pinv = (
            sa(n, LP) for n in ("r", "k", "log_decay", "log_cum", "a", "kk", "kk_sq", "kk_inv", "k2", "rk", "tanh_g", "p_inv"))
        a_P = sa("p_cum", NC, 1 + C)
        form = sa("form", F_COLS)
        A.close()
        f_ar = form[:, F_AR:F_AR + 2 * LP].rearrange("p (c s n) -> p c s n", c=NC, s=2)
        f_b, f_k, f_v, f_sg, f_bon = (form[:, o:o + LP] for o in (F_B, F_K, F_V, F_SG, F_BON))
        f_pc = form[:, F_PC:F_PC + NC]
        LERP = {"k": 0, "r": 1, "v": 2, "g": 3}
        MU = {"r": 0, "k": 1, "v": 2, "g": 3, "w": 4, "a": 5}

        def real(ap):
            return ap[:, PAD:LP].rearrange("p (b n) -> p b n", b=2)

        def by_chunk(ap):
            return ap.rearrange("p (c n) -> p c n", c=NC)

        def rw(which, pair):
            if isinstance(pair, int):
                return pcol("rwkv", which * PAIRS + pair)
            return par[:, bass.ds(pair + (PAR["rwkv"] + which * PAIRS), 1)]

        a_sems = {n: sem("a_" + n) for n in (
            "lerp", "lora_loaded", "lora_low", "proj_w", "proj_a", "tanh_w", "tanh_a", "k_copied", "r_copied", "kk_squared",
            "p_exp", "kk_summed", "kk_rooted", "v_copied", "g_tanh", "pc_copied", "rk_summed", "dve", "pool", "stored")}

        def half_bias(n, pair):
            if isinstance(pair, int):
                return half_w0[:, n * PAIRS + pair:n * PAIRS + pair + 1]
            return half_w0[:, bass.ds(pair + n * PAIRS, 1)]

        s = a_sems
        DVE_A = Count(s["dve"], 15)
        POOL_A = Count(s["pool"], 2)
        EXP_A = Count(s["p_exp"], 2)

        def sp_setup(sp):
            for k in range(KD):
                sp.dma_start(x_t[:, k, :], x_in[:, k, :]).then_inc(x_loaded, 16)
            sp.dma_start(par[:], par_in).then_inc(con_loaded, 16)
            sp.dma_start(con[:], con_in[:, 0:CON_OF["all"][1]]).then_inc(con_loaded, 16)
            ring.load(sp, stream, 0)
            for j in range(3):
                ring.load(sp, stream, 1 + j)

        def act_setup(act):
            act.wait_ge(eps_set, 2)
            act.wait_ge(x_loaded, 16 * KD)
            act_norm(act, norm["act"], lambda k: x_t[:, k, :], KD, L, lambda k: mixed_in[:, 0, k, :], wide_ps(0), 0, D)

        def pe_setup(pe):
            pe.wait_ge(con_loaded, 32)
            pe_norm(pe, norm["pe"], KD, L, lambda k: mixed_in[:, 0, k, :], wide_ps(0))

        def pool_setup(pool):
            pool.memset(u[:, :, 0:1], 0.0).then_inc(const_set, 1)
            for t in (a_r, a_k, a_lw, a_a, a_kk, a_sq, a_inv, form):
                pool.memset(t[:], 0.0).then_inc(const_set, 1)
            pool.memset(a_P[:, :, 0:1], 1.0).then_inc(const_set, 1)

        N_SET = 10

        def dve_setup(dve):
            dve.memset(epsilon[:, 0:1], RMS_EPS).then_inc(eps_set, 1)
            dve.memset(epsilon[:, 1:2], GN_EPS).then_inc(eps_set, 1)
            dve.wait_ge(con_loaded, 32)
            dve.tensor_scalar(half_w0[:], par[:, PAR["rwkv"]:PAR["rwkv"] + 2 * PAIRS], 0.5, None, ALU.mult).then_inc(applied, 1)
            dve_norm(dve, norm["dve"], L)
            dve.wait_ge(const_set, N_SET)
            for k in range(KD):
                dve.scalar_tensor_tensor(u[:, k, 1:], x_t[:, k, :], pcol("pre0", k), inv_rms[:], ALU.mult, ALU.mult).then_inc(applied, 1)
            dve.wait_ge(applied, 1 + KD)
            dve.tensor_tensor(diff[:], u[:, :, 0:L], u[:, :, 1:], ALU.subtract).then_inc(applied, 1)
            dve.wait_ge(applied, 2 + KD)

            def lerp(dst, which):
                for k in range(KD):
                    dve.scalar_tensor_tensor(dst[:, k, :], diff[:, k, :], pcol("mu", MU[which] * KD + k), u[:, k, 1:],
                                             ALU.mult, ALU.add).then_inc(s["lerp"], 1)
            lerp(mixed_in[:, 2], "w")
            lerp(mixed_in[:, 3], "a")
            lerp(mixed_in[:, 0], "k")
            lerp(mixed_in[:, 1], "r")
            dve.wait_ge(s["proj_w"], 1)
            dve.wait_ge(s["proj_a"], 1)
            lerp(mixed_in[:, 2], "v")
            lerp(mixed_in[:, 3], "g")

        def product(pe, dst, load, rhs, step=0, kt=KD):
            for b in range(2):
                for k in range(kt):
                    mm = pe.matmul(dst[:, b, 0:HALF], ring.slot(load)[:, k * P:(k + 1) * P], rhs[:, k, b * HALF:(b + 1) * HALF],
                                   start=k == 0, stop=k == kt - 1)
            return mm

        def pe_lora(pe):
            ring.wait_full(pe, 0)
            pe.wait_ge(s["lerp"], KD)
            product(pe, wide[0], 0, mixed_in[:, 2]).then_inc(s["proj_w"], 1)
            pe.wait_ge(s["lerp"], 2 * KD)
            product(pe, wide[1], 0, mixed_in[:, 3]).then_inc(ring.done(0), 1)
            pe.drain().then_inc(s["proj_a"], 1)

        def act_lora(act):
            act.wait_ge(s["proj_w"], 1)
            act.activation(lora[0:LORA, :].rearrange("p (b n) -> p b n", b=2), wide[0][0:LORA, :, 0:HALF], ACT.Tanh).then_inc(s["lora_low"], 1)
            act.wait_ge(s["proj_a"], 1)
            act.activation(lora[LORA:P, :].rearrange("p (b n) -> p b n", b=2), wide[1][LORA:P, :, 0:HALF], ACT.Copy).then_inc(s["lora_low"], 1)

        LERP_OF = [("k", 2), ("r", 3), ("v", 0), ("g", 1)]

        def pe_pair(pe, i, first):
            def project(j, dst, lerps):
                ring.wait_full(pe, 1 + j, i)
                if first:
                    pe.wait_ge(s["lerp"], lerps * KD)
                product(pe, dst, 1 + j, mixed_in[:, j], i).then_inc(ring.done(1 + j), 1)

            if not first:
                pe.wait_ge(s["kk_rooted"], i)
            project(0, wide[2], 3)
            if not first:
                pe.wait_ge(DVE_A.sem, DVE_A.before(i))
            project(1, wide[3], 4)
            pe.wait_ge(s["lora_loaded"], 16 * i + 16)
            if first:
                pe.wait_ge(s["lora_low"], 2)
            else:
                pe.wait_ge(s["v_copied"], i)
            for low, rows, dst in ((s["proj_w"], slice(0, LORA), wide[0]), (s["proj_a"], slice(LORA, P), wide[1])):
                for b in range(2):
                    mm = pe.matmul(dst[:, b, 0:HALF], lora_w[rows, :], lora[rows, b * HALF:(b + 1) * HALF], start=True, stop=True)
                mm.then_inc(low, 1)
            pe.wait_ge(s["tanh_w"], i + 1)
            project(2, wide[0], 5)
            pe.wait_ge(s["k_copied"], i + 1)
            pe.wait_ge(s["kk_squared"], i + 1)
            for b in range(2):
                mm = pe.matmul(wide[2][:, b, 0:HALF], heads, a_sq[:, PAD + b * HALF:PAD + (b + 1) * HALF], start=True, stop=True)
            mm.then_inc(s["kk_summed"], 1)
            pe.wait_ge(s["tanh_a"], i + 1)
            project(3, wide[1], 6)
            pe.wait_ge(s["r_copied"], i + 1)
            pe.wait_ge(DVE_A.sem, DVE_A.at(i, 7))
            for b in range(2):
                mm = pe.matmul(wide[3][:, b, 0:HALF], heads, a_rk[:, PAD + b * HALF:PAD + (b + 1) * HALF], start=True, stop=True)
            mm.then_inc(s["rk_summed"], 1)

        def act_pair(act, i, first):
            if first:
                act.wait_ge(const_set, N_SET)
                act.wait_ge(applied, 1)
            else:
                act.wait_ge(DVE_A.sem, DVE_A.before(i))
                act.wait_ge(POOL_A.sem, POOL_A.before(i))
            ring.wait_used(act, 1, i)
            act.activation(real(a_k), wide[2][:, :, 0:HALF], ACT.Copy).then_inc(s["k_copied"], 1)
            act.wait_ge(DVE_A.sem, DVE_A.at(i, 1))
            act.activation(a_sq[:], a_kk[:], ACT.Square).then_inc(s["kk_squared"], 1)
            ring.wait_used(act, 2, i)
            act.activation(real(a_r), wide[3][:, :, 0:HALF], ACT.Copy).then_inc(s["r_copied"], 1)
            act.wait_ge(s["proj_w"], i + 2)
            act.activation(real(a_lw), wide[0][:, :, 0:HALF], ACT.Tanh, bias=half_bias(0, i), scale=0.5).then_inc(s["tanh_w"], 1)
            act.wait_ge(s["proj_a"], i + 2)
            act.activation(real(a_a), wide[1][:, :, 0:HALF], ACT.Tanh, bias=half_bias(1, i), scale=0.5).then_inc(s["tanh_a"], 1)
            act.wait_ge(DVE_A.sem, DVE_A.at(i, 3))
            act.activation(a_P[:, :, 1:], by_chunk(a_cum[:]), ACT.Exp).then_inc(EXP_A.sem, 1)
            act.activation(a_Pinv[:], a_cum[:], ACT.Exp, scale=-1.0).then_inc(EXP_A.sem, 1)
            ring.wait_used(act, 3, i)
            if not first:
                act.wait_ge(s["stored"], 16 * i)
            act.activation(real(f_v), wide[0][:, :, 0:HALF], ACT.Copy).then_inc(s["v_copied"], 1)
            act.wait_ge(s["kk_summed"], i + 1)
            act.activation(real(a_inv), wide[2][:, :, 0:HALF], ACT.Sqrt).then_inc(s["kk_rooted"], 1)
            ring.wait_used(act, 4, i)
            act.activation(real(a_tg), wide[1][:, :, 0:HALF], ACT.Tanh, scale=0.5).then_inc(s["g_tanh"], 1)
            act.wait_ge(EXP_A.sem, EXP_A.at(i, 1))
            act.activation(f_pc, a_P[:, :, C:C + 1].rearrange("p c n -> p (c n)"), ACT.Copy).then_inc(s["pc_copied"], 1)

        def dve_pair(dve, i, first):
            def step(ins):
                ins.then_inc(DVE_A.sem, 1)

            def after(k):
                dve.wait_ge(DVE_A.sem, DVE_A.at(i, k))

            half = 0.5 * EXP_M_HALF
            dve.wait_ge(s["k_copied"], i + 1)
            step(dve.tensor_scalar(a_kk[:], a_k[:], rw(KK, i), None, ALU.mult))
            dve.wait_ge(s["tanh_w"], i + 1)
            step(dve.tensor_scalar(a_lw[:, PAD:], a_lw[:, PAD:], -half, -half, ALU.mult, ALU.add))
            after(2)
            step(dve.tensor_tensor_scan(a_cum[:], cons("reset", LP), a_lw[:], 0.0, ALU.mult, ALU.add))
            dve.wait_ge(s["tanh_a"], i + 1)
            step(dve.tensor_scalar(a_a[:, PAD:], a_a[:, PAD:], 0.5, 0.5, ALU.mult, ALU.add))
            after(4)
            step(dve.tensor_scalar(a_k2[:], a_a[:], 1.0, rw(KA, i), ALU.subtract, ALU.mult))
            after(5)
            step(dve.scalar_tensor_tensor(a_k2[:], a_k2[:], 1.0, a_k[:], ALU.add, ALU.mult))
            after(6)
            dve.wait_ge(s["r_copied"], i + 1)
            step(dve.scalar_tensor_tensor(a_rk[:], a_r[:], rw(RK, i), a_k2[:], ALU.mult, ALU.mult))
            dve.wait_ge(s["kk_rooted"], i + 1)
            step(dve.tensor_scalar(a_inv[:, PAD:], a_inv[:, PAD:], 1e-12, None, ALU.max))
            after(8)
            step(dve.reciprocal(a_inv[:, PAD:], a_inv[:, PAD:]))
            after(9)
            step(dve.tensor_tensor(a_kk[:, PAD:], a_kk[:, PAD:], a_inv[:, PAD:], ALU.mult))
            after(10)
            dve.wait_ge(EXP_A.sem, EXP_A.at(i, 2))
            if not first:
                dve.wait_ge(s["stored"], 16 * i)
            step(dve.scalar_tensor_tensor(f_ar[:, :, 0, :], by_chunk(a_kk[:]), -1.0, a_P[:, :, 0:C], ALU.mult, ALU.mult))
            step(dve.tensor_tensor(a_inv[:, PAD:], a_kk[:, PAD:], a_a[:, PAD:], ALU.mult))
            after(12)
            step(dve.tensor_tensor(f_b[:, PAD:], a_inv[:, PAD:], a_Pinv[:, PAD:], ALU.mult))
            dve.wait_ge(s["v_copied"], i + 1)
            dve.wait_ge(s["rk_summed"], i + 1)
            step(dve.tensor_tensor(real(f_bon), wide[3][:, :, 0:HALF], real(f_v), ALU.mult))
            dve.wait_ge(s["g_tanh"], i + 1)
            step(dve.scalar_tensor_tensor(real(f_sg), real(a_tg), 1.0, wide[1][:, :, 0:HALF], ALU.add, ALU.mult))

        def pool_pair(pool, i, first):
            pool.wait_ge(EXP_A.sem, EXP_A.at(i, 2))
            if not first:
                pool.wait_ge(s["stored"], 16 * i)
            pool.wait_ge(DVE_A.sem, DVE_A.at(i, 6))
            pool.tensor_tensor(f_k, a_k2[:], a_Pinv[:], ALU.mult).then_inc(POOL_A.sem, 1)
            pool.wait_ge(s["r_copied"], i + 1)
            pool.tensor_tensor(f_ar[:, :, 1, :], by_chunk(a_r[:]), a_P[:, :, 1:], ALU.mult).then_inc(POOL_A.sem, 1)

        def sp_store(sp, i):
            sp.wait_ge(DVE_A.sem, DVE_A.at(i, 15))
            sp.wait_ge(POOL_A.sem, POOL_A.at(i, 2))
            sp.wait_ge(s["v_copied"], i + 1)
            sp.wait_ge(s["pc_copied"], i + 1)
            sp.dma_start(forms[i], form[:]).then_inc(s["stored"], 16)

        def sp_a(sp):
            sp.dma_start(lora_w[:], lora_in[0]).then_inc(s["lora_loaded"], 16)
            ring.load(sp, stream, 4)
            with sp.Fori(1, PAIRS) as i:
                sp.wait_ge(s["proj_a"], i + 1)
                sp.dma_start(lora_w[:], lora_in[i]).then_inc(s["lora_loaded"], 16)
                for j in range(4):
                    ring.load(sp, stream, 1 + j, i)
                sp_store(sp, i - 1)
            sp_store(sp, PAIRS - 1)

        def over_pairs(eng, body):
            body(eng, 0, True)
            with eng.Fori(1, PAIRS) as i:
                body(eng, i, False)

        B = ExitStack()

        def sbb(name, *shape):
            return B.enter_context(nc.sbuf_tensor(name, [P, *shape], F32))

        def sbr(name, *shape):
            return B.enter_context(nc.sbuf_tensor(name, [P, *shape], mybir.dt.float32r))

        GROUPS, GC = 3, NC // 3
        LEVEL_BUFS = 2
        LEVELS = 5
        b_ar = sbb("a_r", NC, 2, C)
        b_b, b_k, b_v, b_a = (sbb(n, NC, P) for n in ("b_diag", "k_diag", "v_diag", "a_diag"))
        b_r = sbb("r_diag", 2, NC, P)
        b_sgbon, b_pc = sbb("gate_bonus", 2, 2, LP), sbb("p_chunk", 2, NC)
        qg = sbb("b_with_a_r", 2, NC, 2, P)
        mg = sbb("k_with_a_r", 2, NC, 2, P)
        tokens_of = sbb("token_rows", 2, 4, NC, P)
        n_all, n_lvl = sbb("n", NC, P), sbr("n_levels", LEVEL_BUFS, NC, P)
        w_inv = sbb("w_inv", NC, P)
        mv, a_hat = sbb("m_v", NC, P), sbb("a_hat", NC, P)
        w_rnd, x_rnd, e_rnd = (sbr(n, NC, P) for n in ("w_rounded", "x_rounded", "e_rounded"))
        i_less_w = sbb("i_less_w", NC, P)
        state, state_p, u_row = (sbb(n, P) for n in ("state", "state_decayed", "u_rows"))
        y_rows, y_sq, y_diag = sbb("y_rows", NC, C), sbb("y_sq", NC, C), sbb("y_diag", NC, P)
        y_sum, y_mean, y_var = sbb("y_sum", NC), sbb("y_mean", NC), sbb("y_var", NC)
        b_con = sbb("masks", CON_OF["rwkv"][1])
        y_ln = sbb("y_ln", NC, C)
        B.close()
        inv_bank = [wide[0][:, 0, :], wide[0][:, 1, :], wide[1][:, 0, :]]
        state_bank, chunk_bank, y_bank, post_bank = wide[2][:, 0, :], wide[2][:, 1, :], wide[3][:, 0, :], wide[3][:, 1, :]
        odd_bank = [wide[1][:, 1, :], post_bank]
        end_bank = [state_bank, chunk_bank, y_bank]
        b_names = ("forms_loaded", "qg_made", "mg_made", "token_mm", "token_rows", "n_turned", "n_rows",
                   "w_start", "x_start", "n_level", "e_mm", "e_rows", "w_mm", "w_added", "x_mm", "x_rows", "f_mm", "lack", "v_mm", "w_done", "i_less_w", "m_mm", "m_rows", "a_mm", "a_rows",
                   "u_mm", "u_rows", "s_mm", "s_rows", "y_mm", "y_rows", "g_mm", "k_mm", "post", "y_rooted", "y_turned", "z_sum",
                   "z_made", "z_stored", "diag_set")
        sb_ = {n: sem("b_" + n) for n in b_names}
        q = sb_
        HEAD_ROWS = (slice(0, C), slice(C, P))
        N_DIAG = 8
        POST = 15

        def three(ap):
            return ap[:, 0:GC * P].rearrange("p (c n) -> p c n", c=GC)

        def grp(g):
            return slice(g * GC, (g + 1) * GC)

        def mask(name, n=0):
            at = CON[name] - CON_OF["rwkv"][0] + n * P
            return b_con[:, at:at + P].unsqueeze(1).to_broadcast([P, GC, P])

        eye = ident.unsqueeze(1).to_broadcast([P, GC, P])
        tri_at = CON["tri"] - CON_OF["rwkv"][0]
        tri = b_con[:, tri_at:tri_at + 2 * C].rearrange("p (s n) -> p s n", s=2)

        def sp_diag(sp, dst, pair, col, sem_):
            for hd, rows in enumerate(HEAD_ROWS):
                sp.dma_start(dst[rows, :, hd * C:(hd + 1) * C], forms[pair, rows, col:col + LP].rearrange("p (c n) -> p c n", c=NC)).then_inc(sem_, 16)

        def ar_of(pair, rows):
            return forms[pair, rows, F_AR:F_AR + 2 * LP].rearrange("p (c s n) -> p c s n", c=NC, s=2)

        def sp_b_pair(sp, i, par_, post):
            if not (isinstance(i, int) and i == 0):
                sp.wait_ge(q["token_mm"], 12 * i)
            sp.dma_start(b_ar[:], forms[i, :, F_AR:F_AR + 2 * LP].rearrange("p (c s n) -> p c s n", c=NC, s=2)).then_inc(q["forms_loaded"], 16)
            for dst, col in ((b_b, F_B), (b_k, F_K), (b_v, F_V)):
                sp_diag(sp, dst, i, col, q["forms_loaded"])
            for hd, rows in enumerate(HEAD_ROWS):
                sp.dma_start(b_a[rows, :, hd * C:(hd + 1) * C], ar_of(i, rows)[:, :, 0, :]).then_inc(q["forms_loaded"], 16)
            if post:
                sp.wait_ge(q["y_mm"], 9 * (i - 1))
                sp.wait_ge(q["s_rows"], 9 * (i - 1))
            for hd, rows in enumerate(HEAD_ROWS):
                sp.dma_start(b_r[rows, par_, :, hd * C:(hd + 1) * C], ar_of(i, rows)[:, :, 1, :]).then_inc(scan_loaded[par_], 16)
            sp.dma_start(b_pc[:, par_, :], forms[i, :, F_PC:F_PC + NC]).then_inc(scan_loaded[par_], 16)
            if post:
                sp_z(sp, i - 2, par_)
                sp.wait_ge(q["z_stored"], 16 * (i - 1))
            sp.dma_start(b_sgbon[:, par_], forms[i, :, F_SG:F_SG + 2 * LP].rearrange("p (s n) -> p s n", s=2)).then_inc(scan_loaded[par_], 16)

        FORMS_DMAS, SCAN_DMAS = 16 * 9, 16 * 4

        def sp_z(sp, pair, par_):
            sp.wait_ge(q["z_made"], pair + 1)
            sp.dma_start(mixed[pair], b_sgbon[:, par_, 0, PAD:]).then_inc(q["z_stored"], 16)

        scan_loaded = [sem("b_scan_loaded0"), sem("b_scan_loaded1")]

        def wait_scan(eng, pair, parity):
            eng.wait_ge(scan_loaded[parity], SCAN_DMAS // 2 * pair + (SCAN_DMAS // 2 if parity else SCAN_DMAS))

        def is0(i):
            return isinstance(i, int) and i == 0

        def merged(first, second):
            out, done = [], [0, 0]
            total = [max(sum(item[2] for item in part), 1) for part in (first, second)]
            parts = [list(first), list(second)]
            while parts[0] or parts[1]:
                n = 0 if not parts[1] or (parts[0] and done[0] * total[1] <= done[1] * total[0]) else 1
                name, arg, weight = parts[n].pop(0)
                out.append((name, arg))
                done[n] += weight
            return out

        NORM_AT = 8

        def schedule(inv, scan, post):
            setup, levels, ending, walk, norm = [], [], [], [], []
            if inv:
                setup = [("G", g, 3) for g in range(GROUPS)] + [("K", g, 3) for g in range(GROUPS)]
                setup += [("T", g, 2) for g in range(GROUPS)] + [("start", g, 0) for g in range(GROUPS)]
            if post:
                setup += [("stats", 0, 0)]
                norm = [("post", g, 2) for g in range(GROUPS)]
            if inv:
                setup += [("rows", n, 2) for n in range(NORM_AT)]
            if post:
                setup += [("norm", 0, 0)]
            if inv:
                setup += [("rows", n, 2) for n in range(NORM_AT, 12)]
                for lv in range(LEVELS):
                    for g in range(GROUPS):
                        levels += [("E", (lv, g), 1)] + [("X", (lv - 1, g), 1)] * (lv > 0)
                    levels += [("W", (lv, g), 1) for g in range(GROUPS)]
                levels += [("X", (LEVELS - 1, g), 1) for g in range(GROUPS)]
            if scan:
                ending = [(name, g, 1 if name == "V" else 3) for name in "FVMA" for g in range(GROUPS)]
                walk = [("walk", divmod(n, 2), 3) for n in range(2 * NC)]
            return merged(ending, setup) + merged(walk, norm + levels)

        def pe_pass(pe, i, par_, inv, scan, post):
            p = i - 1
            pw = 1 - par_

            def walk(c, part):
                v = tokens_of[:, pw, 2, c, :]
                if part == 0:
                    if c == 0:
                        wait_scan(pe, p, pw)
                        pe.wait_ge(q["a_rows"], GROUPS * i)
                    mm = pe.matmul(chunk_bank[:, 0:P], w_inv[:, c, :], mv[:, c, :], start=True, stop=c == 0)
                    if c > 0:
                        pe.wait_ge(q["s_rows"], 9 * p + c)
                        mm = pe.matmul(chunk_bank[:, 0:P], a_hat[:, c, :], state[:], start=False, stop=True)
                    mm.then_inc(q["u_mm"], 1)
                    pe.matmul(state_bank[:, 0:P], tokens_of[:, pw, 1, c, :], v, start=True, stop=False)
                    if c > 0:
                        pe.wait_ge(q["y_rows"], 9 * p + c)
                        pe.matmul(y_bank[:, 0:P], b_r[:, pw, c, :], state[:], start=True, stop=False)
                    pe.matmul(y_bank[:, 0:P], mg[:, pw, c, 1, :], v, start=c == 0, stop=False)
                else:
                    pe.wait_ge(q["u_rows"], 9 * p + c + 1)
                    pe.matmul(state_bank[:, 0:P], tokens_of[:, pw, 0, c, :], u_row[:], start=False, stop=True).then_inc(q["s_mm"], 1)
                    pe.matmul(y_bank[:, 0:P], qg[:, pw, c, 1, :], u_row[:], start=False, stop=True).then_inc(q["y_mm"], 1)

            def group(out, lhsT, rhs, g, done):
                for c in range(GC):
                    mm = pe.matmul(out[:, c * P:(c + 1) * P], lhsT(g * GC + c), rhs(g * GC + c), start=True, stop=True)
                mm.then_inc(done, 1)

            def turn(out, src, done):
                for c in range(GC):
                    mm = pe.transpose(out[:, c * P:(c + 1) * P], src(c), ident)
                mm.then_inc(done, 1)

            for item, arg in schedule(inv, scan, post):
                if item == "walk":
                    walk(*arg)
                elif item == "G":
                    if arg == 0:
                        pe.wait_ge(q["forms_loaded"], FORMS_DMAS * i + FORMS_DMAS)
                        if not is0(i):
                            pe.wait_ge(q["w_added"], 15 * i)
                    group(inv_bank[arg], lambda c: b_b[:, c, :], lambda c: b_ar[:, c], arg, q["g_mm"])
                elif item == "K":
                    if arg == 0 and not is0(i):
                        pe.wait_ge(q["x_rows"], 15 * i)
                    if arg == 2:
                        pe.wait_ge(q["mg_made"], GROUPS * i + 1)
                    group(odd_bank[arg % 2], lambda c: b_k[:, c, :], lambda c: b_ar[:, c], arg, q["k_mm"])
                elif item == "T":
                    pe.wait_ge(q["qg_made"], GROUPS * i + arg + 1)
                    turn(inv_bank[arg], lambda c: qg[:, par_, arg * GC + c, 0, :], q["n_turned"])
                elif item == "rows":
                    src = (b_b, b_k, b_v, b_a)[arg // 3]
                    if arg < 2:
                        pe.wait_ge(q["mg_made"], GROUPS * i + arg + 2)
                    else:
                        pe.wait_ge(q["token_rows"], 12 * i + arg - 1)
                    turn(odd_bank[(arg + 1) % 2], lambda c: src[:, arg % 3 * GC + c, :], q["token_mm"])
                elif item == "post":
                    if inv and arg == 0:
                        pe.wait_ge(q["token_rows"], 12 * i + 12)
                    pe.wait_ge(q["post"], POST * (i - 2) + 9 + 2 * arg)
                    turn(post_bank, lambda c: y_diag[:, arg * GC + c, :], q["y_turned"])
                elif item == "E":
                    lv, g = arg
                    if lv == 0:
                        pe.wait_ge(q["n_rows"], GROUPS * i + g + 1)
                        pe.wait_ge(q["w_start"], 6 * i + 2 * g + 2)
                    else:
                        pe.wait_ge(q["w_added"], 15 * i + 3 * (lv - 1) + g + 1)
                    pe.wait_ge(q["n_level"], 15 * i + 3 * lv + g + 1)
                    group(inv_bank[g], lambda c: n_lvl[:, lv % LEVEL_BUFS, c, :], lambda c: w_rnd[:, c, :], g, q["e_mm"])
                elif item == "W":
                    lv, g = arg
                    pe.wait_ge(q["e_rows"], 15 * i + 3 * lv + g + 1)
                    if lv == 0:
                        pe.wait_ge(q["x_start"], 6 * i + 2 * g + 2)
                    else:
                        pe.wait_ge(q["x_rows"], 15 * i + 3 * (lv - 1) + g + 1)
                    group(inv_bank[g], lambda c: x_rnd[:, c, :], lambda c: e_rnd[:, c, :], g, q["w_mm"])
                elif item == "X":
                    lv, g = arg
                    if lv == 0 and g == 0:
                        pe.wait_ge(q["token_rows"], 12 * i + 12)
                    if lv == 0 and g == 1 and post:
                        pe.wait_ge(q["post"], POST * (i - 2) + 15)
                    if g == 2:
                        pe.wait_ge(q["x_rows"], 15 * i + 3 * lv + 1)
                    pe.wait_ge(q["w_added"], 15 * i + 3 * lv + g + 1)
                    turn(odd_bank[g % 2], lambda c: w_rnd[:, g * GC + c, :].bitcast(F32), q["x_mm"])
                elif item == "F":
                    pe.wait_ge(q["w_added"], 15 * p + 12 + arg + 1)
                    if arg == 0 and not is0(p):
                        pe.wait_ge(q["u_rows"], 9 * p)
                        pe.wait_ge(q["s_rows"], 9 * p)
                        pe.wait_ge(q["y_rows"], 9 * p)
                    group(end_bank[arg], lambda c: n_all[:, c, :], lambda c: w_rnd[:, c, :].bitcast(F32), arg, q["f_mm"])
                elif item == "V":
                    pe.wait_ge(q["lack"], GROUPS * p + arg + 1)
                    pe.wait_ge(q["x_rows"], 15 * p + 12 + arg + 1)
                    group(end_bank[arg], lambda c: x_rnd[:, c, :], lambda c: e_rnd[:, c, :], arg, q["v_mm"])
                elif item == "M":
                    pe.wait_ge(q["w_done"], GROUPS * p + arg + 1)
                    pe.wait_ge(q["mg_made"], GROUPS * p + arg + 1)
                    pe.wait_ge(q["token_rows"], 12 * p + 12)
                    group(end_bank[arg], lambda c: mg[:, pw, c, 0, :], lambda c: tokens_of[:, pw, 2, c, :], arg, q["m_mm"])
                elif item == "A":
                    pe.wait_ge(q["m_rows"], GROUPS * p + arg + 1)
                    group(end_bank[arg], lambda c: tokens_of[:, pw, 3, c, :], lambda c: w_inv[:, c, :], arg, q["a_mm"])

        def act_pass(act, i, par_, inv, scan, post):
            p = i - 1

            def walk(c, part):
                if part == 0:
                    act.wait_ge(q["u_mm"], 9 * p + c + 1)
                    act.activation(u_row[:], chunk_bank[:, 0:P], ACT.Copy).then_inc(q["u_rows"], 1)
                else:
                    act.wait_ge(q["y_mm"], 9 * p + c + 1)
                    if c == 0 and not is0(p):
                        act.wait_ge(q["post"], POST * (p - 1) + 3)
                    for hd, rows in enumerate(HEAD_ROWS):
                        ins = act.activation(y_rows[rows, c, :], y_bank[rows, hd * C:(hd + 1) * C], ACT.Copy)
                    ins.then_inc(q["y_rows"], 1)

            for item, arg in schedule(inv, scan, post):
                if item == "walk":
                    walk(*arg)
                elif item == "T":
                    if arg == 0 and not is0(i):
                        act.wait_ge(q["n_level"], 15 * i)
                        act.wait_ge(q["f_mm"], GROUPS * i)
                    act.wait_ge(q["n_turned"], GROUPS * i + arg + 1)
                    act.activation(n_all[:, grp(arg), :], three(inv_bank[arg]), ACT.Copy).then_inc(q["n_rows"], 1)
                elif item == "rows":
                    act.wait_ge(q["token_mm"], 12 * i + arg + 1)
                    act.activation(tokens_of[:, par_, arg // 3, grp(arg % 3), :], three(odd_bank[(arg + 1) % 2]), ACT.Copy).then_inc(q["token_rows"], 1)
                elif item == "norm":
                    act.wait_ge(q["post"], POST * (i - 2) + 6)
                    act.activation(y_var[:], y_var[:], ACT.Sqrt, bias=epsilon[:, 1:2], scale=1.0 / C).then_inc(q["y_rooted"], 1)
                elif item == "E":
                    lv, g = arg
                    act.wait_ge(q["e_mm"], 15 * i + 3 * lv + g + 1)
                    act.activation(e_rnd[:, grp(g), :], three(inv_bank[g]), ACT.Copy).then_inc(q["e_rows"], 1)
                elif item == "X":
                    lv, g = arg
                    act.wait_ge(q["x_mm"], 15 * i + 3 * lv + g + 1)
                    act.activation(x_rnd[:, grp(g), :], three(odd_bank[g % 2]), ACT.Copy).then_inc(q["x_rows"], 1)
                elif item == "M":
                    act.wait_ge(q["m_mm"], GROUPS * p + arg + 1)
                    act.activation(mv[:, grp(arg), :], three(end_bank[arg]), ACT.Copy).then_inc(q["m_rows"], 1)
                elif item == "A":
                    act.wait_ge(q["a_mm"], GROUPS * p + arg + 1)
                    act.activation(a_hat[:, grp(arg), :], three(end_bank[arg]), ACT.Copy).then_inc(q["a_rows"], 1)

        def dve_pass(dve, i, par_, inv, scan, post):
            p = i - 1
            pw = 1 - par_

            def walk(c, part):
                if part == 1:
                    if c == 0:
                        wait_scan(dve, p, pw)
                    dve.wait_ge(q["s_mm"], 9 * p + c + 1)
                    decay = b_pc[:, pw, c:c + 1]
                    if c == 0:
                        dve.tensor_scalar(state[:], state_bank[:, 0:P], decay, None, ALU.mult).then_inc(q["s_rows"], 1)
                    else:
                        dve.wait_ge(q["z_sum"], 8 * p + c)
                        dve.scalar_tensor_tensor(state[:], state_bank[:, 0:P], decay, state_p[:], ALU.mult, ALU.add).then_inc(q["s_rows"], 1)
                    if c < NC - 1:
                        dve.wait_ge(q["s_rows"], 9 * p + c + 1)
                        dve.tensor_scalar(state_p[:], state[:], b_pc[:, pw, c + 1:c + 2], None, ALU.mult).then_inc(q["z_sum"], 1)

            def masked(src, dst, g, made):
                for hd, rows in enumerate(HEAD_ROWS):
                    ins = dve.tensor_tensor(dst[rows, par_, grp(g), :, hd * C:(hd + 1) * C],
                                            src[rows, 0:GC * P].rearrange("p (c s n) -> p c s n", c=GC, s=2),
                                            tri[rows].unsqueeze(1).to_broadcast([C, GC, 2, C]), ALU.mult)
                ins.then_inc(made, 1)

            for item, arg in schedule(inv, scan, post):
                if item == "walk":
                    walk(*arg)
                elif item == "G":
                    dve.wait_ge(q["g_mm"], GROUPS * i + arg + 1)
                    masked(inv_bank[arg], qg, arg, q["qg_made"])
                elif item == "K":
                    dve.wait_ge(q["k_mm"], GROUPS * i + arg + 1)
                    masked(odd_bank[arg % 2], mg, arg, q["mg_made"])
                elif item == "stats":
                    dve_stats(dve, i - 2)
                elif item in ("norm", "post"):
                    dve_post(dve, i - 2, par_, item, arg)
                elif item == "W":
                    lv, g = arg
                    dve.wait_ge(q["w_mm"], 15 * i + 3 * lv + g + 1)
                    w = w_rnd[:, grp(g), :]
                    dve.tensor_tensor(w, three(inv_bank[g]), w.bitcast(F32), ALU.add).then_inc(q["w_added"], 1)
                elif item == "start":
                    if arg == 0 and is0(i):
                        dve.wait_ge(con_loaded, 48)
                    elif arg == 0:
                        dve.wait_ge(q["w_done"], GROUPS * i)
                    dve.wait_ge(q["qg_made"], GROUPS * i + arg + 1)
                    w = w_rnd[:, grp(arg), :]
                    dve.tensor_tensor(w, qg[:, par_, grp(arg), 0, :], mask("level0T"), ALU.mult).then_inc(q["w_start"], 1)
                    dve.wait_ge(q["w_start"], 6 * i + 2 * arg + 1)
                    dve.tensor_tensor(w, w.bitcast(F32), eye, ALU.add).then_inc(q["w_start"], 1)
                elif item == "F":
                    dve.wait_ge(q["f_mm"], GROUPS * p + arg + 1)
                    dve.wait_ge(q["i_less_w"], GROUPS * p + arg + 1)
                    dve.tensor_tensor(e_rnd[:, grp(arg), :], three(end_bank[arg]), i_less_w[:, grp(arg), :], ALU.add).then_inc(q["lack"], 1)
                elif item == "V":
                    dve.wait_ge(q["v_mm"], GROUPS * p + arg + 1)
                    dve.tensor_tensor(w_inv[:, grp(arg), :], three(end_bank[arg]), w_rnd[:, grp(arg), :].bitcast(F32), ALU.add).then_inc(q["w_done"], 1)

        def dve_stats(dve, p):
            def step(ins):
                ins.then_inc(q["post"], 1)

            def after(k):
                dve.wait_ge(q["post"], POST * p + k)

            dve.wait_ge(q["y_rows"], 9 * p + 9)
            step(dve.tensor_reduce(y_sum[:], y_rows[:], AX_X, ALU.add))
            after(1)
            step(dve.tensor_scalar(y_mean[:], y_sum[:], 1.0 / C, None, ALU.mult))
            after(2)
            step(dve.tensor_tensor(y_sq[:], y_rows[:], y_mean[:].unsqueeze(2).to_broadcast([P, NC, C]), ALU.subtract))
            after(3)
            step(dve.tensor_tensor(y_ln[:], y_sq[:], y_sq[:], ALU.mult))
            after(4)
            step(dve.tensor_reduce(y_sum[:], y_ln[:], AX_X, ALU.add))
            after(5)
            step(dve.tensor_copy(y_var[:], y_sum[:]))

        def dve_post(dve, p, pp, item, g):
            def step(ins):
                ins.then_inc(q["post"], 1)

            def after(k):
                dve.wait_ge(q["post"], POST * p + k)

            if item == "norm":
                dve.wait_ge(q["y_rooted"], p + 1)
                step(dve.reciprocal(y_mean[:], y_var[:]))
                after(7)
                for hd, rows in enumerate(HEAD_ROWS):
                    step(dve.tensor_tensor(y_diag[rows, :, hd * C:(hd + 1) * C], y_sq[rows],
                                           y_mean[rows].unsqueeze(2).to_broadcast([C, NC, C]), ALU.mult))
                return
            dve.wait_ge(q["y_turned"], GROUPS * p + g + 1)
            for hd, rows in enumerate(HEAD_ROWS):
                step(dve.tensor_scalar(y_ln[rows, grp(g), :], three(post_bank)[rows, :, hd * C:(hd + 1) * C],
                                       rw(LNW, p)[rows], rw(LNB, p)[rows], ALU.mult, ALU.add))
            if g < GROUPS - 1:
                return
            after(15)
            gate, bonus = b_sgbon[:, pp, 0, PAD:], b_sgbon[:, pp, 1, PAD:]
            y = y_ln[:].rearrange("p c n -> p (c n)")[:, PAD:]
            wait_scan(dve, p, pp)
            dve.tensor_tensor(bonus, y, bonus, ALU.add).then_inc(q["diag_set"], 1)
            dve.wait_ge(q["diag_set"], N_DIAG + p + 1)
            dve.scalar_tensor_tensor(gate, bonus, 0.5, gate, ALU.mult, ALU.mult).then_inc(q["z_made"], 1)

        def pool_pass(pool, i, par_, inv, scan, post):
            if not inv:
                return
            if is0(i):
                pool.wait_ge(con_loaded, 48)
            else:
                pool.wait_ge(q["v_mm"], GROUPS * i)
            for g in range(GROUPS):
                pool.wait_ge(q["n_rows"], GROUPS * i + g + 1)
                pool.tensor_tensor(n_lvl[:, 0, grp(g), :], n_all[:, grp(g), :], mask("levels", 1), ALU.mult).then_inc(q["n_level"], 1)
                x = x_rnd[:, grp(g), :]
                pool.tensor_tensor(x, n_all[:, grp(g), :], mask("levels", 0), ALU.mult).then_inc(q["x_start"], 1)
                pool.wait_ge(q["x_start"], 6 * i + 2 * g + 1)
                pool.tensor_tensor(x, x.bitcast(F32), eye, ALU.add).then_inc(q["x_start"], 1)
            for lv in range(1, LEVELS):
                for g in range(GROUPS):
                    if lv >= LEVEL_BUFS:
                        pool.wait_ge(q["e_mm"], 15 * i + 3 * (lv - LEVEL_BUFS) + g + 1)
                    pool.tensor_tensor(n_lvl[:, lv % LEVEL_BUFS, grp(g), :], n_all[:, grp(g), :], mask("levels", lv + 1), ALU.mult).then_inc(q["n_level"], 1)
            for g in range(GROUPS):
                pool.wait_ge(q["w_added"], 15 * i + 12 + g + 1)
                pool.tensor_tensor(i_less_w[:, grp(g), :], eye, w_rnd[:, grp(g), :].bitcast(F32), ALU.subtract).then_inc(q["i_less_w"], 1)

        def dve_b_setup(dve):
            dve.wait_ge(s["stored"], 16 * PAIRS)
            for t in (b_b, b_k, b_v, b_a, b_r, qg, mg, y_diag):
                dve.memset(t[:], 0.0).then_inc(q["diag_set"], 1)
            dve.wait_ge(q["diag_set"], N_DIAG)
            dve.wait_ge(con_loaded, 48)

        def passes(eng, body):
            body(eng, 0, 0, True, False, False)
            body(eng, 1, 1, True, True, False)
            with eng.Fori(1, PAIRS // 2) as j:
                body(eng, 2 * j, 0, True, True, True)
                body(eng, 2 * j + 1, 1, True, True, True)
            body(eng, PAIRS, 0, False, True, True)
            body(eng, PAIRS + 1, 1, False, False, True)

        def sp_b(sp):
            sp.wait_ge(phase_done, 4)
            sp.wait_ge(s["stored"], 16 * PAIRS)
            first, n = CON_OF["rwkv"]
            sp.dma_start(b_con[:], con_in[:, first:first + n]).then_inc(con_loaded, 16)
            sp.wait_ge(q["diag_set"], N_DIAG)
            sp_b_pair(sp, 0, 0, False)
            sp_b_pair(sp, 1, 1, False)
            with sp.Fori(1, PAIRS // 2) as j:
                sp_b_pair(sp, 2 * j, 0, True)
                sp_b_pair(sp, 2 * j + 1, 1, True)
            sp_z(sp, PAIRS - 2, 0)
            sp_z(sp, PAIRS - 1, 1)

        h = sb("h", KD, L)
        m_t = sb("mixer_out", KD, L)
        u2 = sb("normed", KD, L)
        sq = sb("squares", 2, L)
        sq_sum = sb("sq_sum", L)
        tile_left, sq_made, sq_added = (sem(n) for n in ("tile_left", "sq_made", "sq_added"))
        n_summed, n_rooted, n_inverted, n_used = (sem(n) for n in ("n_summed", "n_rooted", "n_inverted", "n_used"))
        h_added = sem("h_added")

        class Seen:
            def __init__(self):
                self.left = self.squares = self.added = self.norms = self.h = 0

        seen = {who: Seen() for who in ("pe", "act", "dve")}

        def tokens(ap, width):
            return ap if width == L else ap[:, META:]

        def tile_ps(t, width):
            return wide[t][:, :, 0:HALF] if width == L else wide[t][:, 0, 0:width]

        def over_tiles(eng, count, per_turn, body):
            with eng.Fori(0, count // per_turn) as j:
                for t in range(per_turn):
                    body(j, t, per_turn * j + t)

        def pe_tiles(pe, load, count, kt, rhs, width, loop=True, after=None):
            st, per = seen["pe"], kt // KD
            turn = SLOTS // per

            def tile(j, t, n):
                pe.wait_ge(tile_left, st.left + n + 1)
                for k in range(kt):
                    if k % KD == 0:
                        ring.wait_full(pe, load + per * t + k // KD, j)
                for b in range(2 if width == L else 1):
                    for k in range(kt):
                        at = load + per * t + k // KD
                        mm = pe.matmul(wide[t][:, b, 0:HALF if width == L else width],
                                       ring.slot(at)[:, k % KD * P:(k % KD + 1) * P], rhs(k, b), start=k == 0, stop=k == kt - 1)
                        if k % KD == KD - 1 and b == (1 if width == L else 0):
                            mm.then_inc(ring.done(at), 1)
                if after:
                    after(n, t)

            if loop:
                over_tiles(pe, count, turn, tile)
            else:
                for n in range(count):
                    tile(n // turn, n % turn, n)
            st.left += count + turn

        def act_tiles(act, load, count, kt, take, loop=True, before=None):
            st, per = seen["act"], kt // KD
            turn = SLOTS // per
            act.drain().then_inc(tile_left, turn)

            def tile(j, t, n):
                if before:
                    before(n, t)
                ring.wait_used(act, load + per * t + per - 1, j)
                take(j, t, n)

            if loop:
                over_tiles(act, count, turn, tile)
            else:
                for n in range(count):
                    tile(n // turn, n % turn, n)
            st.left += count + turn

        def act_square(act, src, slot, n, width):
            st = seen["act"]
            act.wait_ge(sq_added, st.added + n + 1)
            return act.activation(halves(sq[:, slot, 0:width], width) if len(src.shape) == 3 else sq[:, slot, 0:width], src, ACT.Square).then_inc(sq_made, 1)

        def act_root(act, tiles, width):
            st = seen["act"]
            st.norms += 1
            st.squares += tiles
            st.added += tiles + 2
            act.wait_ge(n_summed, st.norms)
            if st.norms > 1:
                act.wait_ge(n_used, st.norms - 1)
            act.activation(halves(inv_rms[:, 0:width], width), tile_ps(3, width), ACT.Sqrt,
                           bias=epsilon[:, 0:1], scale=1.0 / (tiles * P)).then_inc(n_rooted, 1)

        def pe_norm_sum(pe, tiles, width):
            st = seen["pe"]
            st.norms += 1
            st.added += tiles + 2
            pe.wait_ge(sq_added, st.added)
            if st.norms > 1:
                pe.wait_ge(n_rooted, st.norms - 1)
            for b in range(2 if width == L else 1):
                n = HALF if width == L else width
                mm = pe.matmul(wide[3][:, b, 0:n], ones, sq_sum[:, b * n:(b + 1) * n], start=True, stop=True)
            mm.then_inc(n_summed, 1)

        def dve_sum_start(dve, width):
            st = seen["dve"]
            if st.norms:
                dve.wait_ge(n_summed, st.norms)
            dve.memset(sq_sum[:, 0:width], 0.0).then_inc(sq_added, 2)

        def dve_sum(dve, slot, n, width):
            st = seen["dve"]
            dve.wait_ge(sq_made, st.squares + n + 1)
            dve.wait_ge(sq_added, st.added + n + 2)
            dve.tensor_tensor(sq_sum[:, 0:width], sq_sum[:, 0:width], sq[:, slot, 0:width], ALU.add).then_inc(sq_added, 1)

        def dve_invert(dve, tiles, width):
            st = seen["dve"]
            st.norms += 1
            st.squares += tiles
            st.added += tiles + 2
            dve.wait_ge(n_rooted, st.norms)
            dve.reciprocal(inv_rms[:, 0:width], inv_rms[:, 0:width]).then_inc(n_inverted, 1)
            dve.wait_ge(n_inverted, st.norms)

        def dve_apply(dve, tiles, width, src, dst, gain):
            for k in range(tiles):
                ins = dve.scalar_tensor_tensor(dst(k), src(k), pcol(gain, k), inv_rms[:, 0:width], ALU.mult, ALU.mult)
            ins.then_inc(n_used, 1)

        def h_of(k, width):
            return tokens(h[:, k, :], width)

        def pe_project_out(pe, load, kt, src, width, post):
            pe_tiles(pe, load, KD, kt, src, width)
            if post:
                pe_norm_sum(pe, KD, width)
            pe_norm_sum(pe, KD, width if not post else post)

        def act_project_out(act, load, kt, width, post):
            st = seen["act"]
            turn = SLOTS * KD // kt

            def take(j, t, n):
                dst = m_t[:].rearrange("p k n -> p (k n)")[:, bass.ds(n * L, width)]
                if post:
                    act_square(act, tile_ps(t, width), t % 2, n, width)
                    act.activation(halves(dst, width), tile_ps(t, width), ACT.Copy).then_inc(tile_left, 1)
                else:
                    act.activation(dst, tile_ps(t, width), ACT.Copy).then_inc(tile_left, 1)
                    act.wait_ge(h_added, st.h + n + 1)
                    act_square(act, h[:].rearrange("p k n -> p (k n)")[:, bass.ds(n * L + META, width)], t % 2, n, width)
            act_tiles(act, load, KD, kt, take)
            if post:
                act_root(act, KD, width)
                for k in range(KD):
                    act.wait_ge(h_added, st.h + 2 * k + 2)
                    act_square(act, h_of(k, post), k % 2, k, post)
                st.h += KD
            st.h += KD
            act_root(act, KD, post if post else width)

        def dve_project_out(dve, kt, width, post, post_gain, gain, dst):
            st = seen["dve"]
            turn = SLOTS * KD // kt
            dve_sum_start(dve, width)

            def take(j, t, n):
                if not post:
                    dve.wait_ge(tile_left, st.left + turn + n + 1)
                    hn = h[:].rearrange("p k n -> p (k n)")[:, bass.ds(n * L + META, width)]
                    mn = m_t[:].rearrange("p k n -> p (k n)")[:, bass.ds(n * L, width)]
                    dve.tensor_tensor(hn, hn, mn, ALU.add).then_inc(h_added, 1)
                dve_sum(dve, t % 2, n, width)
            over_tiles(dve, KD, turn, take)
            st.left += KD + turn
            if post:
                dve_invert(dve, KD, width)
                dve_sum_start(dve, post)
                for k in range(KD):
                    dve.scalar_tensor_tensor(m_t[:, k, :], m_t[:, k, :], pcol(post_gain, k), inv_rms[:], ALU.mult, ALU.mult).then_inc(h_added, 1)
                    dve.wait_ge(h_added, st.h + 2 * k + 1)
                    ins = dve.tensor_tensor(h[:, k, :], h[:, k, :], m_t[:, k, :], ALU.add).then_inc(h_added, 1)
                    if k:
                        dve_sum(dve, (k - 1) % 2, k - 1, post)
                dve.drain().then_inc(n_used, 1)
                dve_sum(dve, (KD - 1) % 2, KD - 1, post)
                st.h += KD
            st.h += KD
            last = post if post else width
            dve_invert(dve, KD, last)
            dve_apply(dve, KD, last, lambda k: h_of(k, last), dst, gain)

        M = ExitStack()

        def sm(name, *shape):
            return M.enter_context(nc.sbuf_tensor(name, [P, *shape], F32))

        z_t = sm("gated", KI, L)
        latents = sm("latents", Q_TILES + KV_TILES, L)
        k_rope = sm("k_rope", L)
        Q_EDGES = [0] + list(range(META, L + 1, P))
        Q_BLOCKS = len(Q_EDGES) - 1
        v_rows = sm("v_rows", Q_BLOCKS, DI)
        m_con = sm("mla_tables", CON_OF["mla"][1])
        P_AT = [sum(Q_EDGES[1:t + 1]) for t in range(Q_BLOCKS + 1)]
        probs = sm("probs", P_AT[-1])
        probs_t = sm("probs_turned", Q_BLOCKS, L)
        v_now = sm("v_now", 2, Q_BLOCKS, P)
        row_max, row_bias, row_sum = (sm(n, Q_BLOCKS) for n in ("row_max", "row_bias", "row_sum"))
        M.close()
        tanh_gate = [m_t[:, t, :] for t in range(SLOTS)]
        k_rope_raw, rope_cos = m_t[:, SLOTS, :], m_t[:, SLOTS + 1, :]
        q_nope, k_nope, q_rope, q_rope_raw = (u2[:, k, :] for k in range(4))

        def mcon(name, width):
            at = CON[name] - CON_OF["mla"][0]
            return m_con[:, at:at + width]

        mixed_loaded, h_loaded = sem("mixed_loaded"), sem("h_loaded")
        d = {n: sem("d_" + n) for n in ("gated", "rope_mm", "rope", "v_mm", "v_copied", "stats_set")}

        def sp_c(sp):
            sp.wait_ge(q["z_stored"], 16 * PAIRS)
            sp.wait_ge(phase_done, 8)
            for i in range(PAIRS):
                sp.dma_start(z_t[:, i, :], mixed[i]).then_inc(mixed_loaded, 16)
            sp.dma_start(h[:], x_in).then_inc(h_loaded, 16)
            first, n = CON_OF["mla"]
            sp.dma_start(m_con[:], con_in[:, first:first + n]).then_inc(con_loaded, 16)

        def half_of(ap):
            return lambda k, b: ap[:, k, b * HALF:(b + 1) * HALF]

        MLA_IN = FIRST["mla_in"]
        MLA_GATE = MLA_IN + Q_TILES + KV_TILES + 1

        def pe_mla_in(pe):
            st = seen["pe"]
            pe.wait_ge(n_used, st.norms)
            pe_tiles(pe, MLA_IN, Q_TILES, KD, half_of(u2), L, loop=False)
            pe.wait_ge(tile_left, st.left)
            pe_norm_sum(pe, Q_TILES, L)
            pe_tiles(pe, MLA_IN + Q_TILES, KV_TILES + 1, KD, half_of(u2), L, loop=False)
            pe.wait_ge(con_loaded, 64)
            pe.wait_ge(tile_left, st.left)
            for b in range(2):
                mm = pe.matmul(wide[2][:, b, 0:HALF], mcon("rot_mla", P), k_rope_raw[:, b * HALF:(b + 1) * HALF], start=True, stop=True)
            mm.then_inc(d["rope_mm"], 1)
            pe_norm_sum(pe, KV_TILES, L)
            pe.wait_ge(d["rope"], 2)
            pe_tiles(pe, MLA_GATE, KI, KD, half_of(u2), L)
            pe.wait_ge(tile_left, st.left)
            pe.wait_ge(n_used, st.norms)
            n = 0
            for c in range(4):
                load = FIRST["mla_v"] + c
                ring.wait_full(pe, load)
                for t in range(Q_BLOCKS):
                    rows = Q_EDGES[t + 1] - Q_EDGES[t]
                    if n >= 8:
                        pe.wait_ge(d["v_copied"], n - 7)
                    for k in range(KV_TILES):
                        mm = pe.matmul(wide[n // 2 % 4][0:rows, n % 2, :], latents[:, Q_TILES + k, Q_EDGES[t]:Q_EDGES[t + 1]],
                                       ring.slot(load)[:, k * 512:(k + 1) * 512], start=k == 0, stop=k == KV_TILES - 1)
                    mm.then_inc(d["v_mm"], 1)
                    n += 1
                pe.drain().then_inc(ring.done(load), 1)

        def act_mla_in(act):
            st = seen["act"]
            flat = z_t[:].rearrange("p k n -> p (k n)")

            def latent(first):
                def take(j, t, n):
                    if first + n < Q_TILES + KV_TILES:
                        act_square(act, tile_ps(t, L), n % 2, n, L)
                        dst = latents[:, first + n, :]
                    else:
                        dst = k_rope_raw
                    act.activation(halves(dst, L), tile_ps(t, L), ACT.Copy).then_inc(tile_left, 1)
                return take
            act_tiles(act, MLA_IN, Q_TILES, KD, latent(0), loop=False)
            act_root(act, Q_TILES, L)
            act_tiles(act, MLA_IN + Q_TILES, KV_TILES + 1, KD, latent(Q_TILES), loop=False)
            act_root(act, KV_TILES, L)

            def gate(j, t, n):
                act.wait_ge(d["gated"], n + 1)
                act.activation(halves(tanh_gate[t], L), tile_ps(t, L), ACT.Tanh, scale=0.5)
                act.activation(halves(flat[:, bass.ds(n * L, L)], L), tile_ps(t, L), ACT.Copy).then_inc(tile_left, 1)
            act_tiles(act, MLA_GATE, KI, KD, gate)
            n = 0
            for c in range(4):
                for t in range(Q_BLOCKS):
                    rows = Q_EDGES[t + 1] - Q_EDGES[t]
                    act.wait_ge(d["v_mm"], n + 1)
                    act.activation(v_rows[0:rows, t, c * 512:(c + 1) * 512], wide[n // 2 % 4][0:rows, n % 2, :], ACT.Copy).then_inc(d["v_copied"], 1)
                    n += 1

        def dve_mla_in(dve):
            st = seen["dve"]
            flat = z_t[:].rearrange("p k n -> p (k n)")
            for t in (row_max, row_bias, row_sum):
                dve.memset(t[:], 1.0).then_inc(d["stats_set"], 1)
            dve_sum_start(dve, L)
            for n in range(Q_TILES):
                dve_sum(dve, n % 2, n, L)
            dve_invert(dve, Q_TILES, L)
            dve_sum_start(dve, L)
            st.left += Q_TILES + SLOTS
            dve.wait_ge(tile_left, st.left)
            dve_apply(dve, Q_TILES, L, lambda k: latents[:, k, :], lambda k: latents[:, k, :], "q_norm")
            for n in range(KV_TILES):
                dve_sum(dve, n % 2, n, L)
            st.left += KV_TILES + 1 + SLOTS
            dve.wait_ge(con_loaded, 64)
            dve.wait_ge(tile_left, st.left)
            dve.tensor_tensor(k_rope[:], k_rope_raw, mcon("cos_mla", L), ALU.mult).then_inc(d["rope"], 1)
            dve.wait_ge(d["rope_mm"], 1)
            dve.tensor_tensor(halves(rope_cos, L), wide[2][:, :, 0:HALF], halves(mcon("sin_mla", L), L), ALU.mult).then_inc(d["rope"], 1)
            dve.wait_ge(d["rope"], 2)
            dve.tensor_tensor(k_rope[:], k_rope[:], rope_cos, ALU.add).then_inc(d["rope"], 1)
            dve_invert(dve, KV_TILES, L)
            dve_apply(dve, KV_TILES, L, lambda k: latents[:, Q_TILES + k, :], lambda k: latents[:, Q_TILES + k, :], "kv_norm")
            dve.drain().then_inc(d["gated"], SLOTS)

            def gate(j, t, n):
                dve.wait_ge(tile_left, st.left + SLOTS + n + 1)
                at = flat[:, bass.ds(n * L, L)]
                dve.scalar_tensor_tensor(at, tanh_gate[t], 1.0, at, ALU.add, ALU.mult).then_inc(d["gated"], 1)
            over_tiles(dve, KI, SLOTS, gate)
            st.left += KI + SLOTS

        MLA_SCALE = (P + KROPE) ** -0.5
        UP = FIRST["mla_up"]
        PER_TURN = 4
        e = {n: sem("e_" + n) for n in ("made", "evac", "rope", "scores", "dve", "exp", "turned", "pt", "pv", "v_now", "gated")}
        DVE_E = Count(e["dve"], 19)
        SCORE_OF = [wide[0][:, 0, P_AT[t]:P_AT[t + 1]] for t in range(3)] + [wide[0][:, 1, 0:Q_EDGES[4]], wide[1][:, :, 0:HALF]]
        TURNED = [(0, 0, 4, 0, 0, 0), (0, 4, 5, 0, 1, 1), (2, 2, 5, P, 1, 1), (1, 1, 5, 0, 0, 2), (3, 3, 5, 0, 1, 3), (4, 4, 5, 2 * P, 1, 3)]

        def size(t):
            return Q_EDGES[t + 1] - Q_EDGES[t]

        def p_of(t, lo=0, hi=L):
            return probs[0:size(t), P_AT[t] + lo:P_AT[t] + min(hi, Q_EDGES[t + 1])]

        def of_pair(x):
            return UP + 2 * (x // 2), UP + 2 * (x // 2) + 1

        def head_weights(x):
            q_load, k_load = of_pair(x)
            o = x % 2
            return (ring.slot(q_load)[:, o * 512:(o + 1) * 512], ring.slot(k_load)[:, 512 + o * 256:512 + (o + 1) * 256],
                    ring.slot(k_load)[:, 0:512])

        def pe_up(pe, H, x, j, first=False):
            st = seen["pe"]
            wq, wk, wr = head_weights(x)
            q_load, k_load = of_pair(x)

            def product(dst, w, k0, kt):
                for b in range(2):
                    for k in range(kt):
                        mm = pe.matmul(dst[:, b, 0:HALF], w[:, k * P:(k + 1) * P], latents[:, k0 + k, b * HALF:(b + 1) * HALF],
                                       start=k == 0, stop=k == kt - 1)
                return mm

            if not first:
                pe.wait_ge(e["pt"], 6 * H)
            pair = (PER_TURN * j + x) // 2 if isinstance(j, int) else PER_TURN // 2 * j + x // 2
            if x % 2 == 0:
                ring.wait_full(pe, k_load, j)
                product(wide[2], wr, 0, Q_TILES).then_inc(e["made"], 1)
            if not first:
                pe.wait_ge(e["gated"], 2 * H)
            mm = product(wide[3], wk, Q_TILES, KV_TILES)
            mm.then_inc(e["made"] if x % 2 == 0 else ring.done(k_load), 1)
            if x % 2 == 0:
                ring.wait_full(pe, q_load, j)
                pe.wait_ge(e["evac"], 5 * pair + 1)
            mm = product(wide[2], wq, 0, Q_TILES)
            mm.then_inc(e["made"] if x % 2 == 0 else ring.done(q_load), 1)
            if x % 2 == 0:
                pe.wait_ge(e["evac"], 5 * pair + 2)
                for b in range(2):
                    mm = pe.matmul(wide[3][:, b, 0:HALF], mcon("rot_mla", P), q_rope_raw[:, b * HALF:(b + 1) * HALF], start=True, stop=True)
                mm.then_inc(e["made"], 1)

        def act_up(act, x, j, what):
            q_load, k_load = of_pair(x)
            pair = (PER_TURN * j + x) // 2 if isinstance(j, int) else PER_TURN // 2 * j + x // 2
            if x % 2 == 0:
                act.wait_ge(e["made"], 4 * pair + 1 + what)
            else:
                ring.wait_used(act, k_load if what == 1 else q_load, j)
            dst, src = ((q_rope_raw, wide[2]), (k_nope, wide[3]), (q_nope, wide[2]))[what]
            act.activation(halves(dst, L), src[:, :, 0:HALF], ACT.Copy).then_inc(e["evac"], 1)

        def dve_rope(dve, j, x):
            pair = (PER_TURN * j + x) // 2 if isinstance(j, int) else PER_TURN // 2 * j + x // 2
            dve.wait_ge(e["evac"], 5 * pair + 1)
            dve.tensor_tensor(q_rope, q_rope_raw, mcon("cos_mla", L), ALU.mult).then_inc(e["rope"], 1)
            dve.wait_ge(e["made"], 4 * pair + 4)
            dve.tensor_tensor(halves(rope_cos, L), wide[3][:, :, 0:HALF], halves(mcon("sin_mla", L), L), ALU.mult).then_inc(e["rope"], 1)
            dve.wait_ge(e["rope"], 3 * pair + 2)
            dve.tensor_tensor(q_rope, q_rope, rope_cos, ALU.add).then_inc(e["rope"], 1)

        def pe_head(pe, j, x, last):
            H = PER_TURN * j + x
            ends = last and x == PER_TURN - 1
            pair = (PER_TURN * j + x) // 2 if isinstance(j, int) else PER_TURN // 2 * j + x // 2
            pe.wait_ge(e["evac"], 5 * pair + (3 if x % 2 == 0 else 5))
            pe.wait_ge(e["rope"], 3 * pair + 3)
            rows = HEAD_ROWS[x % 2]
            for t in (4, 3, 0, 1, 2):
                lo, hi = Q_EDGES[t], Q_EDGES[t + 1]
                for b in range(2 if t == 4 else 1):
                    keys = slice(b * HALF, (b + 1) * HALF) if t == 4 else slice(0, hi)
                    dst = SCORE_OF[t][0:size(t), b, :] if t == 4 else SCORE_OF[t][0:size(t)]
                    pe.matmul(dst, q_nope[:, lo:hi], k_nope[:, keys], start=True, stop=False)
                    mm = pe.matmul(dst, q_rope[rows, lo:hi], k_rope[rows, keys], start=False, stop=True)
                if t in (4, 3, 2):
                    mm.then_inc(e["scores"], 1)
            if not ends:
                pe_up(pe, H + 1, (x + 1) % PER_TURN, j + (x + 1) // PER_TURN)
                pair_next = pair + (x % 2)
                pe.wait_ge(e["evac"], 5 * pair_next + (3 if x % 2 else 5))
            else:
                pe.wait_ge(e["pt"], 6 * H + 6)
            for n, (kb, q0, q1, col, bank, piece) in enumerate(TURNED):
                if n == 0:
                    pe.wait_ge(DVE_E.sem, DVE_E.at(H, 19))
                if n == 3:
                    pe.wait_ge(e["pt"], 6 * H + 7)
                if n == 4:
                    pe.wait_ge(e["pt"], 6 * H + 9)
                for t in reversed(range(q0, q1)):
                    at = col + Q_EDGES[t] - Q_EDGES[q0]
                    mm = pe.transpose(wide[2][0:size(kb), bank, at:at + size(t)], p_of(t, Q_EDGES[kb], Q_EDGES[kb + 1]), ident[0:size(t), 0:size(t)])
                if n in (0, 2, 3, 5):
                    mm.then_inc(e["turned"], 1)
            pe.wait_ge(e["v_now"], 2 * H + 2)
            if not ends:
                if x % 2:
                    pe.wait_ge(e["rope"], 3 * pair_next + 2)
            else:
                pe.wait_ge(e["gated"], 2 * H + 2)
            cut = Q_EDGES[3]
            for kb, done in ((0, 2), (2, 3), (1, 4), (3, 5), (4, 6)):
                pe.wait_ge(e["pt"], 6 * H + 6 + done)
                for b, (lo, hi) in enumerate(((0, cut), (cut, L))):
                    seen_from = max(lo, Q_EDGES[kb])
                    if seen_from < hi:
                        mm = pe.matmul(wide[3][:, b, seen_from - lo:hi - lo], v_now[0:size(kb), x % 2, kb, :],
                                       probs_t[0:size(kb), kb, seen_from:hi], start=kb == 0, stop=kb == (1, 4)[b])
            mm.then_inc(e["pv"], 1)

        def act_head(act, j, x, last):
            H = PER_TURN * j + x
            ends = last and x == PER_TURN - 1
            nx, nj = (x + 1) % PER_TURN, j + (x + 1) // PER_TURN

            def soften(t, step):
                act.wait_ge(DVE_E.sem, DVE_E.at(H, step))
                act.activation(halves(p_of(t), L) if t == 4 else p_of(t), SCORE_OF[t][0:size(t)], ACT.Exp, bias=row_bias[0:size(t), t:t + 1],
                               scale=MLA_SCALE, accum_out=row_sum[0:size(t), t:t + 1]).then_inc(e["exp"], 1)

            soften(4, 5)
            soften(3, 5)
            if not ends and nx % 2 == 0:
                act_up(act, nx, nj, 0)
            for t in (2, 1, 0):
                soften(t, 12)
            if not ends:
                act_up(act, nx, nj, 1)
                act_up(act, nx, nj, 2)
            for n, (kb, q0, q1, col, bank, piece) in enumerate(TURNED):
                act.wait_ge(e["turned"], 4 * H + piece + 1)
                if n == 0:
                    act.wait_ge(e["pv"], H + 1)
                lo, hi = Q_EDGES[q0], Q_EDGES[q1]
                act.activation(probs_t[0:size(kb), kb, lo:hi], wide[2][0:size(kb), bank, col:col + hi - lo], ACT.Copy).then_inc(e["pt"], 1)

        def dve_head(dve, j, x, last):
            H = PER_TURN * j + x
            ends = last and x == PER_TURN - 1

            def step(ins):
                ins.then_inc(DVE_E.sem, 1)

            def after(k):
                dve.wait_ge(DVE_E.sem, DVE_E.at(H, k))

            def maxima(t, k):
                n = size(t)
                diag = SCORE_OF[t][:, 1, HALF - n:HALF] if t == 4 else SCORE_OF[t][0:n, Q_EDGES[t]:Q_EDGES[t + 1]]
                step(dve.tensor_tensor(diag, diag, mcon("causal", P)[0:n, 0:n], ALU.add))
                after(k)
                step(dve.tensor_reduce(row_max[0:n, t:t + 1], SCORE_OF[t][0:n], mybir.AxisListType.XY if t == 4 else AX_X, ALU.max))

            def bias(ts):
                step(dve.tensor_scalar(row_bias[:, ts], row_max[:, ts], -MLA_SCALE, None, ALU.mult))

            def share(t):
                n = size(t)
                step(dve.tensor_scalar(p_of(t), p_of(t), row_sum[0:n, t:t + 1], None, ALU.mult))

            dve.wait_ge(e["scores"], 3 * H + 1)
            maxima(4, 1)
            dve.wait_ge(e["scores"], 3 * H + 2)
            maxima(3, 3)
            after(4)
            bias(slice(3, 5))
            dve.wait_ge(e["scores"], 3 * H + 3)
            maxima(2, 6)
            maxima(1, 8)
            maxima(0, 10)
            after(11)
            bias(slice(0, 3))
            dve.wait_ge(e["exp"], Q_BLOCKS * H + 2)
            step(dve.reciprocal(row_sum[:, 3:5], row_sum[:, 3:5]))
            after(13)
            share(4)
            share(3)
            dve.wait_ge(e["exp"], Q_BLOCKS * H + 5)
            step(dve.reciprocal(row_sum[:, 0:3], row_sum[:, 0:3]))
            after(16)
            share(2)
            share(1)
            share(0)
            if not ends and x % 2:
                dve_rope(dve, j + (x + 1) // PER_TURN, (x + 1) % PER_TURN)
            dve.wait_ge(e["pv"], H + 2)
            flat = z_t[:].rearrange("p k n -> p (k n)")
            cut = Q_EDGES[3]
            for b, (lo, hi) in enumerate(((0, cut), (cut, L))):
                at = flat[:, bass.ds(H * L + lo, hi - lo)]
                dve.scalar_tensor_tensor(at, wide[3][:, b, 0:hi - lo], 0.5, at, ALU.mult, ALU.mult).then_inc(e["gated"], 1)

        def pool_v(pool, H, slot):
            flat = v_rows[:].rearrange("p t n -> p (t n)")
            pool.tensor_copy(v_now[0:META, slot, 0, :], flat[0:META, bass.ds(H * P, P)]).then_inc(e["v_now"], 1)
            src = v_rows[:, 1:Q_BLOCKS, bass.ds(H * P, P)]
            pool.tensor_copy(v_now[:, slot, 1:Q_BLOCKS, :], src).then_inc(e["v_now"], 1)

        def pool_head(pool, j, x, last):
            H = PER_TURN * j + x
            if last and x >= 2:
                return
            pool.wait_ge(e["pv"], H + 2)
            pool_v(pool, H + 2, x % 2)

        def over_heads(eng, body):
            with eng.Fori(0, HEADS // PER_TURN - 1) as j:
                for x in range(PER_TURN):
                    body(eng, j, x, False)
            for x in range(PER_TURN):
                body(eng, HEADS // PER_TURN - 1, x, True)

        def pe_mla(pe):
            st = seen["pe"]
            pe.wait_ge(d["v_copied"], 4 * Q_BLOCKS)
            pe.drain().then_inc(e["pv"], 1)
            pe_up(pe, 0, 0, 0, first=True)
            over_heads(pe, pe_head)

        def act_mla(act):
            act.drain().then_inc(e["pt"], 6)
            for what in range(3):
                act_up(act, 0, 0, what)
            over_heads(act, act_head)

        def dve_mla(dve):
            dve.drain().then_inc(e["gated"], 2)
            dve_rope(dve, 0, 0)
            dve.wait_ge(d["stats_set"], 3)
            over_heads(dve, dve_head)

        def pool_mla(pool):
            pool.wait_ge(d["v_copied"], 4 * Q_BLOCKS)
            pool_v(pool, 0, 0)
            pool_v(pool, 1, 1)
            over_heads(pool, pool_head)

        def sp_stream(sp, first, end):
            turns = (end - first) // SLOTS
            with sp.Fori(0, turns) as j:
                for n in range(SLOTS):
                    ring.load(sp, stream, first + n, j)
            for n in range(first + turns * SLOTS, end):
                ring.load(sp, stream, n)


        G = ExitStack()

        def sg(name, *shape):
            return G.enter_context(nc.sbuf_tensor(name, [P, *shape], F32))

        g_con = sb("second_tables", CON_OF["odd"][1])
        dft = sg("dft", 2, SEQ // P, SEQ)
        parts = sg("even_parts", 24, SEQ)
        padded = sg("a_c_a_x", 4, SEQ + 2)
        conv = sg("conv", 4, SEQ)
        tanh_z = sg("tanh_z", 4, SEQ)
        spectrum = sg("spectrum", 4, E_G, 2 * E_DIM)
        G.close()
        B_U, A_C, A_X, A_B, A_Z, B_Z = range(0, 24, 4)
        g = {n: sem("g_" + n) for n in ("tanh", "steps", "padded", "part_mm", "part_copied", "dft_mm", "y")}

        def gcon(name, width):
            at = CON[name] - CON_OF["odd"][0]
            return g_con[:, at:at + width]

        def sp_g(sp):
            sp.wait_ge(phase_done, 12)
            first, n = CON_OF["odd"]
            sp.dma_start(g_con[:], con_in[:, first:first + n]).then_inc(con_loaded, 16)
            sp.dma_start(dft[:], dft_in).then_inc(con_loaded, 16)

        def whole(ap):
            return lambda k, b: ap[:, k, 0:SEQ]

        EVEN_FIRST = 16

        def pe_even(pe):
            st = seen["pe"]
            pe_tiles(pe, FIRST["even_in"], EVEN_FIRST, KD, whole(u2), SEQ)
            pe_tiles(pe, FIRST["even_in"] + EVEN_FIRST, 24 - EVEN_FIRST, KD, whole(u2), SEQ)
            pe.wait_ge(con_loaded, 96)
            for n in range(8):
                pair, t = n // 4, n % 4
                if n % 2 == 0:
                    pe.wait_ge(tile_left, st.left - (3 - n // 2 if n < 6 else 0))
                for o in range(2):
                    mm = pe.matmul(wide[n // 2][:, n % 2, o * 256:(o + 1) * 256], parts[:, B_U + 2 * pair + o, t * P:(t + 1) * P],
                                   gcon("dft_d", 2 * E_DIM), start=True, stop=True)
                mm.then_inc(g["part_mm"], 1)
            for grp_ in range(E_G):
                pe.wait_ge(g["part_copied"], 4 + grp_ // 2 * 4)
                for t in range(4):
                    for o in range(2):
                        mm = pe.matmul(wide[grp_][:, 0, :], spectrum[:, t, grp_, o * E_DIM:(o + 1) * E_DIM], dft[:, o, t, :],
                                       start=t + o == 0, stop=t + o == 4)
                mm.then_inc(g["dft_mm"], 1)
            pe.wait_ge(g["y"], 8)

            def y(k, b):
                return parts[:, A_B + k if k < 4 else B_Z + k - 4, :]
            pe_project_out(pe, FIRST["even_out"], KD, y, SEQ, None)

        def act_even(act):
            st = seen["act"]
            flat = parts[:].rearrange("p k n -> p (k n)")

            def keep(j, t, n):
                act.activation(flat[:, bass.ds(n * SEQ, SEQ)], tile_ps(t, SEQ), ACT.Copy).then_inc(tile_left, 1)

            def gate(j, t, n):
                act.wait_ge(g["tanh"], n + 1)
                act.activation(tanh_z[:, t, :], tile_ps(t, SEQ), ACT.Tanh, scale=0.5)
                act.activation(flat[:, bass.ds((n + EVEN_FIRST) * SEQ, SEQ)], tile_ps(t, SEQ), ACT.Copy).then_inc(tile_left, 1)
            act_tiles(act, FIRST["even_in"], EVEN_FIRST, KD, keep)
            act_tiles(act, FIRST["even_in"] + EVEN_FIRST, 24 - EVEN_FIRST, KD, gate)
            for n in range(8):
                pair, t = n // 4, n % 4
                act.wait_ge(g["part_mm"], n + 1)
                act.activation(spectrum[:, t, 2 * pair:2 * pair + 2, :], wide[n // 2][:, n % 2, :].rearrange("p (g n) -> p g n", g=2),
                               ACT.Copy).then_inc(g["part_copied"], 1)
            act_project_out(act, FIRST["even_out"], KD, SEQ, None)

        def dve_even(dve):
            st = seen["dve"]
            dve.memset(padded[:, :, 0:1], 0.0).then_inc(g["padded"], 1)
            dve.memset(padded[:, :, SEQ + 1:SEQ + 2], 0.0).then_inc(g["padded"], 1)
            dve.drain().then_inc(g["tanh"], 4)
            steps = [0]

            def step(ins):
                ins.then_inc(g["steps"], 1)
                steps[0] += 1

            def after():
                dve.wait_ge(g["steps"], steps[0])

            def tiles(n):
                dve.wait_ge(tile_left, st.left + SLOTS + n)
            tiles(A_X + 4)
            step(dve.tensor_tensor(padded[:, :, 1:SEQ + 1], parts[:, A_C:A_C + 4, :], parts[:, A_X:A_X + 4, :], ALU.mult))
            dve.wait_ge(g["padded"], 2)
            after()
            for tap in range(3):
                for t in range(4):
                    w = pcol("conv", tap * 4 + t)
                    src = padded[:, t, tap:tap + SEQ]
                    if tap == 0:
                        step(dve.tensor_scalar(conv[:, t, :], src, w, None, ALU.mult))
                    else:
                        step(dve.scalar_tensor_tensor(conv[:, t, :], src, w, conv[:, t, :], ALU.mult, ALU.add))
                after()
            tiles(A_B + 4)
            step(dve.tensor_tensor(parts[:, A_B:A_B + 4, :], parts[:, A_B:A_B + 4, :], conv[:], ALU.mult))
            after()
            st.left += EVEN_FIRST + SLOTS
            for n in range(8):
                tiles(n + 1)
                z = parts[:, A_Z + n, :]
                step(dve.scalar_tensor_tensor(z, tanh_z[:, n % 4, :], 1.0, z, ALU.add, ALU.mult))
                dve.drain().then_inc(g["tanh"], 1)
                if n < 4:
                    after()
                    y = parts[:, A_B + n, :]
                    dve.scalar_tensor_tensor(y, y, 0.5, z, ALU.mult, ALU.mult).then_inc(g["y"], 1)
            st.left += 24 - EVEN_FIRST + SLOTS
            after()
            for n in range(E_G):
                dve.wait_ge(g["dft_mm"], n + 1)
                z = parts[:, B_Z + n, :]
                dve.scalar_tensor_tensor(z, wide[n][:, 0, :], 0.5, z, ALU.mult, ALU.mult).then_inc(g["y"], 1)
            dve_project_out(dve, KD, SEQ, None, None, "odd", lambda k: u2[:, k, 0:SEQ])

        HH = ExitStack()

        def sh(name, *shape):
            return HH.enter_context(nc.sbuf_tensor(name, [P, *shape], F32))

        NQK = G_HEADS + G_KV
        qk = sh("q_k", NQK, SEQ)
        z_odd = sh("z_odd", G_HEADS, SEQ)
        with_gain, qk_sq, qk_root = sh("with_gain", 2, SEQ), sh("qk_squares", 2, SEQ), sh("qk_root", 2, SEQ)
        rot_sin = sh("rot_sin", SEQ)
        v_odd = sh("v_odd", 4, G_KV * P)
        q_now = sh("q_now", 2, SEQ)
        o_probs, o_probs_t = sh("odd_probs", 2, SEQ), sh("odd_probs_t", 2, SEQ)
        o_max, o_bias, o_sum = (sh("odd_" + n, 8) for n in ("max", "bias", "sum"))
        tanh_odd = sh("tanh_odd", 2, SEQ)
        HH.close()
        o = {n: sem("o_" + n) for n in ("sq", "sum", "rot", "root", "dve", "v_mm", "v_copied", "q_now", "scores", "turned", "pt", "pv",
                                        "exp", "bias", "share", "tanh", "z", "gated")}
        ODD_Z, ODD_K, ODD_V = FIRST["odd_in"] + G_HEADS, FIRST["odd_in"] + 2 * G_HEADS, FIRST["odd_v"]
        ODD_SCALE = P ** -0.5
        DVE_O = Count(o["dve"], 6)
        qk_flat = qk[:].rearrange("p k n -> p (k n)")
        z_flat = z_odd[:].rearrange("p k n -> p (k n)")

        def qk_of(n):
            return qk_flat[:, bass.ds(n * SEQ, SEQ)]

        def pe_qk(pe, n, t):
            pe.wait_ge(o["sq"], n + 1)
            pe.wait_ge(o["root"], n + 1)
            pe.matmul(wide[t % 2][:, 1, :], ones, qk_sq[:, t % 2, :], start=True, stop=True).then_inc(o["sum"], 1)
            pe.wait_ge(o["dve"], 6 * n + 12 + 1)
            pe.matmul(wide[2 + t % 2][:, 1, :], gcon("rot_odd", P), with_gain[:, t % 2, :], start=True, stop=True).then_inc(o["rot"], 1)

        def act_qk(act, n, t):
            act.wait_ge(o["sum"], n + 1)
            act.activation(qk_sq[:, t % 2, :], qk_of(n), ACT.Square).then_inc(o["sq"], 1)
            act.wait_ge(o["sum"], n + 3)
            act.wait_ge(o["dve"], 6 * n + 6)
            act.activation(qk_root[:, t % 2, :], wide[t % 2][:, 1, :], ACT.Sqrt, bias=epsilon[:, 0:1], scale=1.0 / P).then_inc(o["root"], 1)

        def dve_qk(dve, n, t, gain):
            def step(ins):
                ins.then_inc(o["dve"], 1)

            def after(k):
                dve.wait_ge(o["dve"], 6 * n + 12 + k)
            x, y = with_gain[:, t % 2, :], qk_of(n)
            dve.wait_ge(o["rot"], n + 1)
            step(dve.tensor_scalar(x, y, pcol(gain), None, ALU.mult))
            dve.wait_ge(o["sq"], n + 1)
            after(1)
            step(dve.tensor_tensor(y, x, gcon("cos_odd", SEQ), ALU.mult))
            dve.wait_ge(o["rot"], n + 3)
            step(dve.tensor_tensor(rot_sin[:], wide[2 + t % 2][:, 1, :], gcon("sin_odd", SEQ), ALU.mult))
            after(3)
            step(dve.tensor_tensor(y, y, rot_sin[:], ALU.add))
            dve.wait_ge(o["root"], n + 3)
            step(dve.reciprocal(qk_root[:, t % 2, :], qk_root[:, t % 2, :]))
            after(5)
            step(dve.tensor_tensor(y, y, qk_root[:, t % 2, :], ALU.mult))

        def pe_odd_in(pe):
            st = seen["pe"]
            pe.wait_ge(n_used, st.norms)
            pe_tiles(pe, FIRST["odd_in"], G_HEADS, KD, whole(u2), SEQ)
            pe.drain().then_inc(o["sum"], 2)
            pe.drain().then_inc(o["rot"], 2)
            pe_tiles(pe, ODD_Z, G_HEADS, KD, whole(u2), SEQ, after=lambda n, t: pe_qk(pe, n, t))
            pe_tiles(pe, ODD_K, G_KV, KD, whole(u2), SEQ, loop=False)
            for n in range(G_KV):
                pe_qk(pe, G_HEADS + n, n)
            for k in range(2):
                ring.wait_full(pe, ODD_V + k)
            at = ODD_V % SLOTS
            w = ring.tile[:, at:at + 2, :].rearrange("p s (k n) -> p (s k) n", n=G_KV * P)
            for t in range(4):
                pe.wait_ge(tile_left, st.left)
                for k in range(KD):
                    mm = pe.matmul(wide[t][:, 0, 0:G_KV * P], u2[:, k, t * P:(t + 1) * P], w[:, k, :], start=k == 0, stop=k == KD - 1)
                mm.then_inc(o["v_mm"], 1)
            for k in range(2):
                pe.drain().then_inc(ring.done(ODD_V + k), 1)

        def act_odd_in(act):
            act_tiles(act, FIRST["odd_in"], G_HEADS, KD,
                      lambda j, t, n: act.activation(qk_of(n), tile_ps(t, SEQ), ACT.Copy).then_inc(tile_left, 1))
            act.wait_ge(tile_left, seen["act"].left)
            act.drain().then_inc(o["root"], 2)

            def keep_z(j, t, n):
                act.activation(z_flat[:, bass.ds(n * SEQ, SEQ)], tile_ps(t, SEQ), ACT.Copy).then_inc(tile_left, 1)
            act_tiles(act, ODD_Z, G_HEADS, KD, keep_z, before=lambda n, t: act_qk(act, n, t))
            act_tiles(act, ODD_K, G_KV, KD,
                      lambda j, t, n: act.activation(qk_of(G_HEADS + n), tile_ps(t, SEQ), ACT.Copy).then_inc(tile_left, 1), loop=False)
            act.wait_ge(tile_left, seen["act"].left)
            for n in range(G_KV):
                act_qk(act, G_HEADS + n, n)
            for t in range(4):
                act.wait_ge(o["v_mm"], t + 1)
                act.activation(v_odd[:, t, :], wide[t][:, 0, 0:G_KV * P], ACT.Copy).then_inc(o["v_copied"], 1)

        def dve_odd_in(dve):
            st = seen["dve"]
            dve.drain().then_inc(o["dve"], 12)
            dve.wait_ge(tile_left, st.left + G_HEADS + SLOTS)
            over_tiles(dve, G_HEADS, SLOTS, lambda j, t, n: dve_qk(dve, n, t, "q_gain"))
            st.left += 2 * (G_HEADS + SLOTS) + G_KV + SLOTS
            dve.wait_ge(tile_left, st.left)
            for n in range(G_KV):
                dve_qk(dve, G_HEADS + n, n, "k_gain")

        TURNS = G_HEADS // G_KV
        UNITS = G_KV * 4
        AHEAD = 3
        S_BANK = [wide[n // 2][:, n % 2, :] for n in range(4)]

        def pe_scores(pe, j, u):
            j, u = j + u // UNITS, u % UNITS
            x, t = u // 4, u % 4
            if t == 0:
                pe.wait_ge(o["q_now"], 2 * j + x + 1)
            pe.matmul(S_BANK[u % 4], q_now[:, x, t * P:(t + 1) * P], qk[:, G_HEADS + x, :], start=True, stop=True).then_inc(o["scores"], 1)

        def pe_turn(pe, j, last):
            for u in range(UNITS):
                x, t = u // 4, u % 4
                U = UNITS * j + u
                pe.wait_ge(o["share"], 2 * U + 2)
                pe.wait_ge(o["pt"], U + 1)
                for k in range(4):
                    mm = pe.transpose(wide[2][:, u % 2, k * P:(k + 1) * P], o_probs[:, u % 2, k * P:(k + 1) * P], ident)
                mm.then_inc(o["turned"], 1)
                if not (last and u + AHEAD >= UNITS):
                    pe_scores(pe, j, u + AHEAD)
                pe.wait_ge(o["pt"], U + 3)
                if t == 0:
                    pe.wait_ge(o["gated"], 2 * j + x + 1)
                for k in range(4):
                    mm = pe.matmul(wide[3][:, x, t * P:(t + 1) * P], v_odd[:, k, x * P:(x + 1) * P], o_probs_t[:, u % 2, k * P:(k + 1) * P],
                                   start=k == 0, stop=k == 3)
                mm.then_inc(o["pv"], 1)

        def act_turn(act, j, last):
            for x in range(2):
                act.wait_ge(o["z"], 2 * j + x + 1)
                act.activation(tanh_odd[:, x, :], z_flat[:, bass.ds((4 * x + j) * SEQ, SEQ)], ACT.Tanh, scale=0.5).then_inc(o["tanh"], 1)
            for u in range(UNITS):
                U = UNITS * j + u
                act.wait_ge(o["bias"], 2 * U + 2)
                act.wait_ge(o["turned"], U + 1)
                act.activation(o_probs[:, u % 2, :], S_BANK[u % 4], ACT.Exp, bias=o_bias[:, u:u + 1], scale=ODD_SCALE,
                               accum_out=o_sum[:, u:u + 1]).then_inc(o["exp"], 1)
                act.wait_ge(o["turned"], U + 3)
                act.wait_ge(o["pv"], U + 1)
                act.activation(o_probs_t[:, u % 2, :], wide[2][:, u % 2, :], ACT.Copy).then_inc(o["pt"], 1)

        def dve_max(dve, j, u):
            U = UNITS * j + u
            u = u % UNITS
            dve.wait_ge(o["scores"], U + 1)
            dve.tensor_reduce(o_max[:, u:u + 1], S_BANK[u % 4], AX_X, ALU.max).then_inc(o["bias"], 1)
            dve.wait_ge(o["bias"], 2 * U + 1)
            dve.tensor_scalar(o_bias[:, u:u + 1], o_max[:, u:u + 1], -ODD_SCALE, None, ALU.mult).then_inc(o["bias"], 1)

        def dve_turn(dve, j, last):
            for x in range(2):
                dve.wait_ge(o["tanh"], 2 * j + x + 1)
                z = z_flat[:, bass.ds((4 * x + j) * SEQ, SEQ)]
                dve.scalar_tensor_tensor(z, tanh_odd[:, x, :], 1.0, z, ALU.add, ALU.mult).then_inc(o["z"], 1)
            for u in range(UNITS):
                U = UNITS * j + u
                if not (last and u + 1 == UNITS):
                    dve_max(dve, j, u + 1)
                dve.wait_ge(o["exp"], U + 1)
                dve.reciprocal(o_sum[:, u:u + 1], o_sum[:, u:u + 1]).then_inc(o["share"], 1)
                dve.wait_ge(o["share"], 2 * U + 1)
                dve.tensor_scalar(o_probs[:, u % 2, :], o_probs[:, u % 2, :], o_sum[:, u:u + 1], None, ALU.mult).then_inc(o["share"], 1)
                if u % 4 == 3:
                    x = u // 4
                    dve.wait_ge(o["pv"], U + 3)
                    dve.wait_ge(o["z"], 2 * j + x + 3)
                    z = z_flat[:, bass.ds((4 * x + j) * SEQ, SEQ)]
                    dve.scalar_tensor_tensor(z, wide[3][:, x, :], 0.5, z, ALU.mult, ALU.mult).then_inc(o["gated"], 1)

        def pool_q(pool, j, x):
            pool.tensor_copy(q_now[:, x, :], qk_of(4 * x + j)).then_inc(o["q_now"], 1)

        def pool_turn(pool, j, last):
            if not last:
                for x in range(2):
                    pool.wait_ge(o["scores"], UNITS * j + 4 * x + 4)
                    pool_q(pool, j + 1, x)

        def over_turns(eng, body):
            with eng.Fori(0, TURNS - 1) as j:
                body(eng, j, False)
            body(eng, TURNS - 1, True)

        def pe_odd(pe):
            pe.drain().then_inc(o["turned"], 2)
            pe.drain().then_inc(o["pv"], 2)
            pe.wait_ge(o["dve"], 6 * NQK + 12)
            pe.wait_ge(o["v_copied"], 4)
            for u in range(AHEAD):
                pe_scores(pe, 0, u)
            over_turns(pe, pe_turn)
            pe.wait_ge(o["gated"], G_HEADS + 2)
            pe_project_out(pe, FIRST["odd_out"], KD, whole(z_odd), SEQ, None)

        def act_odd(act):
            act.drain().then_inc(o["pt"], 2)
            over_turns(act, act_turn)
            act_project_out(act, FIRST["odd_out"], KD, SEQ, None)

        def dve_odd(dve):
            dve.drain().then_inc(o["z"], 2)
            dve.drain().then_inc(o["gated"], 2)
            dve_max(dve, 0, 0)
            over_turns(dve, dve_turn)
            dve_project_out(dve, KD, SEQ, None, None, "final", lambda k: u2[:, k, 0:SEQ])

        def pool_odd(pool):
            pool.wait_ge(o["dve"], 6 * NQK + 12)
            for x in range(2):
                pool_q(pool, 0, x)
            over_turns(pool, pool_turn)

        def sp_end(sp):
            sp.wait_ge(n_used, NORMS)
            sp.dma_start(out, u2[:, :, 0:SEQ]).then_inc(stored, 16)
            sp.wait_ge(stored, 16)

        stored = sem("stored")
        NORMS = 8

        block = ctx.enter_context(nc.Block())

        @block.sync
        def _(sp):
            sp_setup(sp)
            sp_a(sp)
            sp.wait_ge(s["stored"], 16 * PAIRS)
            for n in range(SLOTS):
                ring.load(sp, stream, FIRST["rwkv_out"] + n)
            sp_b(sp)
            sp_c(sp)
            sp_stream(sp, FIRST["rwkv_out"] + SLOTS, FIRST["even_in"] + SLOTS)
            sp_g(sp)
            sp_stream(sp, FIRST["even_in"] + SLOTS, N_LOADS)
            sp_end(sp)

        @block.tensor
        def _(pe):
            pe_setup(pe)
            pe_lora(pe)
            over_pairs(pe, pe_pair)
            end_phase(pe, "pe")
            passes(pe, pe_pass)
            end_phase(pe, "pe")
            pe.wait_ge(mixed_loaded, 16 * PAIRS)
            pe_project_out(pe, FIRST["rwkv_out"], KI, half_of(z_t), L, L)
            pe_mla_in(pe)
            pe_mla(pe)
            pe.wait_ge(e["gated"], 2 * HEADS + 2)
            pe_project_out(pe, FIRST["mla_out"], KI, half_of(z_t), L, SEQ)
            end_phase(pe, "pe")
            pe_even(pe)
            pe_odd_in(pe)
            pe_odd(pe)

        @block.scalar
        def _(act):
            act_setup(act)
            act_lora(act)
            over_pairs(act, act_pair)
            end_phase(act, "act")
            passes(act, act_pass)
            end_phase(act, "act")
            act_project_out(act, FIRST["rwkv_out"], KI, L, L)
            act_mla_in(act)
            act_mla(act)
            act_project_out(act, FIRST["mla_out"], KI, L, SEQ)
            end_phase(act, "act")
            act_even(act)
            act_odd_in(act)
            act_odd(act)

        @block.vector
        def _(dve):
            dve_setup(dve)
            over_pairs(dve, dve_pair)
            end_phase(dve, "dve")
            dve_b_setup(dve)
            passes(dve, dve_pass)
            end_phase(dve, "dve")
            dve.wait_ge(h_loaded, 16)
            dve_project_out(dve, KI, L, L, "post0", "pre1", lambda k: u2[:, k, :])
            dve_mla_in(dve)
            dve_mla(dve)
            dve_project_out(dve, KI, L, SEQ, "post1", "even", lambda k: u2[:, k, 0:SEQ])
            end_phase(dve, "dve")
            dve_even(dve)
            dve_odd_in(dve)
            dve_odd(dve)

        @block.gpsimd
        def _(pool):
            pool_setup(pool)
            over_pairs(pool, pool_pair)
            end_phase(pool, "pool")
            passes(pool, pool_pass)
            end_phase(pool, "pool")
            pool_mla(pool)
            end_phase(pool, "pool")
            pool_odd(pool)


def tile_columns(w, width=P):
    k, n = w.shape
    return np.ascontiguousarray(w.reshape(k // P, P, n // width, width).transpose(2, 1, 0, 3).reshape(n // width, P, k // P * width))


def loads_of(tiles):
    n, _, m = tiles.shape
    if m >= SLOT:
        return tiles.reshape(n, P, m // SLOT, SLOT).transpose(0, 2, 1, 3).reshape(-1, P, SLOT)
    g = SLOT // m
    return tiles.reshape(n // g, g, P, m).transpose(0, 2, 1, 3).reshape(n // g, P, SLOT)


def weight_stream(a):
    w = a["rwkv_w_in"][0]
    n_main = 4 * DI
    main = tile_columns(w[:, :n_main]).reshape(4, PAIRS, P, SLOT)
    pieces = [tile_columns(w[:, n_main:])]
    pieces.append(np.stack([main[1], main[0], main[2], main[3]], 1).reshape(-1, P, SLOT))
    pieces.append(loads_of(tile_columns(a["rwkv_w_out"][0])))
    m = a["mla_w_in"][0]
    nq, nkv = Q_TILES * P, KV_TILES * P
    rope = m[:, nq + nkv:nq + nkv + KROPE]
    pieces += [tile_columns(m[:, :nq + nkv]), tile_columns(np.concatenate([rope, rope], 1)), tile_columns(m[:, nq + nkv + KROPE:])]
    kv = a["mla_w_kv_up"][0].reshape(nkv, HEADS, 2, P)
    pieces.append(tile_columns(kv[:, :, 1].reshape(nkv, HEADS * P), 512))
    q = a["mla_w_q_up"][0].reshape(nq, HEADS // 2, 2, P + KROPE)
    for j in range(HEADS // 2):
        pieces.append(loads_of(tile_columns(q[:, j, :, :P].reshape(nq, 2 * P))))
        last = np.concatenate([tile_columns(q[:, j, :, P:].reshape(nq, P))[0],
                               tile_columns(kv[:, 2 * j, 0])[0], tile_columns(kv[:, 2 * j + 1, 0])[0]], 1)
        pieces.append(last[None])
    pieces.append(loads_of(tile_columns(a["mla_w_out"][0])))
    e = a["w_in_even_2"][0]
    e = e.reshape(D, 6, 4 * P)
    pieces.append(tile_columns(np.ascontiguousarray(e[:, [4, 2, 0, 1, 3, 5]]).reshape(D, -1)))
    pieces.append(tile_columns(a["w_out_even_2"][0]))
    o = a["w_in_odd_2"][0]
    nq, nkv = G_HEADS * P, G_KV * P
    pieces += [tile_columns(o[:, :nq]), tile_columns(o[:, nq + 2 * nkv:]), tile_columns(o[:, nq:nq + nkv])]
    pieces.append(loads_of(tile_columns(o[:, nq + nkv:nq + 2 * nkv], 2 * P)))
    pieces.append(tile_columns(a["w_out_odd_2"][0]))
    stream = np.concatenate(pieces, 0)
    assert stream.shape == (N_LOADS, P, SLOT), stream.shape
    return stream


def columns(v):
    return np.ascontiguousarray(v.reshape(-1, P).T)


def parameters(a):
    out = np.zeros((P, N_PAR), np.float32)

    def put(name, v):
        c = columns(v)
        out[:, PAR[name]:PAR[name] + c.shape[1]] = c
    for n in range(2):
        put(f"pre{n}", a["norm_pre"][n])
        put(f"post{n}", a["norm_post"][n])
    put("mu", a["rwkv_mu"][0])
    put("rwkv", np.concatenate([a[n][0] for n in ("rwkv_w0", "rwkv_a0", "rwkv_k_k", "rwkv_k_a", "rwkv_r_k", "rwkv_ln_w", "rwkv_ln_b")]))
    put("q_norm", a["mla_q_norm"][0])
    put("kv_norm", a["mla_kv_norm"][0])
    put("even", a["norm_even_2"][0])
    put("conv", a["conv_w_2"][0])
    put("odd", a["norm_odd_2"][0])
    put("q_gain", a["q_gain_2"][0])
    put("k_gain", a["k_gain_2"][0])
    put("final", a["final_norm_2"])
    return out


def constants():
    con = np.zeros((P, N_CON), np.float64)

    def put(name, v):
        con[:, CON[name]:CON[name] + v.shape[1]] = v
    r, c = np.arange(P)[:, None], np.arange(P)[None, :]
    put("ident", np.eye(P))
    put("ones", np.ones((P, P)))
    put("heads", r // C == c // C)
    for n in range(6):
        m = 1 << n
        put_at = (r // (2 * m) == c // (2 * m)) & (r // m % 2 == 1) & (c // m % 2 == 0)
        con[:, CON["levels"] + n * P:CON["levels"] + (n + 1) * P] = put_at
        if n == 0:
            put("level0T", put_at.T)
    s, t = np.arange(P)[:, None] % C, np.arange(C)[None, :]
    put("tri", np.concatenate([s < t, s <= t], 1))
    put("reset", np.repeat((np.arange(LP) % C != 0)[None], P, 0))
    put("causal", np.where(c <= r, 0.0, -BIG))
    half = KROPE // 2
    inv = np.exp(-math.log(10000.0) * np.arange(half) / half)
    ang = (inv[:, None] * np.arange(L)[None, :])[np.arange(P) % half]
    put("cos_mla", np.cos(ang))
    put("sin_mla", np.sin(ang))
    rot = np.zeros((P, P))
    for b in range(0, P, KROPE):
        for n in range(half):
            rot[b + half + n, b + n] = -1
            rot[b + n, b + half + n] = 1
    put("rot_mla", rot)
    pos = np.arange(SEQ)
    inv = 10000.0 ** (-np.arange(P // 4) / (P // 4))
    ang = np.concatenate([(pos // 64)[None] * inv[:, None], (pos % 64)[None] * inv[:, None]], 0)[np.arange(P) // 2]
    put("cos_odd", np.cos(ang))
    put("sin_odd", np.sin(ang))
    rot = np.zeros((P, P))
    for n in range(0, P, 2):
        rot[n + 1, n] = -1
        rot[n, n + 1] = 1
    put("rot_odd", rot)
    d = np.outer(np.arange(E_DIM), np.arange(E_DIM)) % E_DIM * (2 * math.pi / E_DIM)
    put("dft_d", np.concatenate([np.cos(d), np.sin(d)], 1))
    n = np.outer(np.arange(SEQ), np.arange(SEQ)) % SEQ * (2 * math.pi / SEQ)
    scale = (SEQ * E_DIM) ** -0.5
    dft = np.stack([np.cos(n) * scale, -np.sin(n) * scale]).reshape(2, SEQ // P, P, SEQ).transpose(2, 0, 1, 3)
    return con.astype(np.float32), np.ascontiguousarray(dft.astype(np.float32))


def device_inputs(a):
    tokens = np.concatenate([a["meta_tokens"], a["x"][0]], 0)
    con, dft = constants()
    lora = np.concatenate([a["rwkv_w2"][0], a["rwkv_a2"][0]], 0)
    return {
        "tokens": np.ascontiguousarray(tokens.T.reshape(KD, P, L).transpose(1, 0, 2)),
        "stream": weight_stream(a),
        "lora": np.ascontiguousarray(lora.reshape(P, PAIRS, P).transpose(1, 0, 2)),
        "par": parameters(a), "con": con, "dft": dft,
    }


def build(nc, arrays):
    def dram(name, shape, kind):
        return nc.dram_tensor(name, shape, F32, kind=kind).ap()

    ins = [dram(f"in_{n}", arrays[n].shape, "ExternalInput") for n in ("tokens", "stream", "lora", "par", "con", "dft")]
    out = dram("out", (P, KD, SEQ), "ExternalOutput")
    program(nc, *ins, out, dram("forms", (PAIRS, P, F_COLS), "Internal"), dram("mixed", (PAIRS, P, L), "Internal"))


def kernel(**inputs):
    import concourse.bacc as bacc
    from concourse.bass_utils import run_bass_kernel_spmd

    arrays = device_inputs({n: np.asarray(v) for n, v in inputs.items()})
    nc = bacc.Bacc("TRN2", target_bir_lowering=False, num_devices=1)
    build(nc, arrays)
    r = run_bass_kernel_spmd(nc, [{f"in_{n}": v for n, v in arrays.items()}], core_ids=[0])
    got = r.results[0]["out"]
    return np.ascontiguousarray(got.transpose(2, 1, 0).reshape(1, SEQ, D))
```

```python
import math
from contextlib import ExitStack

import numpy as np

import concourse.bass as bass
from concourse import mybir

F32 = mybir.dt.float32
ALU = mybir.AluOpType
ACT = mybir.ActivationFunctionType
AX_X = mybir.AxisListType.X

P = 128
D = 1024
DI = 2048
SEQ = 512
META = 16
L = META + SEQ
HALF = L // 2
KD = D // P
KI = DI // P
PAIRS = DI // P
C = 64
NC = -(-L // C)
LP = NC * C
PAD = LP - L
LORA = 64
RMS_EPS = 1e-6
GN_EPS = 64e-5
EXP_M_HALF = math.exp(-0.5)
Q_TILES, KV_TILES = 4, 2
HEADS = 16
KROPE = 64
E_G, E_DIM = 4, 128
G_HEADS, G_KV = 8, 2
BIG = 1e30

SLOT = 1024
SLOTS = 4
LOADS = [("lora", 1), ("rwkv_in", 4 * PAIRS), ("rwkv_out", 2 * KD), ("mla_in", Q_TILES + KV_TILES + 1 + KI),
         ("mla_v", 4), ("mla_up", HEADS), ("mla_out", 2 * KD), ("even_in", 24), ("even_out", KD),
         ("odd_in", 2 * G_HEADS + G_KV), ("odd_v", 2), ("odd_out", KD)]
FIRST = {}
_n = 0
for _name, _count in LOADS:
    FIRST[_name] = _n
    _n += _count
N_LOADS = _n

PAR = {}
_n = 0
for _name, _count in [("pre0", KD), ("post0", KD), ("pre1", KD), ("post1", KD), ("mu", 6 * KD), ("rwkv", 7 * PAIRS),
                      ("q_norm", Q_TILES), ("kv_norm", KV_TILES), ("even", KD), ("conv", 12), ("odd", KD),
                      ("q_gain", 1), ("k_gain", 1), ("final", KD)]:
    PAR[_name] = _n
    _n += _count
N_PAR = _n
W0, A0, KK, KA, RK, LNW, LNB = range(7)

CON, CON_OF = {}, {}
_n = 0
for _part, _names in [("all", [("ident", P), ("ones", P), ("heads", P), ("reset", LP)]),
                      ("rwkv", [("levels", 6 * P), ("level0T", P), ("tri", 2 * C)]),
                      ("mla", [("causal", P), ("rot_mla", P), ("cos_mla", L), ("sin_mla", L)]),
                      ("odd", [("rot_odd", P), ("cos_odd", SEQ), ("sin_odd", SEQ), ("dft_d", 2 * E_DIM)])]:
    _first = _n
    for _name, _count in _names:
        CON[_name] = _n
        _n += _count
    CON_OF[_part] = (_first, _n - _first)
N_CON = _n

F_AR, F_B, F_K, F_V, F_SG, F_BON, F_PC = 0, 2 * LP, 3 * LP, 4 * LP, 5 * LP, 6 * LP, 7 * LP
F_COLS = F_PC + NC


class Count:

    def __init__(self, sem, per=1):
        self.sem, self.per = sem, per

    def at(self, i, k):
        return i * self.per + k

    def before(self, i):
        return i * self.per


class Ring:

    def __init__(self, tile, full, used):
        self.tile, self.full, self.used = tile, full, used

    def slot(self, load):
        return self.tile[:, load % SLOTS, :]

    def wait_full(self, eng, load, step=0):
        eng.wait_ge(self.full[load % SLOTS], (step + load // SLOTS + 1) * 16)

    def wait_used(self, eng, load, step=0):
        eng.wait_ge(self.used[load % SLOTS], step + load // SLOTS + 1)

    def done(self, load):
        return self.used[load % SLOTS]

    def load(self, sp, stream, load, step=0):
        if not (isinstance(step, int) and load + SLOTS * step < SLOTS):
            sp.wait_ge(self.used[load % SLOTS], step + load // SLOTS)
        sp.dma_start(self.slot(load), stream[step * SLOTS + load]).then_inc(self.full[load % SLOTS], 16)


class Norms:

    def __init__(self, squared, summed, rooted, inverted):
        self.squared, self.summed, self.rooted, self.inverted = squared, summed, rooted, inverted


def program(nc, x_in, stream, lora_in, par_in, con_in, dft_in, out, forms, mixed):
    with ExitStack() as ctx:
        def sb(name, *shape):
            return ctx.enter_context(nc.sbuf_tensor(name, [P, *shape], F32))

        def sem(name):
            return ctx.enter_context(nc.semaphore(name))

        wide = [ctx.enter_context(nc.psum_tensor(f"wide{j}", [P, 2, 512], F32)) for j in range(4)]
        ring = Ring(sb("weights", SLOTS, SLOT), [sem(f"weights_full{s}") for s in range(SLOTS)],
                    [sem(f"weights_used{s}") for s in range(SLOTS)])
        par = sb("par", N_PAR)
        con = sb("con", CON_OF["all"][1])
        inv_rms = sb("inv_rms", L)
        epsilon = sb("epsilon", 2)


        def cons(name, width):
            return con[:, CON[name]:CON[name] + width]

        def pcol(name, n=0):
            return par[:, PAR[name] + n:PAR[name] + n + 1]

        ident, ones, heads = cons("ident", P), cons("ones", P), cons("heads", P)

        x_loaded, con_loaded = [sem(f"x_loaded{k}") for k in range(KD // 2)], sem("con_loaded")
        const_set, eps_set = sem("const_set"), sem("eps_set")
        squared, summed, rooted, inverted = (sem(n) for n in ("squared", "summed", "rooted", "inverted"))
        applied = sem("applied")

        class N:
            sq = 0
            n = 0

        def halves(ap, width):
            return ap.rearrange("p (b n) -> p b n", b=2) if width == L else ap

        def act_norm(act, st, src, kt, width, sq, ps, eps, div):
            for k in range(kt):
                if k % 2 == 0:
                    act.wait_ge(x_loaded[k // 2], 16)
                act.activation(sq(k), src(k), ACT.Square).then_inc(squared, 1)
            st.sq += kt
            st.n += 1
            act.wait_ge(summed, st.n)
            act.activation(halves(inv_rms[:, 0:width], width), ps(width), ACT.Sqrt,
                           bias=epsilon[:, 0:1], scale=1.0 / div).then_inc(rooted, 1)

        def pe_norm(pe, st, kt, width, sq, ps):
            w = ps(width)
            parts = [(w[:, b, :], slice(b * HALF, (b + 1) * HALF)) for b in range(2)] if width == L else [(w, slice(0, width))]
            for k in range(kt):
                st.sq += 1
                pe.wait_ge(squared, st.sq)
                for dst, cols in parts:
                    mm = pe.matmul(dst, ones, sq(k)[:, cols], start=k == 0, stop=k == kt - 1)
            mm.then_inc(summed, 1)

        def dve_norm(dve, st, width):
            st.n += 1
            dve.wait_ge(rooted, st.n)
            dve.reciprocal(inv_rms[:, 0:width], inv_rms[:, 0:width]).then_inc(inverted, 1)
            dve.wait_ge(inverted, st.n)

        def wide_ps(j):
            return lambda width: wide[j][:, :, 0:HALF] if width == L else wide[j][:, 0, 0:width]

        norm = {who: N() for who in ("pe", "act", "dve")}
        for st in norm.values():
            st.sq = st.n = 0

        A = ExitStack()

        def sa(name, *shape):
            return A.enter_context(nc.sbuf_tensor(name, [P, *shape], F32))

        lora = sa("lora", L)
        lora_w = sa("lora_w", P)
        a_r, a_k, a_lw, a_cum, a_a, a_kk, a_sq, a_inv, a_k2, a_rk, a_tg, a_Pinv = (
            sa(n, LP) for n in ("r", "k", "log_decay", "log_cum", "a", "kk", "kk_sq", "kk_inv", "k2", "rk", "tanh_g", "p_inv"))
        a_P = sa("p_cum", NC, 1 + C)
        A_LATE = ExitStack()

        def rounded_over(name, *shape):
            t = A_LATE.enter_context(nc.sbuf_tensor(name, [P, *shape], mybir.dt.float32r))
            A_LATE.close()
            return t
        low_k = rounded_over("low_k", KD, L)
        x_t = sa("x", KD, L)
        low_v = rounded_over("low_v", KD, L)
        u = sa("u", KD, 1 + L)
        w_in = [A_LATE.enter_context(nc.sbuf_tensor(f"w_{n}_rwkv_in", [P, 2, SLOT], mybir.dt.float32r)) for n in ("high", "low")]
        A_LATE.close()
        diff = sa("diff", KD, L)
        mixed_hi = rounded_over("mixed_high", 4, KD, L)
        mixed_in = sa("mixed_in", 4, KD, L)
        form = sa("form", F_COLS)
        half_w0 = sa("half_w0a0", 2 * PAIRS)
        low_r = rounded_over("low_r", KD, L)
        mixed_lo = (low_k, low_r, low_v)
        SPLIT = len(mixed_lo)
        A.close()
        f_ar = form[:, F_AR:F_AR + 2 * LP].rearrange("p (c s n) -> p c s n", c=NC, s=2)
        f_b, f_k, f_v, f_sg, f_bon = (form[:, o:o + LP] for o in (F_B, F_K, F_V, F_SG, F_BON))
        f_pc = form[:, F_PC:F_PC + NC]
        LERP = {"k": 0, "r": 1, "v": 2, "g": 3}
        MU = {"r": 0, "k": 1, "v": 2, "g": 3, "w": 4, "a": 5}

        def real(ap):
            return ap[:, PAD:LP].rearrange("p (b n) -> p b n", b=2)

        def by_chunk(ap):
            return ap.rearrange("p (c n) -> p c n", c=NC)

        def rw(which, pair):
            if isinstance(pair, int):
                return pcol("rwkv", which * PAIRS + pair)
            return par[:, bass.ds(pair + (PAR["rwkv"] + which * PAIRS), 1)]

        a_sems = {n: sem("a_" + n) for n in (
            "diff", "lerp", "lora_loaded", "lora_low", "proj_w", "proj_a", "tanh_w", "tanh_a", "k_copied", "r_copied", "kk_squared",
            "p_exp", "kk_summed", "kk_rooted", "v_copied", "g_tanh", "pc_copied", "rk_summed", "dve", "pool", "stored", "in_rounded", "in_rest", "in_whole")}

        def half_bias(n, pair):
            if isinstance(pair, int):
                return half_w0[:, n * PAIRS + pair:n * PAIRS + pair + 1]
            return half_w0[:, bass.ds(pair + n * PAIRS, 1)]

        s = a_sems
        DVE_A = Count(s["dve"], 15)
        POOL_A = Count(s["pool"], 2)
        EXP_A = Count(s["p_exp"], 2)

        def sp_setup(sp):
            for k in range(0, KD, 2):
                sp.dma_start(x_t[:, k:k + 2, :], x_in[:, k:k + 2, :]).then_inc(x_loaded[k // 2], 16)
            sp.dma_start(par[:], par_in).then_inc(con_loaded, 16)
            sp.dma_start(con[:], con_in[:, 0:CON_OF["all"][1]]).then_inc(con_loaded, 16)
            ring.load(sp, stream, 0)
            for j in range(3):
                ring.load(sp, stream, 1 + j)

        def act_setup(act):
            act.wait_ge(eps_set, 2)
            act_norm(act, norm["act"], lambda k: x_t[:, k, :], KD, L, lambda k: mixed_in[:, 0, k, :], wide_ps(0), 0, D)

        def pe_setup(pe):
            pe.wait_ge(con_loaded, 32)
            pe_norm(pe, norm["pe"], KD, L, lambda k: mixed_in[:, 0, k, :], wide_ps(0))

        def pool_setup(pool):
            pool.memset(u[:, :, 0:1], 0.0).then_inc(const_set, 1)
            for t in (a_r, a_k, a_lw, a_a, a_kk, a_sq, a_inv, form):
                pool.memset(t[:], 0.0).then_inc(const_set, 1)
            pool.memset(a_P[:, :, 0:1], 1.0).then_inc(const_set, 1)

        N_SET = 10

        def dve_setup(dve):
            dve.memset(epsilon[:, 0:1], RMS_EPS).then_inc(eps_set, 1)
            dve.memset(epsilon[:, 1:2], GN_EPS).then_inc(eps_set, 1)
            dve.wait_ge(con_loaded, 32)
            dve.tensor_scalar(half_w0[:], par[:, PAR["rwkv"]:PAR["rwkv"] + 2 * PAIRS], 0.5, None, ALU.mult).then_inc(applied, 1)
            dve_norm(dve, norm["dve"], L)
            dve.wait_ge(const_set, N_SET)

            def lerp_tile(dst, which, k):
                dve.scalar_tensor_tensor(dst[:, k, :], diff[:, k, :], pcol("mu", MU[which] * KD + k), u[:, k, 1:],
                                         ALU.mult, ALU.add).then_inc(s["lerp"], 1)

            def lerp(dst, which):
                for k in range(KD):
                    lerp_tile(dst, which, k)
            for n in range(KD + 2):
                if n < KD:
                    dve.scalar_tensor_tensor(u[:, n, 1:], x_t[:, n, :], pcol("pre0", n), inv_rms[:], ALU.mult, ALU.mult).then_inc(applied, 1)
                if 0 <= n - 1 < KD:
                    dve.wait_ge(applied, 1 + n)
                    dve.tensor_tensor(diff[:, n - 1, :], u[:, n - 1, 0:L], u[:, n - 1, 1:], ALU.subtract).then_inc(s["diff"], 1)
                if n - 2 >= 0:
                    dve.wait_ge(s["diff"], n - 1)
                    lerp_tile(mixed_in[:, 2], "w", n - 2)
            lerp(mixed_in[:, 3], "a")
            lerp(mixed_in[:, 0], "k")
            lerp(mixed_in[:, 1], "r")
            dve.wait_ge(s["proj_w"], 1)
            dve.wait_ge(s["proj_a"], 1)
            lerp(mixed_in[:, 2], "v")
            lerp(mixed_in[:, 3], "g")

        def product(pe, dst, load, rhs, step=0, kt=KD, ready=None):
            for b in range(2):
                for k in range(kt):
                    if ready is not None and b == 0:
                        pe.wait_ge(s["lerp"], ready + k + 1)
                    mm = pe.matmul(dst[:, b, 0:HALF], ring.slot(load)[:, k * P:(k + 1) * P], rhs[:, k, b * HALF:(b + 1) * HALF],
                                   start=k == 0, stop=k == kt - 1)
            return mm

        def pe_lora(pe):
            ring.wait_full(pe, 0)
            product(pe, wide[0], 0, mixed_in[:, 2], ready=0).then_inc(s["proj_w"], 1)
            product(pe, wide[1], 0, mixed_in[:, 3], ready=KD).then_inc(ring.done(0), 1)
            pe.drain().then_inc(s["proj_a"], 1)

        def act_lora(act):
            act.wait_ge(s["proj_w"], 1)
            act.activation(lora[0:LORA, :].rearrange("p (b n) -> p b n", b=2), wide[0][0:LORA, :, 0:HALF], ACT.Tanh).then_inc(s["lora_low"], 1)
            act.wait_ge(s["proj_a"], 1)
            act.activation(lora[LORA:P, :].rearrange("p (b n) -> p b n", b=2), wide[1][LORA:P, :, 0:HALF], ACT.Copy).then_inc(s["lora_low"], 1)

        LERP_OF = [("k", 2), ("r", 3), ("v", 0), ("g", 1)]

        def pe_pair(pe, i, first):
            def project(j, dst, lerps):
                if not first and j < SPLIT:
                    pe.wait_ge(w_split, SPLIT * i + (j + 1 - SPLIT))
                    for k in range(KD):
                        pe.wait_ge(s["in_whole"], KD * j + k + 1)
                        for b in range(2):
                            half = slice(b * HALF, (b + 1) * HALF)
                            mm = split_products(pe, dst[:, b, 0:HALF], [w[:, (1 + j) % 2, k * P:(k + 1) * P] for w in w_in],
                                                [mixed_hi[:, j, k, half], mixed_lo[j][:, k, half]], k == 0, k == KD - 1)
                    mm.then_inc(ring.done(1 + j), 1)
                    return
                ring.wait_full(pe, 1 + j, i)
                product(pe, dst, 1 + j, mixed_in[:, j], i, ready=(lerps - 1) * KD if first else None).then_inc(ring.done(1 + j), 1)

            if not first:
                pe.wait_ge(s["kk_rooted"], i)
            project(0, wide[2], 3)
            if not first:
                pe.wait_ge(DVE_A.sem, DVE_A.before(i))
            project(1, wide[3], 4)
            pe.wait_ge(s["lora_loaded"], 16 * i + 16)
            if first:
                pe.wait_ge(s["lora_low"], 2)
            else:
                pe.wait_ge(s["v_copied"], i)
            for low, rows, dst in ((s["proj_w"], slice(0, LORA), wide[0]), (s["proj_a"], slice(LORA, P), wide[1])):
                for b in range(2):
                    mm = pe.matmul(dst[:, b, 0:HALF], lora_w[rows, :], lora[rows, b * HALF:(b + 1) * HALF], start=True, stop=True)
                mm.then_inc(low, 1)
            pe.wait_ge(s["tanh_w"], i + 1)
            project(2, wide[0], 5)
            pe.wait_ge(s["k_copied"], i + 1)
            pe.wait_ge(s["kk_squared"], i + 1)
            for b in range(2):
                mm = pe.matmul(wide[2][:, b, 0:HALF], heads, a_sq[:, PAD + b * HALF:PAD + (b + 1) * HALF], start=True, stop=True)
            mm.then_inc(s["kk_summed"], 1)
            pe.wait_ge(s["tanh_a"], i + 1)
            project(3, wide[1], 6)
            pe.wait_ge(s["r_copied"], i + 1)
            pe.wait_ge(DVE_A.sem, DVE_A.at(i, 7))
            for b in range(2):
                mm = pe.matmul(wide[3][:, b, 0:HALF], heads, a_rk[:, PAD + b * HALF:PAD + (b + 1) * HALF], start=True, stop=True)
            mm.then_inc(s["rk_summed"], 1)

        def act_pair(act, i, first):
            if first:
                act.wait_ge(const_set, N_SET)
                act.wait_ge(applied, 1)
            else:
                act.wait_ge(DVE_A.sem, DVE_A.before(i))
                act.wait_ge(POOL_A.sem, POOL_A.before(i))
            ring.wait_used(act, 1, i)
            act.activation(real(a_k), wide[2][:, :, 0:HALF], ACT.Copy).then_inc(s["k_copied"], 1)
            act.wait_ge(DVE_A.sem, DVE_A.at(i, 1))
            act.activation(a_sq[:], a_kk[:], ACT.Square).then_inc(s["kk_squared"], 1)
            ring.wait_used(act, 2, i)
            act.activation(real(a_r), wide[3][:, :, 0:HALF], ACT.Copy).then_inc(s["r_copied"], 1)
            act.wait_ge(s["proj_w"], i + 2)
            act.activation(real(a_lw), wide[0][:, :, 0:HALF], ACT.Tanh, bias=half_bias(0, i), scale=0.5).then_inc(s["tanh_w"], 1)
            act.wait_ge(s["proj_a"], i + 2)
            act.activation(real(a_a), wide[1][:, :, 0:HALF], ACT.Tanh, bias=half_bias(1, i), scale=0.5).then_inc(s["tanh_a"], 1)
            act.wait_ge(DVE_A.sem, DVE_A.at(i, 3))
            act.activation(a_P[:, :, 1:], by_chunk(a_cum[:]), ACT.Exp).then_inc(EXP_A.sem, 1)
            act.activation(a_Pinv[:], a_cum[:], ACT.Exp, scale=-1.0).then_inc(EXP_A.sem, 1)
            ring.wait_used(act, 3, i)
            if not first:
                act.wait_ge(s["stored"], 16 * i)
            act.activation(real(f_v), wide[0][:, :, 0:HALF], ACT.Copy).then_inc(s["v_copied"], 1)
            act.wait_ge(s["kk_summed"], i + 1)
            act.activation(real(a_inv), wide[2][:, :, 0:HALF], ACT.Sqrt).then_inc(s["kk_rooted"], 1)
            ring.wait_used(act, 4, i)
            act.activation(real(a_tg), wide[1][:, :, 0:HALF], ACT.Tanh, scale=0.5).then_inc(s["g_tanh"], 1)
            act.wait_ge(EXP_A.sem, EXP_A.at(i, 1))
            act.activation(f_pc, a_P[:, :, C:C + 1].rearrange("p c n -> p (c n)"), ACT.Copy).then_inc(s["pc_copied"], 1)

        def act_in_parts(act):
            act.wait_ge(s["lerp"], 6 * KD)
            n_tiles = SPLIT * KD
            for n in range(n_tiles + 2):
                if n < n_tiles:
                    act.activation(mixed_lo[n // KD][:, n % KD, :], mixed_in[:, n // KD, n % KD, :], ACT.Copy).then_inc(s["in_rounded"], 1)
                if n >= 2:
                    j, k = divmod(n - 2, KD)
                    act.wait_ge(s["in_rest"], n - 1)
                    act.activation(mixed_hi[:, j, k, :], mixed_in[:, j, k, :], ACT.Copy).then_inc(s["in_whole"], 1)

        def dve_in_parts(dve):
            for n in range(SPLIT * KD):
                j, k = divmod(n, KD)
                dve.wait_ge(s["in_rounded"], n + 1)
                dve.tensor_tensor(mixed_lo[j][:, k, :], mixed_in[:, j, k, :], mixed_lo[j][:, k, :].bitcast(F32), ALU.subtract).then_inc(s["in_rest"], 1)

        def dve_pair(dve, i, first):
            def step(ins):
                ins.then_inc(DVE_A.sem, 1)

            def after(k):
                dve.wait_ge(DVE_A.sem, DVE_A.at(i, k))

            half = 0.5 * EXP_M_HALF
            dve.wait_ge(s["k_copied"], i + 1)
            step(dve.tensor_scalar(a_kk[:], a_k[:], rw(KK, i), None, ALU.mult))
            dve.wait_ge(s["tanh_w"], i + 1)
            step(dve.tensor_scalar(a_lw[:, PAD:], a_lw[:, PAD:], -half, -half, ALU.mult, ALU.add))
            after(2)
            step(dve.tensor_tensor_scan(a_cum[:], cons("reset", LP), a_lw[:], 0.0, ALU.mult, ALU.add))
            dve.wait_ge(s["tanh_a"], i + 1)
            step(dve.tensor_scalar(a_a[:, PAD:], a_a[:, PAD:], 0.5, 0.5, ALU.mult, ALU.add))
            after(4)
            step(dve.tensor_scalar(a_k2[:], a_a[:], 1.0, rw(KA, i), ALU.subtract, ALU.mult))
            after(5)
            step(dve.scalar_tensor_tensor(a_k2[:], a_k2[:], 1.0, a_k[:], ALU.add, ALU.mult))
            after(6)
            dve.wait_ge(s["r_copied"], i + 1)
            step(dve.scalar_tensor_tensor(a_rk[:], a_r[:], rw(RK, i), a_k2[:], ALU.mult, ALU.mult))
            dve.wait_ge(s["kk_rooted"], i + 1)
            step(dve.tensor_scalar(a_inv[:, PAD:], a_inv[:, PAD:], 1e-12, None, ALU.max))
            after(8)
            step(dve.reciprocal(a_inv[:, PAD:], a_inv[:, PAD:]))
            after(9)
            step(dve.tensor_tensor(a_kk[:, PAD:], a_kk[:, PAD:], a_inv[:, PAD:], ALU.mult))
            after(10)
            dve.wait_ge(EXP_A.sem, EXP_A.at(i, 2))
            if not first:
                dve.wait_ge(s["stored"], 16 * i)
            step(dve.scalar_tensor_tensor(f_ar[:, :, 0, :], by_chunk(a_kk[:]), -1.0, a_P[:, :, 0:C], ALU.mult, ALU.mult))
            step(dve.tensor_tensor(a_inv[:, PAD:], a_kk[:, PAD:], a_a[:, PAD:], ALU.mult))
            after(12)
            step(dve.tensor_tensor(f_b[:, PAD:], a_inv[:, PAD:], a_Pinv[:, PAD:], ALU.mult))
            dve.wait_ge(s["v_copied"], i + 1)
            dve.wait_ge(s["rk_summed"], i + 1)
            step(dve.tensor_tensor(real(f_bon), wide[3][:, :, 0:HALF], real(f_v), ALU.mult))
            dve.wait_ge(s["g_tanh"], i + 1)
            step(dve.scalar_tensor_tensor(real(f_sg), real(a_tg), 1.0, wide[1][:, :, 0:HALF], ALU.add, ALU.mult))

        def pool_pair(pool, i, first):
            if not first:
                pool.wait_ge(s["lerp"], 6 * KD)
                for j, (before, step) in enumerate(((3, i - 1), (2, i - 1), (1, i))):
                    load, at = 1 + j, (1 + j) % 2
                    ring.wait_full(pool, load, i)
                    ring.wait_used(pool, before, step)
                    pool.tensor_tensor(w_in[0][:, at, :].rearrange("p (k n) -> p k n", k=KD), ring.slot(load).rearrange("p (k n) -> p k n", k=KD),
                                       ones.unsqueeze(1).to_broadcast([P, KD, P]), ALU.mult).then_inc(w_high, 1)
                    pool.wait_ge(w_high, SPLIT * i + (j + 1 - SPLIT))
                    pool.tensor_tensor(w_in[1][:, at, :], ring.slot(load), w_in[0][:, at, :].bitcast(F32), ALU.subtract).then_inc(w_split, 1)
            pool.wait_ge(EXP_A.sem, EXP_A.at(i, 2))
            if not first:
                pool.wait_ge(s["stored"], 16 * i)
            pool.wait_ge(DVE_A.sem, DVE_A.at(i, 6))
            pool.tensor_tensor(f_k, a_k2[:], a_Pinv[:], ALU.mult).then_inc(POOL_A.sem, 1)
            pool.wait_ge(s["r_copied"], i + 1)
            pool.tensor_tensor(f_ar[:, :, 1, :], by_chunk(a_r[:]), a_P[:, :, 1:], ALU.mult).then_inc(POOL_A.sem, 1)

        def sp_store(sp, i):
            sp.wait_ge(DVE_A.sem, DVE_A.at(i, 15))
            sp.wait_ge(POOL_A.sem, POOL_A.at(i, 2))
            sp.wait_ge(s["v_copied"], i + 1)
            sp.wait_ge(s["pc_copied"], i + 1)
            sp.dma_start(forms[i], form[:]).then_inc(s["stored"], 16)

        def sp_a(sp):
            sp.dma_start(lora_w[:], lora_in[0]).then_inc(s["lora_loaded"], 16)
            ring.load(sp, stream, 4)
            with sp.Fori(1, PAIRS) as i:
                sp.wait_ge(s["proj_a"], i + 1)
                sp.dma_start(lora_w[:], lora_in[i]).then_inc(s["lora_loaded"], 16)
                for j in range(4):
                    ring.load(sp, stream, 1 + j, i)
                sp_store(sp, i - 1)
            sp.wait_ge(q["early_set"], 4)
            first, n = CON_OF["rwkv"]
            sp.dma_start(b_con[:], con_in[:, first:first + n]).then_inc(con_loaded, 16)
            sp.wait_ge(s["stored"], 16 * (PAIRS - 1))
            sp_forms(sp, 0)
            sp_store(sp, PAIRS - 1)

        def over_pairs(eng, body, after_first=None):
            body(eng, 0, True)
            if after_first:
                after_first(eng)
            with eng.Fori(1, PAIRS) as i:
                body(eng, i, False)

        B = ExitStack()

        def sbb(name, *shape):
            return B.enter_context(nc.sbuf_tensor(name, [P, *shape], F32))

        def sbr(name, *shape):
            return B.enter_context(nc.sbuf_tensor(name, [P, *shape], mybir.dt.float32r))

        GROUPS, GC = 3, NC // 3
        LEVEL_BUFS = 2
        LEVELS = 5
        n_all = sbb("n", NC, P)
        w_rnd, x_rnd, e_rnd = (sbr(n, NC, P) for n in ("w_rounded", "x_rounded", "e_rounded"))
        qg = sbb("b_with_a_r", 2, NC, 2, P)
        w_inv = sbb("w_inv", NC, P)
        mv, a_hat = sbb("m_v", NC, P), sbb("a_hat", NC, P)
        state, state_p, u_row = (sbb(n, P) for n in ("state", "state_decayed", "u_rows"))
        y_sum, y_mean, y_var = sbb("y_sum", NC), sbb("y_mean", NC), sbb("y_var", NC)
        b_con = sbb("masks", CON_OF["rwkv"][1])
        b_ar = sbb("a_r", NC, 2, C)
        b_b, b_k, b_v, b_a = (sbb(n, NC, P) for n in ("b_diag", "k_diag", "v_diag", "a_diag"))
        n_lvl = sbr("n_levels", LEVEL_BUFS, NC, P)
        Z_LOW = ExitStack()

        def z_low(n, tiles):
            t = Z_LOW.enter_context(nc.sbuf_tensor(f"z_low_{n}", [P, tiles, L], mybir.dt.float32r))
            Z_LOW.close()
            return t
        z_low_c = z_low("c", 4)
        i_less_w = sbb("i_less_w", NC, P)
        b_r = sbb("r_diag", 2, NC, P)
        b_sgbon, b_pc = sbb("gate_bonus", 2, 2, LP), sbb("p_chunk", 2, NC)
        z_low_a = z_low("a", 6)
        mg = sbb("k_with_a_r", 2, NC, 2, P)
        z_low_b = z_low("b", 8)
        tokens_of = sbb("token_rows", 2, 4, NC, P)
        y_rows, y_sq, y_ln = sbb("y_rows", NC, C), sbb("y_sq", NC, C), sbb("y_ln", NC, C)
        y_diag = sbb("y_diag", NC, P)
        B.close()
        inv_bank = [wide[0][:, 0, :], wide[0][:, 1, :], wide[1][:, 0, :]]
        state_bank, chunk_bank, y_bank, post_bank = wide[2][:, 0, :], wide[2][:, 1, :], wide[3][:, 0, :], wide[3][:, 1, :]
        odd_bank = [wide[1][:, 1, :], post_bank]
        end_bank = [state_bank, chunk_bank, y_bank]
        b_names = ("forms_loaded", "qg_made", "mg_made", "token_mm", "token_rows", "n_turned", "n_rows",
                   "w_start", "x_start", "n_level", "e_mm", "e_rows", "w_mm", "w_added", "x_mm", "x_rows", "f_mm", "lack", "v_mm", "w_done", "i_less_w", "m_mm", "m_rows", "a_mm", "a_rows",
                   "u_mm", "u_rows", "s_mm", "s_rows", "y_mm", "y_rows", "g_mm", "k_mm", "post", "y_rooted", "y_turned", "z_sum",
                   "z_made", "z_stored", "diag_set", "early_set", "late_set")
        sb_ = {n: sem("b_" + n) for n in b_names}
        q = sb_
        HEAD_ROWS = (slice(0, C), slice(C, P))
        N_DIAG = 1
        POST = 15

        def three(ap):
            return ap[:, 0:GC * P].rearrange("p (c n) -> p c n", c=GC)

        def grp(g):
            return slice(g * GC, (g + 1) * GC)

        def mask(name, n=0):
            at = CON[name] - CON_OF["rwkv"][0] + n * P
            return b_con[:, at:at + P].unsqueeze(1).to_broadcast([P, GC, P])

        eye = ident.unsqueeze(1).to_broadcast([P, GC, P])
        tri_at = CON["tri"] - CON_OF["rwkv"][0]
        tri = b_con[:, tri_at:tri_at + 2 * C].rearrange("p (s n) -> p s n", s=2)

        def sp_diag(sp, dst, pair, col, sem_):
            for hd, rows in enumerate(HEAD_ROWS):
                sp.dma_start(dst[rows, :, hd * C:(hd + 1) * C], forms[pair, rows, col:col + LP].rearrange("p (c n) -> p c n", c=NC)).then_inc(sem_, 16)

        def ar_of(pair, rows):
            return forms[pair, rows, F_AR:F_AR + 2 * LP].rearrange("p (c s n) -> p c s n", c=NC, s=2)

        def sp_forms(sp, i):
            if not is0(i):
                sp.wait_ge(q["token_mm"], 12 * i)
            sp.dma_start(b_ar[:], forms[i, :, F_AR:F_AR + 2 * LP].rearrange("p (c s n) -> p c s n", c=NC, s=2)).then_inc(q["forms_loaded"], 16)
            for dst, col in ((b_b, F_B), (b_k, F_K), (b_v, F_V)):
                sp_diag(sp, dst, i, col, q["forms_loaded"])
            for hd, rows in enumerate(HEAD_ROWS):
                sp.dma_start(b_a[rows, :, hd * C:(hd + 1) * C], ar_of(i, rows)[:, :, 0, :]).then_inc(q["forms_loaded"], 16)

        def sp_scan(sp, i, par_, post):
            if post:
                sp.wait_ge(q["y_mm"], 9 * (i - 1))
                sp.wait_ge(q["s_rows"], 9 * (i - 1))
            for hd, rows in enumerate(HEAD_ROWS):
                sp.dma_start(b_r[rows, par_, :, hd * C:(hd + 1) * C], ar_of(i, rows)[:, :, 1, :]).then_inc(scan_loaded[par_], 16)
            sp.dma_start(b_pc[:, par_, :], forms[i, :, F_PC:F_PC + NC]).then_inc(scan_loaded[par_], 16)
            if post:
                sp_z(sp, i - 2, par_)
                sp.wait_ge(q["z_stored"], 16 * (i - 1))
            sp.dma_start(b_sgbon[:, par_], forms[i, :, F_SG:F_SG + 2 * LP].rearrange("p (s n) -> p s n", s=2)).then_inc(scan_loaded[par_], 16)

        FORMS_DMAS, SCAN_DMAS = 16 * 9, 16 * 4

        def sp_z(sp, pair, par_):
            sp.wait_ge(q["z_made"], pair + 1)
            sp.dma_start(mixed[pair], b_sgbon[:, par_, 0, PAD:]).then_inc(q["z_stored"], 16)

        scan_loaded = [sem("b_scan_loaded0"), sem("b_scan_loaded1")]

        def wait_scan(eng, pair, parity):
            eng.wait_ge(scan_loaded[parity], SCAN_DMAS // 2 * pair + (SCAN_DMAS // 2 if parity else SCAN_DMAS))

        def is0(i):
            return isinstance(i, int) and i == 0

        def merged(first, second):
            out, done = [], [0, 0]
            total = [max(sum(item[2] for item in part), 1) for part in (first, second)]
            parts = [list(first), list(second)]
            while parts[0] or parts[1]:
                n = 0 if not parts[1] or (parts[0] and done[0] * total[1] <= done[1] * total[0]) else 1
                name, arg, weight = parts[n].pop(0)
                out.append((name, arg))
                done[n] += weight
            return out

        NORM_AT = 8

        def schedule(inv, scan, post):
            setup, levels, ending, walk, norm = [], [], [], [], []
            if inv:
                setup = [("G", g, 3) for g in range(GROUPS)] + [("K", g, 3) for g in range(GROUPS)]
                setup += [("T", g, 2) for g in range(GROUPS)] + [("start", g, 0) for g in range(GROUPS)]
            if post:
                setup += [("stats", 0, 0)]
                norm = [("post", g, 2) for g in range(GROUPS)]
            if inv:
                setup += [("rows", n, 2) for n in range(NORM_AT)]
            if post:
                setup += [("norm", 0, 0)]
            if inv:
                setup += [("rows", n, 2) for n in range(NORM_AT, 12)]
                for lv in range(LEVELS):
                    for g in range(GROUPS):
                        levels += [("E", (lv, g), 1)] + [("X", (lv - 1, g), 1)] * (lv > 0)
                    levels += [("W", (lv, g), 1) for g in range(GROUPS)]
                levels += [("X", (LEVELS - 1, g), 1) for g in range(GROUPS)]
            if scan:
                ending = [(name, g, 1 if name == "V" else 3) for name in "FVMA" for g in range(GROUPS)]
                walk = [("walk", divmod(n, 2), 3) for n in range(2 * NC)]
            return merged(ending, setup) + merged(walk, norm + levels)

        def pe_pass(pe, i, par_, inv, scan, post):
            p = i - 1
            pw = 1 - par_

            def walk(c, part):
                v = tokens_of[:, pw, 2, c, :]
                if part == 0:
                    if c == 0:
                        wait_scan(pe, p, pw)
                        pe.wait_ge(q["a_rows"], GROUPS * i)
                    mm = pe.matmul(chunk_bank[:, 0:P], w_inv[:, c, :], mv[:, c, :], start=True, stop=c == 0)
                    if c > 0:
                        pe.wait_ge(q["s_rows"], 9 * p + c)
                        mm = pe.matmul(chunk_bank[:, 0:P], a_hat[:, c, :], state[:], start=False, stop=True)
                    mm.then_inc(q["u_mm"], 1)
                    pe.matmul(state_bank[:, 0:P], tokens_of[:, pw, 1, c, :], v, start=True, stop=False)
                    if c > 0:
                        pe.wait_ge(q["y_rows"], 9 * p + c)
                        pe.matmul(y_bank[:, 0:P], b_r[:, pw, c, :], state[:], start=True, stop=False)
                    pe.matmul(y_bank[:, 0:P], mg[:, pw, c, 1, :], v, start=c == 0, stop=False)
                else:
                    pe.wait_ge(q["u_rows"], 9 * p + c + 1)
                    pe.matmul(state_bank[:, 0:P], tokens_of[:, pw, 0, c, :], u_row[:], start=False, stop=True).then_inc(q["s_mm"], 1)
                    pe.matmul(y_bank[:, 0:P], qg[:, pw, c, 1, :], u_row[:], start=False, stop=True).then_inc(q["y_mm"], 1)

            def group(out, lhsT, rhs, g, done):
                for c in range(GC):
                    mm = pe.matmul(out[:, c * P:(c + 1) * P], lhsT(g * GC + c), rhs(g * GC + c), start=True, stop=True)
                mm.then_inc(done, 1)

            def turn(out, src, done):
                for c in range(GC):
                    mm = pe.transpose(out[:, c * P:(c + 1) * P], src(c), ident)
                mm.then_inc(done, 1)

            for item, arg in schedule(inv, scan, post):
                if item == "walk":
                    walk(*arg)
                elif item == "G":
                    if arg == 0:
                        pe.wait_ge(q["forms_loaded"], FORMS_DMAS * i + FORMS_DMAS)
                        if is0(i):
                            pe.wait_ge(DVE_A.sem, DVE_A.before(PAIRS))
                        if not is0(i):
                            pe.wait_ge(q["w_added"], 15 * i)
                    group(inv_bank[arg], lambda c: b_b[:, c, :], lambda c: b_ar[:, c], arg, q["g_mm"])
                elif item == "K":
                    if arg == 0 and not is0(i):
                        pe.wait_ge(q["x_rows"], 15 * i)
                    if arg == 2:
                        pe.wait_ge(q["mg_made"], GROUPS * i + 1)
                    group(odd_bank[arg % 2], lambda c: b_k[:, c, :], lambda c: b_ar[:, c], arg, q["k_mm"])
                elif item == "T":
                    pe.wait_ge(q["qg_made"], GROUPS * i + arg + 1)
                    turn(inv_bank[arg], lambda c: qg[:, par_, arg * GC + c, 0, :], q["n_turned"])
                elif item == "rows":
                    src = (b_b, b_k, b_v, b_a)[arg // 3]
                    if arg < 2:
                        pe.wait_ge(q["mg_made"], GROUPS * i + arg + 2)
                    else:
                        pe.wait_ge(q["token_rows"], 12 * i + arg - 1)
                    turn(odd_bank[(arg + 1) % 2], lambda c: src[:, arg % 3 * GC + c, :], q["token_mm"])
                elif item == "post":
                    if inv and arg == 0:
                        pe.wait_ge(q["token_rows"], 12 * i + 12)
                    pe.wait_ge(q["post"], POST * (i - 2) + 9 + 2 * arg)
                    turn(post_bank, lambda c: y_diag[:, arg * GC + c, :], q["y_turned"])
                elif item == "E":
                    lv, g = arg
                    if lv == 0:
                        pe.wait_ge(q["n_rows"], GROUPS * i + g + 1)
                        pe.wait_ge(q["w_start"], 6 * i + 2 * g + 2)
                    else:
                        pe.wait_ge(q["w_added"], 15 * i + 3 * (lv - 1) + g + 1)
                    pe.wait_ge(q["n_level"], 15 * i + 3 * lv + g + 1)
                    group(inv_bank[g], lambda c: n_lvl[:, lv % LEVEL_BUFS, c, :], lambda c: w_rnd[:, c, :], g, q["e_mm"])
                elif item == "W":
                    lv, g = arg
                    pe.wait_ge(q["e_rows"], 15 * i + 3 * lv + g + 1)
                    if lv == 0:
                        pe.wait_ge(q["x_start"], 6 * i + 2 * g + 2)
                    else:
                        pe.wait_ge(q["x_rows"], 15 * i + 3 * (lv - 1) + g + 1)
                    group(inv_bank[g], lambda c: x_rnd[:, c, :], lambda c: e_rnd[:, c, :], g, q["w_mm"])
                elif item == "X":
                    lv, g = arg
                    if lv == 0 and g == 0:
                        pe.wait_ge(q["token_rows"], 12 * i + 12)
                    if lv == 0 and g == 1 and post:
                        pe.wait_ge(q["post"], POST * (i - 2) + 15)
                    if g == 2:
                        pe.wait_ge(q["x_rows"], 15 * i + 3 * lv + 1)
                    pe.wait_ge(q["w_added"], 15 * i + 3 * lv + g + 1)
                    turn(odd_bank[g % 2], lambda c: w_rnd[:, g * GC + c, :].bitcast(F32), q["x_mm"])
                elif item == "F":
                    pe.wait_ge(q["w_added"], 15 * p + 12 + arg + 1)
                    if arg == 0 and not is0(p):
                        pe.wait_ge(q["u_rows"], 9 * p)
                        pe.wait_ge(q["s_rows"], 9 * p)
                        pe.wait_ge(q["y_rows"], 9 * p)
                    group(end_bank[arg], lambda c: n_all[:, c, :], lambda c: w_rnd[:, c, :].bitcast(F32), arg, q["f_mm"])
                elif item == "V":
                    pe.wait_ge(q["lack"], GROUPS * p + arg + 1)
                    pe.wait_ge(q["x_rows"], 15 * p + 12 + arg + 1)
                    group(end_bank[arg], lambda c: x_rnd[:, c, :], lambda c: e_rnd[:, c, :], arg, q["v_mm"])
                elif item == "M":
                    pe.wait_ge(q["w_done"], GROUPS * p + arg + 1)
                    pe.wait_ge(q["mg_made"], GROUPS * p + arg + 1)
                    pe.wait_ge(q["token_rows"], 12 * p + 12)
                    group(end_bank[arg], lambda c: mg[:, pw, c, 0, :], lambda c: tokens_of[:, pw, 2, c, :], arg, q["m_mm"])
                elif item == "A":
                    pe.wait_ge(q["m_rows"], GROUPS * p + arg + 1)
                    group(end_bank[arg], lambda c: tokens_of[:, pw, 3, c, :], lambda c: w_inv[:, c, :], arg, q["a_mm"])

        def act_pass(act, i, par_, inv, scan, post):
            p = i - 1

            def walk(c, part):
                if part == 0:
                    act.wait_ge(q["u_mm"], 9 * p + c + 1)
                    act.activation(u_row[:], chunk_bank[:, 0:P], ACT.Copy).then_inc(q["u_rows"], 1)
                else:
                    act.wait_ge(q["y_mm"], 9 * p + c + 1)
                    if c == 0 and not is0(p):
                        act.wait_ge(q["post"], POST * (p - 1) + 3)
                    for hd, rows in enumerate(HEAD_ROWS):
                        ins = act.activation(y_rows[rows, c, :], y_bank[rows, hd * C:(hd + 1) * C], ACT.Copy)
                    ins.then_inc(q["y_rows"], 1)

            for item, arg in schedule(inv, scan, post):
                if item == "walk":
                    walk(*arg)
                elif item == "T":
                    if arg == 0 and not is0(i):
                        act.wait_ge(q["n_level"], 15 * i)
                        act.wait_ge(q["f_mm"], GROUPS * i)
                    act.wait_ge(q["n_turned"], GROUPS * i + arg + 1)
                    act.activation(n_all[:, grp(arg), :], three(inv_bank[arg]), ACT.Copy).then_inc(q["n_rows"], 1)
                elif item == "rows":
                    if arg == 0 and is0(i):
                        act.wait_ge(s["stored"], 16 * PAIRS)
                    act.wait_ge(q["token_mm"], 12 * i + arg + 1)
                    act.activation(tokens_of[:, par_, arg // 3, grp(arg % 3), :], three(odd_bank[(arg + 1) % 2]), ACT.Copy).then_inc(q["token_rows"], 1)
                elif item == "norm":
                    act.wait_ge(q["post"], POST * (i - 2) + 6)
                    act.activation(y_var[:], y_var[:], ACT.Sqrt, bias=epsilon[:, 1:2], scale=1.0 / C).then_inc(q["y_rooted"], 1)
                elif item == "E":
                    lv, g = arg
                    act.wait_ge(q["e_mm"], 15 * i + 3 * lv + g + 1)
                    act.activation(e_rnd[:, grp(g), :], three(inv_bank[g]), ACT.Copy).then_inc(q["e_rows"], 1)
                elif item == "X":
                    lv, g = arg
                    act.wait_ge(q["x_mm"], 15 * i + 3 * lv + g + 1)
                    act.activation(x_rnd[:, grp(g), :], three(odd_bank[g % 2]), ACT.Copy).then_inc(q["x_rows"], 1)
                elif item == "M":
                    act.wait_ge(q["m_mm"], GROUPS * p + arg + 1)
                    act.activation(mv[:, grp(arg), :], three(end_bank[arg]), ACT.Copy).then_inc(q["m_rows"], 1)
                elif item == "A":
                    act.wait_ge(q["a_mm"], GROUPS * p + arg + 1)
                    act.activation(a_hat[:, grp(arg), :], three(end_bank[arg]), ACT.Copy).then_inc(q["a_rows"], 1)

        def dve_pass(dve, i, par_, inv, scan, post):
            p = i - 1
            pw = 1 - par_

            def walk(c, part):
                if part == 1:
                    if c == 0:
                        wait_scan(dve, p, pw)
                    dve.wait_ge(q["s_mm"], 9 * p + c + 1)
                    decay = b_pc[:, pw, c:c + 1]
                    if c == 0:
                        dve.tensor_scalar(state[:], state_bank[:, 0:P], decay, None, ALU.mult).then_inc(q["s_rows"], 1)
                    else:
                        dve.wait_ge(q["z_sum"], 8 * p + c)
                        dve.scalar_tensor_tensor(state[:], state_bank[:, 0:P], decay, state_p[:], ALU.mult, ALU.add).then_inc(q["s_rows"], 1)
                    if c < NC - 1:
                        dve.wait_ge(q["s_rows"], 9 * p + c + 1)
                        dve.tensor_scalar(state_p[:], state[:], b_pc[:, pw, c + 1:c + 2], None, ALU.mult).then_inc(q["z_sum"], 1)

            def masked(src, dst, g, made):
                for hd, rows in enumerate(HEAD_ROWS):
                    ins = dve.tensor_tensor(dst[rows, par_, grp(g), :, hd * C:(hd + 1) * C],
                                            src[rows, 0:GC * P].rearrange("p (c s n) -> p c s n", c=GC, s=2),
                                            tri[rows].unsqueeze(1).to_broadcast([C, GC, 2, C]), ALU.mult)
                ins.then_inc(made, 1)

            for item, arg in schedule(inv, scan, post):
                if item == "walk":
                    walk(*arg)
                elif item == "G":
                    dve.wait_ge(q["g_mm"], GROUPS * i + arg + 1)
                    masked(inv_bank[arg], qg, arg, q["qg_made"])
                elif item == "K":
                    dve.wait_ge(q["k_mm"], GROUPS * i + arg + 1)
                    masked(odd_bank[arg % 2], mg, arg, q["mg_made"])
                elif item == "stats":
                    dve_stats(dve, i - 2)
                elif item in ("norm", "post"):
                    dve_post(dve, i - 2, par_, item, arg)
                elif item == "W":
                    lv, g = arg
                    dve.wait_ge(q["w_mm"], 15 * i + 3 * lv + g + 1)
                    w = w_rnd[:, grp(g), :]
                    dve.tensor_tensor(w, three(inv_bank[g]), w.bitcast(F32), ALU.add).then_inc(q["w_added"], 1)
                elif item == "start":
                    if arg == 0 and is0(i):
                        dve.wait_ge(con_loaded, 48)
                    elif arg == 0:
                        dve.wait_ge(q["w_done"], GROUPS * i)
                    dve.wait_ge(q["qg_made"], GROUPS * i + arg + 1)
                    w = w_rnd[:, grp(arg), :]
                    dve.tensor_tensor(w, qg[:, par_, grp(arg), 0, :], mask("level0T"), ALU.mult).then_inc(q["w_start"], 1)
                    dve.wait_ge(q["w_start"], 6 * i + 2 * arg + 1)
                    dve.tensor_tensor(w, w.bitcast(F32), eye, ALU.add).then_inc(q["w_start"], 1)
                elif item == "F":
                    dve.wait_ge(q["f_mm"], GROUPS * p + arg + 1)
                    dve.wait_ge(q["i_less_w"], GROUPS * p + arg + 1)
                    dve.tensor_tensor(e_rnd[:, grp(arg), :], three(end_bank[arg]), i_less_w[:, grp(arg), :], ALU.add).then_inc(q["lack"], 1)
                elif item == "V":
                    dve.wait_ge(q["v_mm"], GROUPS * p + arg + 1)
                    dve.tensor_tensor(w_inv[:, grp(arg), :], three(end_bank[arg]), w_rnd[:, grp(arg), :].bitcast(F32), ALU.add).then_inc(q["w_done"], 1)

        def dve_stats(dve, p):
            def step(ins):
                ins.then_inc(q["post"], 1)

            def after(k):
                dve.wait_ge(q["post"], POST * p + k)

            dve.wait_ge(q["y_rows"], 9 * p + 9)
            step(dve.tensor_reduce(y_sum[:], y_rows[:], AX_X, ALU.add))
            after(1)
            step(dve.tensor_scalar(y_mean[:], y_sum[:], 1.0 / C, None, ALU.mult))
            after(2)
            step(dve.tensor_tensor(y_sq[:], y_rows[:], y_mean[:].unsqueeze(2).to_broadcast([P, NC, C]), ALU.subtract))
            after(3)
            step(dve.tensor_tensor(y_ln[:], y_sq[:], y_sq[:], ALU.mult))
            after(4)
            step(dve.tensor_reduce(y_sum[:], y_ln[:], AX_X, ALU.add))
            after(5)
            step(dve.tensor_copy(y_var[:], y_sum[:]))

        def dve_post(dve, p, pp, item, g):
            def step(ins):
                ins.then_inc(q["post"], 1)

            def after(k):
                dve.wait_ge(q["post"], POST * p + k)

            if item == "norm":
                dve.wait_ge(q["y_rooted"], p + 1)
                step(dve.reciprocal(y_mean[:], y_var[:]))
                after(7)
                for hd, rows in enumerate(HEAD_ROWS):
                    step(dve.tensor_tensor(y_diag[rows, :, hd * C:(hd + 1) * C], y_sq[rows],
                                           y_mean[rows].unsqueeze(2).to_broadcast([C, NC, C]), ALU.mult))
                return
            dve.wait_ge(q["y_turned"], GROUPS * p + g + 1)
            for hd, rows in enumerate(HEAD_ROWS):
                step(dve.tensor_scalar(y_ln[rows, grp(g), :], three(post_bank)[rows, :, hd * C:(hd + 1) * C],
                                       rw(LNW, p)[rows], rw(LNB, p)[rows], ALU.mult, ALU.add))
            if g < GROUPS - 1:
                return
            after(15)
            gate, bonus = b_sgbon[:, pp, 0, PAD:], b_sgbon[:, pp, 1, PAD:]
            y = y_ln[:].rearrange("p c n -> p (c n)")[:, PAD:]
            wait_scan(dve, p, pp)
            dve.tensor_tensor(bonus, y, bonus, ALU.add).then_inc(q["diag_set"], 1)
            dve.wait_ge(q["diag_set"], N_DIAG + p + 1)
            dve.scalar_tensor_tensor(gate, bonus, 0.5, gate, ALU.mult, ALU.mult).then_inc(q["z_made"], 1)

        def pool_pass(pool, i, par_, inv, scan, post):
            if not inv:
                return
            if is0(i):
                pool.wait_ge(con_loaded, 48)
            else:
                pool.wait_ge(q["v_mm"], GROUPS * i)
            for g in range(GROUPS):
                pool.wait_ge(q["n_rows"], GROUPS * i + g + 1)
                pool.tensor_tensor(n_lvl[:, 0, grp(g), :], n_all[:, grp(g), :], mask("levels", 1), ALU.mult).then_inc(q["n_level"], 1)
                x = x_rnd[:, grp(g), :]
                pool.tensor_tensor(x, n_all[:, grp(g), :], mask("levels", 0), ALU.mult).then_inc(q["x_start"], 1)
                pool.wait_ge(q["x_start"], 6 * i + 2 * g + 1)
                pool.tensor_tensor(x, x.bitcast(F32), eye, ALU.add).then_inc(q["x_start"], 1)
            for lv in range(1, LEVELS):
                for g in range(GROUPS):
                    if lv >= LEVEL_BUFS:
                        pool.wait_ge(q["e_mm"], 15 * i + 3 * (lv - LEVEL_BUFS) + g + 1)
                    pool.tensor_tensor(n_lvl[:, lv % LEVEL_BUFS, grp(g), :], n_all[:, grp(g), :], mask("levels", lv + 1), ALU.mult).then_inc(q["n_level"], 1)
            for g in range(GROUPS):
                pool.wait_ge(q["w_added"], 15 * i + 12 + g + 1)
                pool.tensor_tensor(i_less_w[:, grp(g), :], eye, w_rnd[:, grp(g), :].bitcast(F32), ALU.subtract).then_inc(q["i_less_w"], 1)

        def dve_b_setup(dve):
            dve.wait_ge(DVE_A.sem, DVE_A.before(PAIRS))
            dve.wait_ge(POOL_A.sem, POOL_A.before(PAIRS))
            dve.wait_ge(s["pc_copied"], PAIRS)
            dve.memset(qg[:], 0.0).then_inc(q["diag_set"], 1)
            dve.wait_ge(q["diag_set"], N_DIAG)
            dve.wait_ge(con_loaded, 48)
            dve.wait_ge(q["late_set"], 3)

        def pool_b_early(pool):
            ring.wait_used(pool, SPLIT, PAIRS - 1)
            for t in (b_b, b_k, b_v, b_a):
                pool.memset(t[:], 0.0).then_inc(q["early_set"], 1)

        def pool_b_setup(pool):
            pool.wait_ge(s["rk_summed"], PAIRS)
            for t in (mg, b_r, y_diag):
                pool.memset(t[:], 0.0).then_inc(q["late_set"], 1)

        def passes(eng, body):
            body(eng, 0, 0, True, False, False)
            body(eng, 1, 1, True, True, False)
            with eng.Fori(1, PAIRS // 2) as j:
                body(eng, 2 * j, 0, True, True, True)
                body(eng, 2 * j + 1, 1, True, True, True)
            body(eng, PAIRS, 0, False, True, True)
            body(eng, PAIRS + 1, 1, False, False, True)

        def sp_b(sp):
            sp.wait_ge(q["late_set"], 3)
            sp_scan(sp, 0, 0, False)
            sp_forms(sp, 1)
            sp_scan(sp, 1, 1, False)
            with sp.Fori(1, PAIRS // 2) as j:
                for par_ in range(2):
                    sp_forms(sp, 2 * j + par_)
                    sp_scan(sp, 2 * j + par_, par_, True)

        h = sb("h", KD, L)
        R = ExitStack()
        u_lo = R.enter_context(nc.sbuf_tensor("u_low_second", [P, KD, L], mybir.dt.float32r))
        R.close()
        y_lo = R.enter_context(nc.sbuf_tensor("y_low_mla", [P, KI - SLOTS, L], mybir.dt.float32r))
        R.close()
        m_t = sb("mixer_out", KD, L)
        w_rwkv = [R.enter_context(nc.sbuf_tensor(f"w_{n}_rwkv_out", [P, 2, SLOT], mybir.dt.float32r)) for n in ("high", "low")]
        R.close()
        u2 = sb("normed", KD, L)
        sq = sb("squares", 2, L)
        sq_sum = sb("sq_sum", L)
        tile_left, sq_made, sq_added = (sem(n) for n in ("tile_left", "sq_made", "sq_added"))
        n_summed, n_rooted, n_inverted, n_applied, n_used = (sem(n) for n in ("n_summed", "n_rooted", "n_inverted", "n_applied", "n_used"))
        h_added = sem("h_added")

        class Seen:
            def __init__(self):
                self.left = self.squares = self.added = self.norms = self.h = self.u = self.splits = 0

        seen = {who: Seen() for who in ("pe", "act", "dve")}
        seen["pe"].splits = SPLIT * (PAIRS - 1)

        def tokens(ap, width):
            return ap if width == L else ap[:, META:]

        def tile_ps(t, width):
            return wide[t][:, :, 0:HALF] if width == L else wide[t][:, 0, 0:width]

        def over_tiles(eng, count, per_turn, body):
            with eng.Fori(0, count // per_turn) as j:
                for t in range(per_turn):
                    body(j, t, per_turn * j + t)

        def pe_tiles(pe, load, count, kt, rhs, width, loop=True, after=None, ready=None, split=None, order=None):
            st, per = seen["pe"], kt // KD
            splits = st.splits
            st.splits += count * per if split else 0
            turn = SLOTS // per

            def tile(j, t, n):
                pe.wait_ge(tile_left, st.left + n + 1)
                for i, k in enumerate(order or range(kt)):
                    at = load + per * t + k // KD
                    if i % KD == 0:
                        if split:
                            pe.wait_ge(w_split, splits + per * n + i // KD + 1)
                        else:
                            ring.wait_full(pe, at, j)
                    if ready is not None:
                        ready(i)
                    cols = slice(k % KD * P, (k % KD + 1) * P)
                    for b in range(2 if width == L else 1):
                        dst = wide[t][:, b, 0:HALF if width == L else width]
                        if split:
                            mm = split_products(pe, dst, [w[:, at % 2, cols] for w in split], rhs(k, b), i == 0, i == kt - 1)
                        else:
                            mm = pe.matmul(dst, ring.slot(at)[:, cols], rhs(k, b), start=i == 0, stop=i == kt - 1)
                    if i % KD == KD - 1:
                        mm.then_inc(ring.done(at), 1)
                if after:
                    after(n, t)

            if loop:
                over_tiles(pe, count, turn, tile)
            else:
                for n in range(count):
                    tile(n // turn, n % turn, n)
            st.left += count + turn

        def split_products(pe, dst, w, x, start, stop):
            pe.matmul(dst, w[0], x[0], start=start, stop=False)
            pe.matmul(dst, w[0], x[1], start=False, stop=False)
            return pe.matmul(dst, w[1], x[0], start=False, stop=stop)

        def normed(pe, before):
            return lambda i: pe.wait_ge(u_low[i % 2], (before + i) // 2 + 1)

        def pool_split_y(pool, src, hi, lo, n):
            pool.tensor_tensor(hi.rearrange("p (a b) -> p a b", b=P), src.rearrange("p (a b) -> p a b", b=P),
                               ones.unsqueeze(1).to_broadcast([P, SEQ // P, P]), ALU.mult).then_inc(y_high, 1)
            pool.wait_ge(y_high, n + 1)
            pool.tensor_tensor(lo, src, hi.bitcast(F32), ALU.subtract).then_inc(y_split, 1)

        def pool_split(pool, loads, parts):
            first, count = loads
            w_hi, w_lo = parts
            base = splits_made[0]
            splits_made[0] += count

            def one(load, j, n):
                ring.wait_full(pool, load, j)
                ring.wait_used(pool, load - 2, j)
                pool.tensor_tensor(w_hi[:, load % 2, :].rearrange("p (k n) -> p k n", k=KD), ring.slot(load).rearrange("p (k n) -> p k n", k=KD),
                                   ones.unsqueeze(1).to_broadcast([P, KD, P]), ALU.mult).then_inc(w_high, 1)
                pool.wait_ge(w_high, base + n + 1)
                pool.tensor_tensor(w_lo[:, load % 2, :], ring.slot(load), w_hi[:, load % 2, :].bitcast(F32), ALU.subtract).then_inc(w_split, 1)
            turns = count // SLOTS
            if turns > 1:
                with pool.Fori(0, turns) as j:
                    for n in range(SLOTS):
                        one(first + n, j, SLOTS * j + n)
            for n in range(turns * SLOTS if turns > 1 else 0, count):
                one(first + n, 0, n)

        def act_split_u(act, u_parts, width):
            hi = u_parts[0]
            st = seen["act"]
            for k in range(KD):
                act.wait_ge(n_applied, st.u + k + 1)
                act.activation(hi[:, k, 0:width], u2[:, k, 0:width], ACT.Copy).then_inc(u_high, 1)

        def pool_split_u(pool, u_parts, width):
            for k in range(1, KD, 2):
                pool.wait_ge(u_high, splits_made[1] + k + 1)
                take_rest(pool, u_parts, k, width)
            splits_made[1] += KD

        def take_rest(eng, u_parts, k, width):
            hi, lo = u_parts
            eng.tensor_tensor(lo[:, k, 0:width], u2[:, k, 0:width], hi[:, k, 0:width].bitcast(F32), ALU.subtract).then_inc(u_low[k % 2], 1)

        splits_made = [SPLIT * (PAIRS - 1), 0]
        w_high, w_split, u_high, y_high, y_split = (sem(n) for n in ("w_high", "w_split", "u_high", "y_high", "y_split"))
        u_low = [sem("u_low_even"), sem("u_low_odd")]

        def act_tiles(act, load, count, kt, take, loop=True, before=None, prelude=None):
            st, per = seen["act"], kt // KD
            turn = SLOTS // per
            act.drain().then_inc(tile_left, turn)
            if prelude:
                prelude()

            def tile(j, t, n):
                if before:
                    before(n, t)
                ring.wait_used(act, load + per * t + per - 1, j)
                take(j, t, n)

            if loop:
                over_tiles(act, count, turn, tile)
            else:
                for n in range(count):
                    tile(n // turn, n % turn, n)
            st.left += count + turn

        def act_square(act, src, slot, n, width):
            st = seen["act"]
            act.wait_ge(sq_added, st.added + n + 1)
            return act.activation(halves(sq[:, slot, 0:width], width) if len(src.shape) == 3 else sq[:, slot, 0:width], src, ACT.Square).then_inc(sq_made, 1)

        def act_root(act, tiles, width):
            st = seen["act"]
            st.norms += 1
            st.squares += tiles
            st.added += tiles + 2
            act.wait_ge(n_summed, st.norms)
            if st.norms > 1:
                act.wait_ge(n_used, st.norms - 1)
            act.activation(halves(inv_rms[:, 0:width], width), tile_ps(3, width), ACT.Sqrt,
                           bias=epsilon[:, 0:1], scale=1.0 / (tiles * P)).then_inc(n_rooted, 1)

        def pe_norm_sum(pe, tiles, width):
            st = seen["pe"]
            st.norms += 1
            st.added += tiles + 2
            pe.wait_ge(sq_added, st.added)
            if st.norms > 1:
                pe.wait_ge(n_rooted, st.norms - 1)
            for b in range(2 if width == L else 1):
                n = HALF if width == L else width
                mm = pe.matmul(wide[3][:, b, 0:n], ones, sq_sum[:, b * n:(b + 1) * n], start=True, stop=True)
            mm.then_inc(n_summed, 1)

        def dve_sum_start(dve, width):
            st = seen["dve"]
            if st.norms:
                dve.wait_ge(n_summed, st.norms)
            dve.memset(sq_sum[:, 0:width], 0.0).then_inc(sq_added, 2)

        def dve_sum(dve, slot, n, width):
            st = seen["dve"]
            dve.wait_ge(sq_made, st.squares + n + 1)
            dve.wait_ge(sq_added, st.added + n + 2)
            dve.tensor_tensor(sq_sum[:, 0:width], sq_sum[:, 0:width], sq[:, slot, 0:width], ALU.add).then_inc(sq_added, 1)

        def dve_invert(dve, tiles, width):
            st = seen["dve"]
            st.norms += 1
            st.squares += tiles
            st.added += tiles + 2
            dve.wait_ge(n_rooted, st.norms)
            dve.reciprocal(inv_rms[:, 0:width], inv_rms[:, 0:width]).then_inc(n_inverted, 1)
            dve.wait_ge(n_inverted, st.norms)

        def dve_apply(dve, tiles, width, src, dst, gain, u_parts=None):
            st = seen["dve"]

            def rest(k):
                dve.wait_ge(u_high, st.u + k + 1)
                take_rest(dve, u_parts, k, width)
            for k in range(tiles):
                if u_parts and k % 2 == 0 and k >= 4:
                    rest(k - 4)
                dve.scalar_tensor_tensor(dst(k), src(k), pcol(gain, k), inv_rms[:, 0:width], ALU.mult, ALU.mult).then_inc(n_applied, 1)
            dve.drain().then_inc(n_used, 1)
            if u_parts:
                for k in range(tiles - 4, tiles, 2):
                    rest(k)
                st.u += tiles

        def h_of(k, width):
            return tokens(h[:, k, :], width)

        def pe_project_out(pe, load, kt, src, width, post, **split):
            pe_tiles(pe, load, KD, kt, src, width, **split)
            if post:
                pe_norm_sum(pe, KD, width)
            pe_norm_sum(pe, KD, width if not post else post)

        def act_project_out(act, load, kt, width, post, m=None, prelude=None):
            st = seen["act"]
            turn = SLOTS * KD // kt

            def take(j, t, n):
                dst = (m if post else u2)[:].rearrange("p k n -> p (k n)")[:, bass.ds(n * L, width)]
                if post:
                    act_square(act, tile_ps(t, width), t % 2, n, width)
                    act.activation(halves(dst, width), tile_ps(t, width), ACT.Copy).then_inc(tile_left, 1)
                else:
                    act.activation(dst, tile_ps(t, width), ACT.Copy).then_inc(tile_left, 1)
                    act.wait_ge(h_added, st.h + n + 1)
                    act_square(act, h[:].rearrange("p k n -> p (k n)")[:, bass.ds(n * L + META, width)], t % 2, n, width)
            act_tiles(act, load, KD, kt, take, prelude=prelude)
            if post:
                act_root(act, KD, width)
                for k in range(KD):
                    act.wait_ge(h_added, st.h + 2 * k + 2)
                    act_square(act, h_of(k, post), k % 2, k, post)
                st.h += KD
            st.h += KD
            act_root(act, KD, post if post else width)

        def dve_project_out(dve, kt, width, post, post_gain, gain, dst, u_parts=None, m=None):
            st = seen["dve"]
            turn = SLOTS * KD // kt
            dve_sum_start(dve, width)

            def take(j, t, n):
                if not post:
                    dve.wait_ge(tile_left, st.left + turn + n + 1)
                    hn = h[:].rearrange("p k n -> p (k n)")[:, bass.ds(n * L + META, width)]
                    mn = u2[:].rearrange("p k n -> p (k n)")[:, bass.ds(n * L, width)]
                    dve.tensor_tensor(hn, hn, mn, ALU.add).then_inc(h_added, 1)
                dve_sum(dve, t % 2, n, width)
            over_tiles(dve, KD, turn, take)
            st.left += KD + turn
            if post:
                dve_invert(dve, KD, width)
                dve_sum_start(dve, post)
                for k in range(KD):
                    dve.scalar_tensor_tensor(m[:, k, :], m[:, k, :], pcol(post_gain, k), inv_rms[:], ALU.mult, ALU.mult).then_inc(h_added, 1)
                    dve.wait_ge(h_added, st.h + 2 * k + 1)
                    ins = dve.tensor_tensor(h[:, k, :], h[:, k, :], m[:, k, :], ALU.add).then_inc(h_added, 1)
                    if k:
                        dve_sum(dve, (k - 1) % 2, k - 1, post)
                dve.drain().then_inc(n_used, 1)
                dve_sum(dve, (KD - 1) % 2, KD - 1, post)
                st.h += KD
            st.h += KD
            last = post if post else width
            dve_invert(dve, KD, last)
            dve_apply(dve, KD, last, lambda k: h_of(k, last), dst, gain, u_parts)

        M = ExitStack()

        def sm(name, *shape):
            return M.enter_context(nc.sbuf_tensor(name, [P, *shape], F32))

        def sm_rounded(name, *shape):
            return M.enter_context(nc.sbuf_tensor(name, [P, *shape], mybir.dt.float32r))

        M_EARLY = ExitStack()
        y_hi = M_EARLY.enter_context(nc.sbuf_tensor("y_high_mla", [P, KI, L], mybir.dt.float32r))
        M_EARLY.close()
        z_t = sm("gated", KI, L)
        y_lo_last = M_EARLY.enter_context(nc.sbuf_tensor("y_low_mla_last", [P, Q_TILES, L], mybir.dt.float32r))
        M_EARLY.close()
        latents = sm("latents", Q_TILES + KV_TILES, L)
        k_rope = sm("k_rope", L)
        Q_EDGES = [0] + list(range(META, L + 1, P))
        Q_BLOCKS = len(Q_EDGES) - 1
        m_con = sm("mla_tables", CON_OF["mla"][1])
        M_LATE = ExitStack()
        u_hi = M_LATE.enter_context(nc.sbuf_tensor("u_high_mla", [P, KD, L], mybir.dt.float32r))
        u_mla = (u_hi, M_LATE.enter_context(nc.sbuf_tensor("u_low_mla", [P, KD, L], mybir.dt.float32r)))
        w_parts = [M_LATE.enter_context(nc.sbuf_tensor(f"w_{n}_mla", [P, 2, SLOT], mybir.dt.float32r)) for n in ("high", "low")]
        M_LATE.close()
        m_mla = M_LATE.enter_context(nc.sbuf_tensor("mla_out", [P, KD, L], F32))
        M_LATE.close()
        v_rows = sm("v_rows", Q_BLOCKS, DI)
        P_AT = [sum(Q_EDGES[1:t + 1]) for t in range(Q_BLOCKS + 1)]
        probs = sm("probs", P_AT[-1])
        probs_t = sm("probs_turned", Q_BLOCKS, L)
        v_now = sm("v_now", 2, Q_BLOCKS, P)
        row_max, row_bias, row_sum = (sm(n, Q_BLOCKS) for n in ("row_max", "row_bias", "row_sum"))
        w_out = [sm_rounded(f"w_{n}_mla_out", 2, SLOT) for n in ("high", "low")]
        M.close()
        tanh_gate = [m_t[:, t, :] for t in range(SLOTS)]
        k_rope_raw, rope_cos = m_t[:, SLOTS, :], m_t[:, SLOTS + 1, :]
        q_nope, k_nope, q_rope, q_rope_raw = (u2[:, k, :] for k in range(4, KD))

        def mcon(name, width):
            at = CON[name] - CON_OF["mla"][0]
            return m_con[:, at:at + width]

        mixed_loaded, h_loaded, z_rounded, z_rest, z_whole = (sem(n) for n in ("mixed_loaded", "h_loaded", "z_rounded", "z_rest", "z_whole"))
        d = {n: sem("d_" + n) for n in ("gated", "rope_mm", "rope", "v_mm", "v_copied", "stats_set")}

        def sp_c(sp):
            sp.wait_ge(q["token_mm"], 12 * PAIRS)
            sp.wait_ge(q["e_mm"], 15 * PAIRS)
            sp.wait_ge(q["lack"], GROUPS * PAIRS)
            sp.wait_ge(q["z_stored"], 16 * (PAIRS - 2))
            for i in range(PAIRS - 2):
                sp.dma_start(z_t[:, i, :], mixed[i]).then_inc(mixed_loaded, 16)
            sp.wait_ge(q["w_done"], GROUPS * PAIRS)
            sp.dma_start(h[:], x_in).then_inc(h_loaded, 16)
            sp.wait_ge(z_rest, PAIRS - POOLED)
            first, n = CON_OF["mla"]
            sp.dma_start(m_con[:], con_in[:, first:first + n]).then_inc(con_loaded, 16)

        STORED, POOLED = PAIRS - 2, 6

        def z_low_of(k):
            if k == PAIRS - 1:
                return z_low_a[:, 5, :]
            return z_low_a[:, k, :] if k < 4 else z_low_b[:, k - 4, :] if k < 12 else z_low_c[:, k - 11, :]

        def z_parts(k, b):
            return [part[:, b * HALF:(b + 1) * HALF] for part in (y_hi[:, k, :], z_low_of(k))]

        def pe_c(pe):
            def ready(i):
                if i < POOLED:
                    pe.wait_ge(y_split, i + 1)
                else:
                    pe.wait_ge(z_whole if i < STORED else z_rest, i - POOLED + 1)
            pe_project_out(pe, FIRST["rwkv_out"], KI, z_parts, L, L, split=w_rwkv, ready=ready)

        def gated_pair(pair):
            return b_sgbon[:, pair % 2, 0, PAD:]

        def act_c(act):
            act.wait_ge(mixed_loaded, 16 * STORED)
            for k in range(POOLED, STORED):
                act.activation(z_low_of(k), z_t[:, k, :], ACT.Copy).then_inc(z_rounded, 1)
            for pair in range(STORED, PAIRS):
                act.wait_ge(q["z_made"], pair + 1)
                act.activation(y_hi[:, pair, :], gated_pair(pair), ACT.Copy).then_inc(z_rounded, 1)
            for k in range(POOLED, STORED):
                act.wait_ge(z_rest, k - POOLED + 1)
                act.activation(y_hi[:, k, :], z_t[:, k, :], ACT.Copy).then_inc(z_whole, 1)

        def dve_c(dve):
            dve.wait_ge(mixed_loaded, 16 * STORED)
            for k in range(POOLED, PAIRS):
                z, hi = (z_t[:, k, :], z_low_of(k)) if k < STORED else (gated_pair(k), y_hi[:, k, :])
                dve.wait_ge(z_rounded, k - POOLED + 1)
                dve.tensor_tensor(z_low_of(k), z, hi.bitcast(F32), ALU.subtract).then_inc(z_rest, 1)

        def pool_c(pool):
            pool.wait_ge(mixed_loaded, 16 * STORED)
            pool.wait_ge(q["y_mm"], NC * STORED + NC)
            pool.wait_ge(q["s_rows"], NC * STORED + NC)
            for k in range(POOLED):
                pool_split_tile(pool, z_t[:, k, :], y_hi[:, k, :], z_low_of(k))
            pool.wait_ge(q["y_mm"], NC * PAIRS)
            pool.wait_ge(q["s_rows"], NC * PAIRS)
            pool_split(pool, (FIRST["rwkv_out"], 2 * KD), w_rwkv)

        def pool_split_tile(pool, z, hi, lo):
            def rounded(dst):
                return pool.tensor_tensor(dst.rearrange("p (a b) -> p a b", a=11), z.rearrange("p (a b) -> p a b", a=11),
                                          ones[:, 0:L // 11].unsqueeze(1).to_broadcast([P, 11, L // 11]), ALU.mult)
            rounded(lo)
            pool.drain()
            pool.tensor_tensor(lo, z, lo.bitcast(F32), ALU.subtract)
            pool.drain()
            rounded(hi).then_inc(y_split, 1)


        def half_parts(u_parts):
            return lambda k, b: [ap[:, k, b * HALF:(b + 1) * HALF] for ap in u_parts]

        MLA_IN = FIRST["mla_in"]
        MLA_GATE = MLA_IN + Q_TILES + KV_TILES + 1

        def pe_mla_in(pe):
            st = seen["pe"]
            pe_tiles(pe, MLA_IN, Q_TILES, KD, half_parts(u_mla), L, loop=False, ready=normed(pe, 0), split=w_parts)
            pe.wait_ge(tile_left, st.left)
            pe_norm_sum(pe, Q_TILES, L)
            pe_tiles(pe, MLA_IN + Q_TILES, KV_TILES + 1, KD, half_parts(u_mla), L, loop=False, split=w_parts)
            pe.wait_ge(con_loaded, 64)
            pe.wait_ge(tile_left, st.left)
            for b in range(2):
                mm = pe.matmul(wide[2][:, b, 0:HALF], mcon("rot_mla", P), k_rope_raw[:, b * HALF:(b + 1) * HALF], start=True, stop=True)
            mm.then_inc(d["rope_mm"], 1)
            pe_norm_sum(pe, KV_TILES, L)
            pe.wait_ge(d["rope"], 2)
            pe_tiles(pe, MLA_GATE, KI, KD, half_parts(u_mla), L, split=w_parts)
            pe.wait_ge(tile_left, st.left)
            pe.wait_ge(n_used, st.norms)
            n = 0
            for c in range(4):
                load = FIRST["mla_v"] + c
                ring.wait_full(pe, load)
                for t in range(Q_BLOCKS):
                    rows = Q_EDGES[t + 1] - Q_EDGES[t]
                    if n >= 8:
                        pe.wait_ge(d["v_copied"], n - 7)
                    for k in range(KV_TILES):
                        mm = pe.matmul(wide[n // 2 % 4][0:rows, n % 2, :], latents[:, Q_TILES + k, Q_EDGES[t]:Q_EDGES[t + 1]],
                                       ring.slot(load)[:, k * 512:(k + 1) * 512], start=k == 0, stop=k == KV_TILES - 1)
                    mm.then_inc(d["v_mm"], 1)
                    n += 1
                pe.drain().then_inc(ring.done(load), 1)

        def act_mla_in(act):
            st = seen["act"]
            flat = z_t[:].rearrange("p k n -> p (k n)")

            def latent(first):
                def take(j, t, n):
                    if first + n < Q_TILES + KV_TILES:
                        act_square(act, tile_ps(t, L), n % 2, n, L)
                        dst = latents[:, first + n, :]
                    else:
                        dst = k_rope_raw
                    act.activation(halves(dst, L), tile_ps(t, L), ACT.Copy).then_inc(tile_left, 1)
                return take
            act_tiles(act, MLA_IN, Q_TILES, KD, latent(0), loop=False, prelude=lambda: act_split_u(act, u_mla, L))
            st.u += KD + Q_TILES + KV_TILES
            act_root(act, Q_TILES, L)
            act_tiles(act, MLA_IN + Q_TILES, KV_TILES + 1, KD, latent(Q_TILES), loop=False)
            act_root(act, KV_TILES, L)

            def gate(j, t, n):
                act.wait_ge(d["gated"], n + 1)
                act.activation(halves(tanh_gate[t], L), tile_ps(t, L), ACT.Tanh, scale=0.5)
                act.activation(halves(flat[:, bass.ds(n * L, L)], L), tile_ps(t, L), ACT.Copy).then_inc(tile_left, 1)
            act_tiles(act, MLA_GATE, KI, KD, gate)
            n = 0
            for c in range(4):
                for t in range(Q_BLOCKS):
                    rows = Q_EDGES[t + 1] - Q_EDGES[t]
                    act.wait_ge(d["v_mm"], n + 1)
                    act.activation(v_rows[0:rows, t, c * 512:(c + 1) * 512], wide[n // 2 % 4][0:rows, n % 2, :], ACT.Copy).then_inc(d["v_copied"], 1)
                    n += 1

        def dve_mla_in(dve):
            st = seen["dve"]
            flat = z_t[:].rearrange("p k n -> p (k n)")
            for t in (row_max, row_bias, row_sum):
                dve.memset(t[:], 1.0).then_inc(d["stats_set"], 1)
            dve_sum_start(dve, L)
            for n in range(Q_TILES):
                dve_sum(dve, n % 2, n, L)
            dve_invert(dve, Q_TILES, L)
            dve_sum_start(dve, L)
            st.left += Q_TILES + SLOTS
            dve.wait_ge(tile_left, st.left)
            dve_apply(dve, Q_TILES, L, lambda k: latents[:, k, :], lambda k: latents[:, k, :], "q_norm")
            for n in range(KV_TILES):
                dve_sum(dve, n % 2, n, L)
            st.left += KV_TILES + 1 + SLOTS
            dve.wait_ge(con_loaded, 64)
            dve.wait_ge(tile_left, st.left)
            dve.tensor_tensor(k_rope[:], k_rope_raw, mcon("cos_mla", L), ALU.mult).then_inc(d["rope"], 1)
            dve.wait_ge(d["rope_mm"], 1)
            dve.tensor_tensor(halves(rope_cos, L), wide[2][:, :, 0:HALF], halves(mcon("sin_mla", L), L), ALU.mult).then_inc(d["rope"], 1)
            dve.wait_ge(d["rope"], 2)
            dve.tensor_tensor(k_rope[:], k_rope[:], rope_cos, ALU.add).then_inc(d["rope"], 1)
            dve_invert(dve, KV_TILES, L)
            dve_apply(dve, KV_TILES, L, lambda k: latents[:, Q_TILES + k, :], lambda k: latents[:, Q_TILES + k, :], "kv_norm")
            dve.drain().then_inc(d["gated"], SLOTS)

            def gate(j, t, n):
                dve.wait_ge(tile_left, st.left + SLOTS + n + 1)
                at = flat[:, bass.ds(n * L, L)]
                dve.scalar_tensor_tensor(at, tanh_gate[t], 1.0, at, ALU.add, ALU.mult).then_inc(d["gated"], 1)
            over_tiles(dve, KI, SLOTS, gate)
            st.left += KI + SLOTS

        MLA_SCALE = (P + KROPE) ** -0.5
        UP = FIRST["mla_up"]
        PER_TURN = 4
        e = {n: sem("e_" + n) for n in ("made", "evac", "rope", "scores", "dve", "exp", "turned", "pt", "pv", "v_now", "gated")}
        DVE_E = Count(e["dve"], 19)
        SCORE_OF = [wide[0][:, 0, P_AT[t]:P_AT[t + 1]] for t in range(3)] + [wide[0][:, 1, 0:Q_EDGES[4]], wide[1][:, :, 0:HALF]]
        TURNED = [(0, 0, 4, 0, 0, 0), (0, 4, 5, 0, 1, 1), (2, 2, 5, P, 1, 1), (1, 1, 5, 0, 0, 2), (3, 3, 5, 0, 1, 3), (4, 4, 5, 2 * P, 1, 3)]

        def size(t):
            return Q_EDGES[t + 1] - Q_EDGES[t]

        def p_of(t, lo=0, hi=L):
            return probs[0:size(t), P_AT[t] + lo:P_AT[t] + min(hi, Q_EDGES[t + 1])]

        def of_pair(x):
            return UP + 2 * (x // 2), UP + 2 * (x // 2) + 1

        def head_weights(x):
            q_load, k_load = of_pair(x)
            o = x % 2
            return (ring.slot(q_load)[:, o * 512:(o + 1) * 512], ring.slot(k_load)[:, 512 + o * 256:512 + (o + 1) * 256],
                    ring.slot(k_load)[:, 0:512])

        def pe_up(pe, H, x, j, first=False):
            st = seen["pe"]
            wq, wk, wr = head_weights(x)
            q_load, k_load = of_pair(x)

            def product(dst, w, k0, kt):
                for b in range(2):
                    for k in range(kt):
                        mm = pe.matmul(dst[:, b, 0:HALF], w[:, k * P:(k + 1) * P], latents[:, k0 + k, b * HALF:(b + 1) * HALF],
                                       start=k == 0, stop=k == kt - 1)
                return mm

            if not first:
                pe.wait_ge(e["pt"], 6 * H)
            pair = (PER_TURN * j + x) // 2 if isinstance(j, int) else PER_TURN // 2 * j + x // 2
            if x % 2 == 0:
                ring.wait_full(pe, k_load, j)
                product(wide[2], wr, 0, Q_TILES).then_inc(e["made"], 1)
            if not first:
                pe.wait_ge(e["gated"], 2 * H)
            mm = product(wide[3], wk, Q_TILES, KV_TILES)
            mm.then_inc(e["made"] if x % 2 == 0 else ring.done(k_load), 1)
            if x % 2 == 0:
                ring.wait_full(pe, q_load, j)
                pe.wait_ge(e["evac"], 5 * pair + 1)
            mm = product(wide[2], wq, 0, Q_TILES)
            mm.then_inc(e["made"] if x % 2 == 0 else ring.done(q_load), 1)
            if x % 2 == 0:
                pe.wait_ge(e["evac"], 5 * pair + 2)
                for b in range(2):
                    mm = pe.matmul(wide[3][:, b, 0:HALF], mcon("rot_mla", P), q_rope_raw[:, b * HALF:(b + 1) * HALF], start=True, stop=True)
                mm.then_inc(e["made"], 1)

        def act_up(act, x, j, what):
            q_load, k_load = of_pair(x)
            pair = (PER_TURN * j + x) // 2 if isinstance(j, int) else PER_TURN // 2 * j + x // 2
            if x % 2 == 0:
                act.wait_ge(e["made"], 4 * pair + 1 + what)
            else:
                ring.wait_used(act, k_load if what == 1 else q_load, j)
            dst, src = ((q_rope_raw, wide[2]), (k_nope, wide[3]), (q_nope, wide[2]))[what]
            act.activation(halves(dst, L), src[:, :, 0:HALF], ACT.Copy).then_inc(e["evac"], 1)

        def dve_rope(dve, j, x):
            pair = (PER_TURN * j + x) // 2 if isinstance(j, int) else PER_TURN // 2 * j + x // 2
            dve.wait_ge(e["evac"], 5 * pair + 1)
            dve.tensor_tensor(q_rope, q_rope_raw, mcon("cos_mla", L), ALU.mult).then_inc(e["rope"], 1)
            dve.wait_ge(e["made"], 4 * pair + 4)
            dve.tensor_tensor(halves(sq[:, 0, :], L), wide[3][:, :, 0:HALF], halves(mcon("sin_mla", L), L), ALU.mult).then_inc(e["rope"], 1)
            dve.wait_ge(e["rope"], 3 * pair + 2)
            dve.tensor_tensor(q_rope, q_rope, sq[:, 0, :], ALU.add).then_inc(e["rope"], 1)

        def pe_head(pe, j, x, last):
            H = PER_TURN * j + x
            ends = last and x == PER_TURN - 1
            pair = (PER_TURN * j + x) // 2 if isinstance(j, int) else PER_TURN // 2 * j + x // 2
            pe.wait_ge(e["evac"], 5 * pair + (3 if x % 2 == 0 else 5))
            pe.wait_ge(e["rope"], 3 * pair + 3)
            rows = HEAD_ROWS[x % 2]
            for t in (4, 3, 0, 1, 2):
                lo, hi = Q_EDGES[t], Q_EDGES[t + 1]
                for b in range(2 if t == 4 else 1):
                    keys = slice(b * HALF, (b + 1) * HALF) if t == 4 else slice(0, hi)
                    dst = SCORE_OF[t][0:size(t), b, :] if t == 4 else SCORE_OF[t][0:size(t)]
                    pe.matmul(dst, q_nope[:, lo:hi], k_nope[:, keys], start=True, stop=False)
                    mm = pe.matmul(dst, q_rope[rows, lo:hi], k_rope[rows, keys], start=False, stop=True)
                if t in (4, 3, 2):
                    mm.then_inc(e["scores"], 1)
            if not ends:
                pe_up(pe, H + 1, (x + 1) % PER_TURN, j + (x + 1) // PER_TURN)
                pair_next = pair + (x % 2)
                pe.wait_ge(e["evac"], 5 * pair_next + (3 if x % 2 else 5))
            else:
                pe.wait_ge(e["pt"], 6 * H + 6)
            for n, (kb, q0, q1, col, bank, piece) in enumerate(TURNED):
                if n == 0:
                    pe.wait_ge(DVE_E.sem, DVE_E.at(H, 19))
                if n == 3:
                    pe.wait_ge(e["pt"], 6 * H + 7)
                if n == 4:
                    pe.wait_ge(e["pt"], 6 * H + 9)
                for t in reversed(range(q0, q1)):
                    at = col + Q_EDGES[t] - Q_EDGES[q0]
                    mm = pe.transpose(wide[2][0:size(kb), bank, at:at + size(t)], p_of(t, Q_EDGES[kb], Q_EDGES[kb + 1]), ident[0:size(t), 0:size(t)])
                if n in (0, 2, 3, 5):
                    mm.then_inc(e["turned"], 1)
            pe.wait_ge(e["v_now"], 2 * H + 2)
            if not ends:
                if x % 2:
                    pe.wait_ge(e["rope"], 3 * pair_next + 2)
            else:
                pe.wait_ge(e["gated"], 2 * H + 2)
            cut = Q_EDGES[3]
            for kb, done in ((0, 2), (2, 3), (1, 4), (3, 5), (4, 6)):
                pe.wait_ge(e["pt"], 6 * H + 6 + done)
                for b, (lo, hi) in enumerate(((0, cut), (cut, L))):
                    seen_from = max(lo, Q_EDGES[kb])
                    if seen_from < hi:
                        mm = pe.matmul(wide[3][:, b, seen_from - lo:hi - lo], v_now[0:size(kb), x % 2, kb, :],
                                       probs_t[0:size(kb), kb, seen_from:hi], start=kb == 0, stop=kb == (1, 4)[b])
            mm.then_inc(e["pv"], 1)

        def act_head(act, j, x, last):
            H = PER_TURN * j + x
            ends = last and x == PER_TURN - 1
            nx, nj = (x + 1) % PER_TURN, j + (x + 1) // PER_TURN

            def soften(t, step):
                act.wait_ge(DVE_E.sem, DVE_E.at(H, step))
                act.activation(halves(p_of(t), L) if t == 4 else p_of(t), SCORE_OF[t][0:size(t)], ACT.Exp, bias=row_bias[0:size(t), t:t + 1],
                               scale=MLA_SCALE, accum_out=row_sum[0:size(t), t:t + 1]).then_inc(e["exp"], 1)

            soften(4, 5)
            soften(3, 5)
            if not ends and nx % 2 == 0:
                act_up(act, nx, nj, 0)
            for t in (2, 1, 0):
                soften(t, 12)
            if not ends:
                act_up(act, nx, nj, 1)
                act_up(act, nx, nj, 2)
            for n, (kb, q0, q1, col, bank, piece) in enumerate(TURNED):
                act.wait_ge(e["turned"], 4 * H + piece + 1)
                if n == 0:
                    act.wait_ge(e["pv"], H + 1)
                lo, hi = Q_EDGES[q0], Q_EDGES[q1]
                act.activation(probs_t[0:size(kb), kb, lo:hi], wide[2][0:size(kb), bank, col:col + hi - lo], ACT.Copy).then_inc(e["pt"], 1)

        def dve_head(dve, j, x, last):
            H = PER_TURN * j + x
            ends = last and x == PER_TURN - 1

            def step(ins):
                ins.then_inc(DVE_E.sem, 1)

            def after(k):
                dve.wait_ge(DVE_E.sem, DVE_E.at(H, k))

            def maxima(t, k):
                n = size(t)
                diag = SCORE_OF[t][:, 1, HALF - n:HALF] if t == 4 else SCORE_OF[t][0:n, Q_EDGES[t]:Q_EDGES[t + 1]]
                step(dve.tensor_tensor(diag, diag, mcon("causal", P)[0:n, 0:n], ALU.add))
                after(k)
                step(dve.tensor_reduce(row_max[0:n, t:t + 1], SCORE_OF[t][0:n], mybir.AxisListType.XY if t == 4 else AX_X, ALU.max))

            def bias(ts):
                step(dve.tensor_scalar(row_bias[:, ts], row_max[:, ts], -MLA_SCALE, None, ALU.mult))

            def share(t):
                n = size(t)
                step(dve.tensor_scalar(p_of(t), p_of(t), row_sum[0:n, t:t + 1], None, ALU.mult))

            dve.wait_ge(e["scores"], 3 * H + 1)
            maxima(4, 1)
            dve.wait_ge(e["scores"], 3 * H + 2)
            maxima(3, 3)
            after(4)
            bias(slice(3, 5))
            dve.wait_ge(e["scores"], 3 * H + 3)
            maxima(2, 6)
            maxima(1, 8)
            maxima(0, 10)
            after(11)
            bias(slice(0, 3))
            dve.wait_ge(e["exp"], Q_BLOCKS * H + 2)
            step(dve.reciprocal(row_sum[:, 3:5], row_sum[:, 3:5]))
            after(13)
            share(4)
            share(3)
            dve.wait_ge(e["exp"], Q_BLOCKS * H + 5)
            step(dve.reciprocal(row_sum[:, 0:3], row_sum[:, 0:3]))
            after(16)
            share(2)
            share(1)
            share(0)
            if not ends and x % 2:
                dve_rope(dve, j + (x + 1) // PER_TURN, (x + 1) % PER_TURN)
            dve.wait_ge(e["pv"], H + 2)
            flat = z_t[:].rearrange("p k n -> p (k n)")
            cut = Q_EDGES[3]
            for b, (lo, hi) in enumerate(((0, cut), (cut, L))):
                at = flat[:, bass.ds(H * L + lo, hi - lo)]
                dve.scalar_tensor_tensor(at, wide[3][:, b, 0:hi - lo], 0.5, at, ALU.mult, ALU.mult).then_inc(e["gated"], 1)

        def pool_v(pool, H, slot):
            flat = v_rows[:].rearrange("p t n -> p (t n)")
            pool.tensor_copy(v_now[0:META, slot, 0, :], flat[0:META, bass.ds(H * P, P)]).then_inc(e["v_now"], 1)
            src = v_rows[:, 1:Q_BLOCKS, bass.ds(H * P, P)]
            pool.tensor_copy(v_now[:, slot, 1:Q_BLOCKS, :], src).then_inc(e["v_now"], 1)

        def y_low(k):
            return y_lo_last[:, k - (KI - SLOTS), :] if k >= KI - SLOTS else y_lo[:, k, :]

        def gated_parts(k, b):
            return [part[:, b * HALF:(b + 1) * HALF] for part in (y_hi[:, k, :], y_low(k))]

        def pool_split_head(pool, H, low):
            pool.wait_ge(e["gated"], 2 * H + 4)
            z, hi = (ap[:].rearrange("p k n -> p (k n)")[:, bass.ds(H * L, L)] for ap in (z_t, y_hi))
            pool_split_tile(pool, z, hi, low(H))

        def pool_head(pool, j, x, last):
            H = PER_TURN * j + x
            if last and x == 3:
                pool_split(pool, (FIRST["mla_out"], 2), w_out)
                pool_split_head(pool, H, y_low)
                return
            pool.wait_ge(e["pv"], H + 2)
            if last and x == 2:
                for k in range(H - 2, H + 1):
                    pool_split_head(pool, k, y_low)
                return
            pool_v(pool, H + 2, x % 2)
            if not last:
                pool_split_head(pool, H, lambda n: y_lo[:].rearrange("p k n -> p (k n)")[:, bass.ds(n * L, L)])

        def over_heads(eng, body):
            with eng.Fori(0, HEADS // PER_TURN - 1) as j:
                for x in range(PER_TURN):
                    body(eng, j, x, False)
            for x in range(PER_TURN):
                body(eng, HEADS // PER_TURN - 1, x, True)

        def pe_mla(pe):
            st = seen["pe"]
            pe.wait_ge(d["v_copied"], 4 * Q_BLOCKS)
            pe.drain().then_inc(e["pv"], 1)
            pe_up(pe, 0, 0, 0, first=True)
            over_heads(pe, pe_head)

        def act_mla(act):
            act.drain().then_inc(e["pt"], 6)
            for what in range(3):
                act_up(act, 0, 0, what)
            over_heads(act, act_head)

        def dve_mla(dve):
            dve.drain().then_inc(e["gated"], 2)
            dve_rope(dve, 0, 0)
            dve.wait_ge(d["stats_set"], 3)
            over_heads(dve, dve_head)

        def pool_mla_in(pool):
            ring.wait_used(pool, MLA_IN - 1)
            pool_split(pool, (MLA_IN, 2), w_parts)
            pool_split_u(pool, u_mla, L)
            pool_split(pool, (MLA_IN + 2, MLA_GATE - MLA_IN - 2), w_parts)
            pool_split(pool, (MLA_GATE, KI), w_parts)

        def pool_mla(pool):
            pool.wait_ge(d["v_copied"], 4 * Q_BLOCKS)
            pool_v(pool, 0, 0)
            pool_v(pool, 1, 1)
            over_heads(pool, pool_head)

        def sp_stream(sp, first, end):
            turns = (end - first) // SLOTS
            with sp.Fori(0, turns) as j:
                for n in range(SLOTS):
                    ring.load(sp, stream, first + n, j)
            for n in range(first + turns * SLOTS, end):
                ring.load(sp, stream, n)


        G = ExitStack()

        def sg(name, *shape):
            return G.enter_context(nc.sbuf_tensor(name, [P, *shape], F32))

        w_parts2 = [ctx.enter_context(nc.sbuf_tensor(f"w_{n}", [P, 2, SLOT], mybir.dt.float32r)) for n in ("high", "low")]
        g_con = sb("second_tables", CON_OF["odd"][1])
        dft = sg("dft", 2, SEQ // P, SEQ)
        parts = sg("even_parts", 24, SEQ)
        G1 = ExitStack()
        y_even = (G1.enter_context(nc.sbuf_tensor("y_high_even", [P, KD, SEQ], mybir.dt.float32r)), u_lo)
        G1.close()
        padded = sg("a_c_a_x", 4, SEQ + 2)
        tanh_z = sg("tanh_z", 4, SEQ)
        G2 = ExitStack()
        u_even = (G2.enter_context(nc.sbuf_tensor("u_high_even", [P, KD, SEQ], mybir.dt.float32r)), u_lo)
        G2.close()
        spectrum = sg("spectrum", 4, E_G, 2 * E_DIM)
        G.close()
        B_U, A_C, A_X, A_B, A_Z, B_Z = range(0, 24, 4)
        conv = parts[:, A_X:A_X + 4, :]
        g = {n: sem("g_" + n) for n in ("tanh", "steps", "padded", "part_mm", "part_copied", "dft_mm", "y")}

        def gcon(name, width):
            at = CON[name] - CON_OF["odd"][0]
            return g_con[:, at:at + width]

        def sp_g(sp):
            sp.wait_ge(n_rooted, 5)
            first, n = CON_OF["odd"]
            sp.dma_start(g_con[:], con_in[:, first:first + n]).then_inc(con_loaded, 16)
            sp.dma_start(dft[:], dft_in).then_inc(con_loaded, 16)

        def whole(ap):
            return lambda k, b: ap[:, k, 0:SEQ]

        def whole_parts(u_parts):
            return lambda k, b: [ap[:, k, 0:SEQ] for ap in u_parts]

        def pool_even(pool):
            pool.wait_ge(n_rooted, 5)
            pool_split(pool, (FIRST["even_in"], 2), w_parts2)
            pool_split_u(pool, u_even, SEQ)
            pool_split(pool, (FIRST["even_in"] + 2, 2), w_parts2)
            pool_split(pool, (FIRST["even_in"] + 4, 20), w_parts2)
            pool_split(pool, (FIRST["even_out"], 2), w_parts2)
            for k in range(KD):
                pool.wait_ge(g["y"], k + 1)
                pool_split_y(pool, y_of(k), y_even[0][:, k, :], y_even[1][:, k, 0:SEQ], k)
            pool_split(pool, (FIRST["even_out"] + 2, KD - 2), w_parts2)

        def y_of(k):
            return parts[:, A_B + k if k < 4 else B_Z + k - 4, :]

        EVEN_FIRST = 16

        def pe_even(pe):
            st = seen["pe"]
            pe_tiles(pe, FIRST["even_in"], EVEN_FIRST, KD, whole_parts(u_even), SEQ, ready=normed(pe, KD), split=w_parts2)
            pe_tiles(pe, FIRST["even_in"] + EVEN_FIRST, 24 - EVEN_FIRST, KD, whole_parts(u_even), SEQ, split=w_parts2)
            pe.wait_ge(con_loaded, 96)
            for n in range(8):
                pair, t = n // 4, n % 4
                if n % 2 == 0:
                    pe.wait_ge(tile_left, st.left - (3 - n // 2 if n < 6 else 0))
                for o in range(2):
                    mm = pe.matmul(wide[n // 2][:, n % 2, o * 256:(o + 1) * 256], parts[:, B_U + 2 * pair + o, t * P:(t + 1) * P],
                                   gcon("dft_d", 2 * E_DIM), start=True, stop=True)
                mm.then_inc(g["part_mm"], 1)
            for grp_ in range(E_G):
                pe.wait_ge(g["part_copied"], 4 + grp_ // 2 * 4)
                for t in range(4):
                    for o in range(2):
                        mm = pe.matmul(wide[grp_][:, 0, :], spectrum[:, t, grp_, o * E_DIM:(o + 1) * E_DIM], dft[:, o, t, :],
                                       start=t + o == 0, stop=t + o == 4)
                mm.then_inc(g["dft_mm"], 1)
            pe.wait_ge(g["y"], 5)
            pe_project_out(pe, FIRST["even_out"], KD, whole_parts(y_even), SEQ, None, split=w_parts2,
                           ready=lambda i: pe.wait_ge(y_split, POOLED + HEADS + i + 1))

        def act_even(act):
            st = seen["act"]
            flat = parts[:].rearrange("p k n -> p (k n)")

            def keep(j, t, n):
                act.activation(flat[:, bass.ds(n * SEQ, SEQ)], tile_ps(t, SEQ), ACT.Copy).then_inc(tile_left, 1)

            def gate(j, t, n):
                act.wait_ge(g["tanh"], n + 1)
                act.activation(tanh_z[:, t, :], tile_ps(t, SEQ), ACT.Tanh, scale=0.5)
                act.activation(flat[:, bass.ds((n + EVEN_FIRST) * SEQ, SEQ)], tile_ps(t, SEQ), ACT.Copy).then_inc(tile_left, 1)
            act_tiles(act, FIRST["even_in"], EVEN_FIRST, KD, keep, prelude=lambda: act_split_u(act, u_even, SEQ))
            st.u += KD
            act_tiles(act, FIRST["even_in"] + EVEN_FIRST, 24 - EVEN_FIRST, KD, gate)
            for n in range(8):
                pair, t = n // 4, n % 4
                act.wait_ge(g["part_mm"], n + 1)
                act.activation(spectrum[:, t, 2 * pair:2 * pair + 2, :], wide[n // 2][:, n % 2, :].rearrange("p (g n) -> p g n", g=2),
                               ACT.Copy).then_inc(g["part_copied"], 1)
            act_project_out(act, FIRST["even_out"], KD, SEQ, None)

        def dve_even(dve):
            st = seen["dve"]
            dve.memset(padded[:, :, 0:1], 0.0).then_inc(g["padded"], 1)
            dve.memset(padded[:, :, SEQ + 1:SEQ + 2], 0.0).then_inc(g["padded"], 1)
            dve.drain().then_inc(g["tanh"], 4)
            steps = [0]

            def step(ins):
                ins.then_inc(g["steps"], 1)
                steps[0] += 1

            def after():
                dve.wait_ge(g["steps"], steps[0])

            def tiles(n):
                dve.wait_ge(tile_left, st.left + SLOTS + n)
            tiles(A_X + 4)
            step(dve.tensor_tensor(padded[:, :, 1:SEQ + 1], parts[:, A_C:A_C + 4, :], parts[:, A_X:A_X + 4, :], ALU.mult))
            dve.wait_ge(g["padded"], 2)
            after()
            for tap in range(3):
                for t in range(4):
                    w = pcol("conv", tap * 4 + t)
                    src = padded[:, t, tap:tap + SEQ]
                    if tap == 0:
                        step(dve.tensor_scalar(conv[:, t, :], src, w, None, ALU.mult))
                    else:
                        step(dve.scalar_tensor_tensor(conv[:, t, :], src, w, conv[:, t, :], ALU.mult, ALU.add))
                after()
            tiles(A_B + 4)
            step(dve.tensor_tensor(parts[:, A_B:A_B + 4, :], parts[:, A_B:A_B + 4, :], conv, ALU.mult))
            after()
            st.left += EVEN_FIRST + SLOTS
            for n in range(8):
                tiles(n + 1)
                z = parts[:, A_Z + n, :]
                step(dve.scalar_tensor_tensor(z, tanh_z[:, n % 4, :], 1.0, z, ALU.add, ALU.mult))
                dve.drain().then_inc(g["tanh"], 1)
                if n < 4:
                    after()
                    y = parts[:, A_B + n, :]
                    dve.scalar_tensor_tensor(y, y, 0.5, z, ALU.mult, ALU.mult).then_inc(g["y"], 1)
            st.left += 24 - EVEN_FIRST + SLOTS
            after()
            for n in range(E_G):
                dve.wait_ge(g["dft_mm"], n + 1)
                z = parts[:, B_Z + n, :]
                dve.scalar_tensor_tensor(z, wide[n][:, 0, :], 0.5, z, ALU.mult, ALU.mult).then_inc(g["y"], 1)
            dve_project_out(dve, KD, SEQ, None, None, "odd", lambda k: u2[:, k, 0:SEQ], u_odd)

        HH = ExitStack()

        def sh(name, *shape):
            return HH.enter_context(nc.sbuf_tensor(name, [P, *shape], F32))

        NQK = G_HEADS + G_KV
        qk = sh("q_k", NQK, SEQ)
        z_odd = sh("z_odd", G_HEADS, SEQ)
        with_gain, qk_sq, qk_root = sh("with_gain", 2, SEQ), sh("qk_squares", 2, SEQ), sh("qk_root", 2, SEQ)
        rot_sin = sh("rot_sin", SEQ)
        v_odd = sh("v_odd", 4, G_KV * P)
        q_now = sh("q_now", 2, SEQ)
        o_probs, o_probs_t = sh("odd_probs", 2, SEQ), sh("odd_probs_t", 2, SEQ)
        o_max, o_bias, o_sum = (sh("odd_" + n, 8) for n in ("max", "bias", "sum"))
        tanh_odd = sh("tanh_odd", G_HEADS, SEQ)
        u_odd = (HH.enter_context(nc.sbuf_tensor("u_high_odd", [P, KD, SEQ], mybir.dt.float32r)), u_lo)
        HH.close()
        o = {n: sem("o_" + n) for n in ("sq", "sum", "rot", "root", "dve", "v_mm", "v_copied", "q_now", "scores", "turned", "pt", "pv",
                                        "exp", "bias", "share", "tanh", "z", "gated")}
        ODD_Z, ODD_K, ODD_V = FIRST["odd_in"] + G_HEADS, FIRST["odd_in"] + 2 * G_HEADS, FIRST["odd_v"]
        ODD_SCALE = P ** -0.5
        DVE_O = Count(o["dve"], 6)
        qk_flat = qk[:].rearrange("p k n -> p (k n)")
        z_flat = z_odd[:].rearrange("p k n -> p (k n)")

        def qk_of(n):
            return qk_flat[:, bass.ds(n * SEQ, SEQ)]

        def pe_qk(pe, n, t):
            pe.wait_ge(o["sq"], n + 1)
            pe.wait_ge(o["root"], n + 1)
            pe.matmul(wide[t % 2][:, 1, :], ones, qk_sq[:, t % 2, :], start=True, stop=True).then_inc(o["sum"], 1)
            pe.wait_ge(o["dve"], 6 * n + 12 + 1)
            pe.matmul(wide[2 + t % 2][:, 1, :], gcon("rot_odd", P), with_gain[:, t % 2, :], start=True, stop=True).then_inc(o["rot"], 1)

        def act_qk(act, n, t):
            act.wait_ge(o["sum"], n + 1)
            act.activation(qk_sq[:, t % 2, :], qk_of(n), ACT.Square).then_inc(o["sq"], 1)
            act.wait_ge(o["sum"], n + 3)
            act.wait_ge(o["dve"], 6 * n + 6)
            act.activation(qk_root[:, t % 2, :], wide[t % 2][:, 1, :], ACT.Sqrt, bias=epsilon[:, 0:1], scale=1.0 / P).then_inc(o["root"], 1)

        def dve_qk(dve, n, t, gain):
            def step(ins):
                ins.then_inc(o["dve"], 1)

            def after(k):
                dve.wait_ge(o["dve"], 6 * n + 12 + k)
            x, y = with_gain[:, t % 2, :], qk_of(n)
            dve.wait_ge(o["rot"], n + 1)
            step(dve.tensor_scalar(x, y, pcol(gain), None, ALU.mult))
            dve.wait_ge(o["sq"], n + 1)
            after(1)
            step(dve.tensor_tensor(y, x, gcon("cos_odd", SEQ), ALU.mult))
            dve.wait_ge(o["rot"], n + 3)
            step(dve.tensor_tensor(rot_sin[:], wide[2 + t % 2][:, 1, :], gcon("sin_odd", SEQ), ALU.mult))
            after(3)
            step(dve.tensor_tensor(y, y, rot_sin[:], ALU.add))
            dve.wait_ge(o["root"], n + 3)
            step(dve.reciprocal(qk_root[:, t % 2, :], qk_root[:, t % 2, :]))
            after(5)
            step(dve.tensor_tensor(y, y, qk_root[:, t % 2, :], ALU.mult))

        def pe_odd_in(pe):
            st = seen["pe"]
            pe_tiles(pe, FIRST["odd_in"], G_HEADS, KD, whole_parts(u_odd), SEQ, ready=normed(pe, 2 * KD), split=w_parts2)
            pe.drain().then_inc(o["sum"], 2)
            pe.drain().then_inc(o["rot"], 2)
            pe_tiles(pe, ODD_Z, G_HEADS, KD, whole_parts(u_odd), SEQ, split=w_parts2, after=lambda n, t: pe_qk(pe, n, t))
            pe_tiles(pe, ODD_K, G_KV, KD, whole_parts(u_odd), SEQ, loop=False, split=w_parts2)
            for n in range(G_KV):
                pe_qk(pe, G_HEADS + n, n)
            st.splits += 2
            pe.wait_ge(w_split, st.splits)
            w = [part[:].rearrange("p s (k n) -> p (s k) n", n=G_KV * P) for part in w_parts2]
            for t in range(4):
                pe.wait_ge(tile_left, st.left)
                block = slice(t * P, (t + 1) * P)
                for k in range(KD):
                    mm = split_products(pe, wide[t][:, 0, 0:G_KV * P], [part[:, k, block] for part in u_odd],
                                        (w[0][:, k, :], w[1][:, k, :]), k == 0, k == KD - 1)
                mm.then_inc(o["v_mm"], 1)
            for k in range(2):
                pe.drain().then_inc(ring.done(ODD_V + k), 1)

        def act_odd_in(act):
            act_tiles(act, FIRST["odd_in"], G_HEADS, KD,
                      lambda j, t, n: act.activation(qk_of(n), tile_ps(t, SEQ), ACT.Copy).then_inc(tile_left, 1),
                      prelude=lambda: act_split_u(act, u_odd, SEQ))
            act.wait_ge(tile_left, seen["act"].left)
            act.drain().then_inc(o["root"], 2)

            def keep_z(j, t, n):
                act.activation(z_flat[:, bass.ds(n * SEQ, SEQ)], tile_ps(t, SEQ), ACT.Copy).then_inc(tile_left, 1)
            act_tiles(act, ODD_Z, G_HEADS, KD, keep_z, before=lambda n, t: act_qk(act, n, t))
            act_tiles(act, ODD_K, G_KV, KD,
                      lambda j, t, n: act.activation(qk_of(G_HEADS + n), tile_ps(t, SEQ), ACT.Copy).then_inc(tile_left, 1), loop=False)
            act.wait_ge(tile_left, seen["act"].left)
            for n in range(G_KV):
                act_qk(act, G_HEADS + n, n)
            for n in range(G_HEADS):
                act.activation(tanh_odd[:, n, :], z_odd[:, n, :], ACT.Tanh, scale=0.5).then_inc(o["tanh"], 1)
            for t in range(4):
                act.wait_ge(o["v_mm"], t + 1)
                act.activation(v_odd[:, t, :], wide[t][:, 0, 0:G_KV * P], ACT.Copy).then_inc(o["v_copied"], 1)

        def dve_odd_in(dve):
            st = seen["dve"]
            dve.drain().then_inc(o["dve"], 12)
            dve.wait_ge(tile_left, st.left + G_HEADS + SLOTS)
            over_tiles(dve, G_HEADS, SLOTS, lambda j, t, n: dve_qk(dve, n, t, "q_gain"))
            st.left += 2 * (G_HEADS + SLOTS) + G_KV + SLOTS
            dve.wait_ge(tile_left, st.left)
            for n in range(G_KV):
                dve_qk(dve, G_HEADS + n, n, "k_gain")
            for n in range(G_HEADS):
                dve.wait_ge(o["tanh"], n + 1)
                dve.scalar_tensor_tensor(z_odd[:, n, :], tanh_odd[:, n, :], 1.0, z_odd[:, n, :], ALU.add, ALU.mult).then_inc(o["z"], 1)
            dve.wait_ge(o["z"], G_HEADS)

        TURNS = G_HEADS // G_KV
        UNITS = G_KV * 4
        AHEAD = 3
        S_BANK = [wide[n // 2][:, n % 2, :] for n in range(4)]

        def pe_scores(pe, j, u):
            j, u = j + u // UNITS, u % UNITS
            x, t = u // 4, u % 4
            if t == 0:
                pe.wait_ge(o["q_now"], 2 * j + x + 1)
            pe.matmul(S_BANK[u % 4], q_now[:, x, t * P:(t + 1) * P], qk[:, G_HEADS + x, :], start=True, stop=True).then_inc(o["scores"], 1)

        def pe_turn(pe, j, last):
            for u in range(UNITS):
                x, t = u // 4, u % 4
                U = UNITS * j + u
                pe.wait_ge(o["share"], 2 * U + 2)
                pe.wait_ge(o["pt"], U + 1)
                for k in range(4):
                    mm = pe.transpose(wide[2][:, u % 2, k * P:(k + 1) * P], o_probs[:, u % 2, k * P:(k + 1) * P], ident)
                mm.then_inc(o["turned"], 1)
                if not (last and u + AHEAD >= UNITS):
                    pe_scores(pe, j, u + AHEAD)
                pe.wait_ge(o["pt"], U + 3)
                if t == 0:
                    pe.wait_ge(o["gated"], 2 * j + x + 1)
                for k in range(4):
                    mm = pe.matmul(wide[3][:, x, t * P:(t + 1) * P], v_odd[:, k, x * P:(x + 1) * P], o_probs_t[:, u % 2, k * P:(k + 1) * P],
                                   start=k == 0, stop=k == 3)
                mm.then_inc(o["pv"], 1)

        def act_turn(act, j, last):
            for u in range(UNITS):
                U = UNITS * j + u
                act.wait_ge(o["bias"], 2 * U + 2)
                act.wait_ge(o["turned"], U + 1)
                act.activation(o_probs[:, u % 2, :], S_BANK[u % 4], ACT.Exp, bias=o_bias[:, u:u + 1], scale=ODD_SCALE,
                               accum_out=o_sum[:, u:u + 1]).then_inc(o["exp"], 1)
                act.wait_ge(o["turned"], U + 3)
                act.wait_ge(o["pv"], U + 1)
                act.activation(o_probs_t[:, u % 2, :], wide[2][:, u % 2, :], ACT.Copy).then_inc(o["pt"], 1)

        def dve_max(dve, j, u):
            U = UNITS * j + u
            u = u % UNITS
            dve.wait_ge(o["scores"], U + 1)
            dve.tensor_reduce(o_max[:, u:u + 1], S_BANK[u % 4], AX_X, ALU.max).then_inc(o["bias"], 1)
            dve.wait_ge(o["bias"], 2 * U + 1)
            dve.tensor_scalar(o_bias[:, u:u + 1], o_max[:, u:u + 1], -ODD_SCALE, None, ALU.mult).then_inc(o["bias"], 1)

        def dve_turn(dve, j, last):
            for u in range(UNITS):
                U = UNITS * j + u
                if not (last and u + 1 == UNITS):
                    dve_max(dve, j, u + 1)
                dve.wait_ge(o["exp"], U + 1)
                dve.reciprocal(o_sum[:, u:u + 1], o_sum[:, u:u + 1]).then_inc(o["share"], 1)
                dve.wait_ge(o["share"], 2 * U + 1)
                dve.tensor_scalar(o_probs[:, u % 2, :], o_probs[:, u % 2, :], o_sum[:, u:u + 1], None, ALU.mult).then_inc(o["share"], 1)
                if u in (4, UNITS - 1):
                    x = u // 5
                    dve.wait_ge(o["pv"], UNITS * j + 4 * x + 6)
                    z = z_flat[:, bass.ds((4 * x + j) * SEQ, SEQ)]
                    dve.scalar_tensor_tensor(z, wide[3][:, x, :], 0.5, z, ALU.mult, ALU.mult).then_inc(o["gated"], 1)

        def pool_q(pool, j, x):
            pool.tensor_copy(q_now[:, x, :], qk_of(4 * x + j)).then_inc(o["q_now"], 1)

        def pool_turn(pool, j, last):
            if not last:
                for x in range(2):
                    pool.wait_ge(o["scores"], UNITS * j + 4 * x + 4)
                    pool_q(pool, j + 1, x)
            if last:
                pool_split(pool, (FIRST["odd_out"], 2), w_parts2)
            hi, lo = (part[:].rearrange("p k n -> p (k n)") for part in u_odd)
            for x in range(G_KV):
                k = TURNS * x + j
                pool.wait_ge(o["gated"], G_KV * j + x + 3)
                pool_split_y(pool, z_flat[:, bass.ds(k * SEQ, SEQ)], hi[:, bass.ds(k * SEQ, SEQ)], lo[:, bass.ds(k * L, SEQ)], KD + G_KV * j + x)

        def over_turns(eng, body):
            with eng.Fori(0, TURNS - 1) as j:
                body(eng, j, False)
            body(eng, TURNS - 1, True)

        def pe_odd(pe):
            pe.drain().then_inc(o["turned"], 2)
            pe.drain().then_inc(o["pv"], 2)
            pe.wait_ge(o["dve"], 6 * NQK + 12)
            pe.wait_ge(o["v_copied"], 4)
            for u in range(AHEAD):
                pe_scores(pe, 0, u)
            over_turns(pe, pe_turn)
            pe_project_out(pe, FIRST["odd_out"], KD, whole_parts(u_odd), SEQ, None, split=w_parts2,
                           order=[TURNS * x + j for j in range(TURNS) for x in range(G_KV)], ready=lambda i: pe.wait_ge(y_split, POOLED + HEADS + KD + i + 1))

        def act_odd(act):
            act.drain().then_inc(o["pt"], 2)
            over_turns(act, act_turn)
            act_project_out(act, FIRST["odd_out"], KD, SEQ, None)

        def dve_odd(dve):
            dve.drain().then_inc(o["gated"], 2)
            dve_max(dve, 0, 0)
            over_turns(dve, dve_turn)
            dve_project_out(dve, KD, SEQ, None, None, "final", lambda k: u2[:, k, 0:SEQ])

        def pool_odd_in(pool):
            pool_split(pool, (FIRST["odd_in"], 2), w_parts2)
            pool_split_u(pool, u_odd, SEQ)
            pool_split(pool, (FIRST["odd_in"] + 2, 2), w_parts2)
            pool_split(pool, (FIRST["odd_in"] + 4, 16), w_parts2)

        def pool_odd(pool):
            pool.wait_ge(o["dve"], 6 * NQK + 12)
            for x in range(2):
                pool_q(pool, 0, x)
            over_turns(pool, pool_turn)
            pool_split(pool, (FIRST["odd_out"] + 2, KD - 2), w_parts2)

        def sp_end(sp):
            sp.wait_ge(n_used, NORMS)
            sp.dma_start(out, u2[:, :, 0:SEQ]).then_inc(stored, 16)
            sp.wait_ge(stored, 16)

        stored = sem("stored")
        NORMS = 8

        block = ctx.enter_context(nc.Block())

        @block.sync
        def _(sp):
            sp_setup(sp)
            sp_a(sp)
            sp.wait_ge(s["stored"], 16 * PAIRS)
            for n in range(SLOTS):
                ring.load(sp, stream, FIRST["rwkv_out"] + n)
            sp_b(sp)
            sp_c(sp)
            sp_stream(sp, FIRST["rwkv_out"] + SLOTS, FIRST["even_in"] + SLOTS)
            sp_g(sp)
            sp_stream(sp, FIRST["even_in"] + SLOTS, N_LOADS)
            sp_end(sp)

        @block.tensor
        def _(pe):
            pe_setup(pe)
            pe_lora(pe)
            over_pairs(pe, pe_pair)
            passes(pe, pe_pass)
            pe_c(pe)
            pe_mla_in(pe)
            pe_mla(pe)
            pe_project_out(pe, FIRST["mla_out"], KI, gated_parts, L, SEQ, split=w_out,
                           ready=lambda i: pe.wait_ge(y_split, POOLED + i + 1))
            pe_even(pe)
            pe_odd_in(pe)
            pe_odd(pe)

        @block.scalar
        def _(act):
            act_setup(act)
            act_lora(act)
            over_pairs(act, act_pair, act_in_parts)
            passes(act, act_pass)
            act_project_out(act, FIRST["rwkv_out"], KI, L, L, m_t, prelude=lambda: act_c(act))
            act_mla_in(act)
            act_mla(act)
            act_project_out(act, FIRST["mla_out"], KI, L, SEQ, m_mla)
            act_even(act)
            act_odd_in(act)
            act_odd(act)

        @block.vector
        def _(dve):
            dve_setup(dve)
            over_pairs(dve, dve_pair, dve_in_parts)
            dve_b_setup(dve)
            passes(dve, dve_pass)
            dve_c(dve)
            dve.wait_ge(h_loaded, 16)
            dve_project_out(dve, KI, L, L, "post0", "pre1", lambda k: u2[:, k, :], u_mla, m_t)
            dve_mla_in(dve)
            dve_mla(dve)
            dve_project_out(dve, KI, L, SEQ, "post1", "even", lambda k: u2[:, k, 0:SEQ], u_even, m_mla)
            dve_even(dve)
            dve_odd_in(dve)
            dve_odd(dve)

        @block.gpsimd
        def _(pool):
            pool_setup(pool)
            over_pairs(pool, pool_pair)
            pool_b_early(pool)
            pool_b_setup(pool)
            passes(pool, pool_pass)
            pool_c(pool)
            pool_mla_in(pool)
            pool_mla(pool)
            pool_split(pool, (FIRST["mla_out"] + 2, 2 * KD - 2), w_out)
            pool_even(pool)
            pool_odd_in(pool)
            pool_odd(pool)


def tile_columns(w, width=P):
    k, n = w.shape
    return np.ascontiguousarray(w.reshape(k // P, P, n // width, width).transpose(2, 1, 0, 3).reshape(n // width, P, k // P * width))


def loads_of(tiles):
    n, _, m = tiles.shape
    if m >= SLOT:
        return tiles.reshape(n, P, m // SLOT, SLOT).transpose(0, 2, 1, 3).reshape(-1, P, SLOT)
    g = SLOT // m
    return tiles.reshape(n // g, g, P, m).transpose(0, 2, 1, 3).reshape(n // g, P, SLOT)


def weight_stream(a):
    w = a["rwkv_w_in"][0]
    n_main = 4 * DI
    main = tile_columns(w[:, :n_main]).reshape(4, PAIRS, P, SLOT)
    pieces = [tile_columns(w[:, n_main:])]
    pieces.append(np.stack([main[1], main[0], main[2], main[3]], 1).reshape(-1, P, SLOT))
    pieces.append(loads_of(tile_columns(a["rwkv_w_out"][0])))
    m = a["mla_w_in"][0]
    nq, nkv = Q_TILES * P, KV_TILES * P
    rope = m[:, nq + nkv:nq + nkv + KROPE]
    pieces += [tile_columns(m[:, :nq + nkv]), tile_columns(np.concatenate([rope, rope], 1)), tile_columns(m[:, nq + nkv + KROPE:])]
    kv = a["mla_w_kv_up"][0].reshape(nkv, HEADS, 2, P)
    pieces.append(tile_columns(kv[:, :, 1].reshape(nkv, HEADS * P), 512))
    q = a["mla_w_q_up"][0].reshape(nq, HEADS // 2, 2, P + KROPE)
    for j in range(HEADS // 2):
        pieces.append(loads_of(tile_columns(q[:, j, :, :P].reshape(nq, 2 * P))))
        last = np.concatenate([tile_columns(q[:, j, :, P:].reshape(nq, P))[0],
                               tile_columns(kv[:, 2 * j, 0])[0], tile_columns(kv[:, 2 * j + 1, 0])[0]], 1)
        pieces.append(last[None])
    pieces.append(loads_of(tile_columns(a["mla_w_out"][0])))
    e = a["w_in_even_2"][0]
    e = e.reshape(D, 6, 4 * P)
    pieces.append(tile_columns(np.ascontiguousarray(e[:, [4, 2, 0, 1, 3, 5]]).reshape(D, -1)))
    pieces.append(tile_columns(a["w_out_even_2"][0]))
    o = a["w_in_odd_2"][0]
    nq, nkv = G_HEADS * P, G_KV * P
    pieces += [tile_columns(o[:, :nq]), tile_columns(o[:, nq + 2 * nkv:]), tile_columns(o[:, nq:nq + nkv])]
    pieces.append(loads_of(tile_columns(o[:, nq + nkv:nq + 2 * nkv], 2 * P)))
    pieces.append(tile_columns(a["w_out_odd_2"][0]))
    stream = np.concatenate(pieces, 0)
    assert stream.shape == (N_LOADS, P, SLOT), stream.shape
    return stream


def columns(v):
    return np.ascontiguousarray(v.reshape(-1, P).T)


def parameters(a):
    out = np.zeros((P, N_PAR), np.float32)

    def put(name, v):
        c = columns(v)
        out[:, PAR[name]:PAR[name] + c.shape[1]] = c
    for n in range(2):
        put(f"pre{n}", a["norm_pre"][n])
        put(f"post{n}", a["norm_post"][n])
    put("mu", a["rwkv_mu"][0])
    put("rwkv", np.concatenate([a[n][0] for n in ("rwkv_w0", "rwkv_a0", "rwkv_k_k", "rwkv_k_a", "rwkv_r_k", "rwkv_ln_w", "rwkv_ln_b")]))
    put("q_norm", a["mla_q_norm"][0])
    put("kv_norm", a["mla_kv_norm"][0])
    put("even", a["norm_even_2"][0])
    put("conv", a["conv_w_2"][0])
    put("odd", a["norm_odd_2"][0])
    put("q_gain", a["q_gain_2"][0])
    put("k_gain", a["k_gain_2"][0])
    put("final", a["final_norm_2"])
    return out


def constants():
    con = np.zeros((P, N_CON), np.float64)

    def put(name, v):
        con[:, CON[name]:CON[name] + v.shape[1]] = v
    r, c = np.arange(P)[:, None], np.arange(P)[None, :]
    put("ident", np.eye(P))
    put("ones", np.ones((P, P)))
    put("heads", r // C == c // C)
    for n in range(6):
        m = 1 << n
        put_at = (r // (2 * m) == c // (2 * m)) & (r // m % 2 == 1) & (c // m % 2 == 0)
        con[:, CON["levels"] + n * P:CON["levels"] + (n + 1) * P] = put_at
        if n == 0:
            put("level0T", put_at.T)
    s, t = np.arange(P)[:, None] % C, np.arange(C)[None, :]
    put("tri", np.concatenate([s < t, s <= t], 1))
    put("reset", np.repeat((np.arange(LP) % C != 0)[None], P, 0))
    put("causal", np.where(c <= r, 0.0, -BIG))
    half = KROPE // 2
    inv = np.exp(-math.log(10000.0) * np.arange(half) / half)
    ang = (inv[:, None] * np.arange(L)[None, :])[np.arange(P) % half]
    put("cos_mla", np.cos(ang))
    put("sin_mla", np.sin(ang))
    rot = np.zeros((P, P))
    for b in range(0, P, KROPE):
        for n in range(half):
            rot[b + half + n, b + n] = -1
            rot[b + n, b + half + n] = 1
    put("rot_mla", rot)
    pos = np.arange(SEQ)
    inv = 10000.0 ** (-np.arange(P // 4) / (P // 4))
    ang = np.concatenate([(pos // 64)[None] * inv[:, None], (pos % 64)[None] * inv[:, None]], 0)[np.arange(P) // 2]
    put("cos_odd", np.cos(ang))
    put("sin_odd", np.sin(ang))
    rot = np.zeros((P, P))
    for n in range(0, P, 2):
        rot[n + 1, n] = -1
        rot[n, n + 1] = 1
    put("rot_odd", rot)
    d = np.outer(np.arange(E_DIM), np.arange(E_DIM)) % E_DIM * (2 * math.pi / E_DIM)
    put("dft_d", np.concatenate([np.cos(d), np.sin(d)], 1))
    n = np.outer(np.arange(SEQ), np.arange(SEQ)) % SEQ * (2 * math.pi / SEQ)
    scale = (SEQ * E_DIM) ** -0.5
    dft = np.stack([np.cos(n) * scale, -np.sin(n) * scale]).reshape(2, SEQ // P, P, SEQ).transpose(2, 0, 1, 3)
    return con.astype(np.float32), np.ascontiguousarray(dft.astype(np.float32))


def device_inputs(a):
    tokens = np.concatenate([a["meta_tokens"], a["x"][0]], 0)
    con, dft = constants()
    lora = np.concatenate([a["rwkv_w2"][0], a["rwkv_a2"][0]], 0)
    return {
        "tokens": np.ascontiguousarray(tokens.T.reshape(KD, P, L).transpose(1, 0, 2)),
        "stream": weight_stream(a),
        "lora": np.ascontiguousarray(lora.reshape(P, PAIRS, P).transpose(1, 0, 2)),
        "par": parameters(a), "con": con, "dft": dft,
    }


def build(nc, arrays):
    def dram(name, shape, kind):
        return nc.dram_tensor(name, shape, F32, kind=kind).ap()

    ins = [dram(f"in_{n}", arrays[n].shape, "ExternalInput") for n in ("tokens", "stream", "lora", "par", "con", "dft")]
    out = dram("out", (P, KD, SEQ), "ExternalOutput")
    program(nc, *ins, out, dram("forms", (PAIRS, P, F_COLS), "Internal"), dram("mixed", (PAIRS, P, L), "Internal"))


def kernel(**inputs):
    import concourse.bacc as bacc
    from concourse.bass_utils import run_bass_kernel_spmd

    arrays = device_inputs({n: np.asarray(v) for n, v in inputs.items()})
    nc = bacc.Bacc("TRN2", target_bir_lowering=False, num_devices=1)
    build(nc, arrays)
    r = run_bass_kernel_spmd(nc, [{f"in_{n}": v for n, v in arrays.items()}], core_ids=[0])
    got = r.results[0]["out"]
    return np.ascontiguousarray(got.transpose(2, 1, 0).reshape(1, SEQ, D))
```
